# Optimizing a Trainium2 kernel written in Bass

```python
import math
import jax, jax.numpy as jnp
from jax import lax
import numpy as np
import jax
import jax.numpy as jnp

D_MODEL = 1024
BATCH = 1
SEQ = 256
DEPTH = 2

PLE_DIM = 256
N_EVEN = (DEPTH + 1) // 2
N_ODD = DEPTH // 2

DA_HEADS = 4
DA_HEAD_DIM = 64
DA_V_DIM = 2 * DA_HEAD_DIM
DA_QK_WIDTH = DA_HEADS * 2 * DA_HEAD_DIM
DA_WIDTH = DA_HEADS * DA_V_DIM

HG_HEADS = 4
HG_KDIM = 128
HG_VDIM = 128
HG_KWIDTH = HG_HEADS * HG_KDIM
HG_WIDTH = HG_HEADS * HG_VDIM
HG_CHUNK = 64

DL_HEADS = 16
DL_HEAD_DIM = D_MODEL // DL_HEADS
DL_PAIRS = ((128, 1), (512, 4), (2048, 16))

FFN_DIM = 4 * D_MODEL
ROPE_THETA = 500000.0
ROT_DIM = 64 // 4
ALPHA = (2 * DEPTH) ** 0.25
BETA = (8 * DEPTH) ** -0.25
LN_EPS = 1e-5
Q_BLOCK = 128


def layer_norm(x, g, b):
    xf = x.astype(jnp.float32)
    mu = jnp.mean(xf, -1, keepdims=True)
    var = jnp.mean(jnp.square(xf - mu), -1, keepdims=True)
    return ((xf - mu) * lax.rsqrt(var + LN_EPS) * g + b).astype(x.dtype)

def rms_norm(x, g):
    xf = x.astype(jnp.float32)
    return (xf * lax.rsqrt(jnp.mean(xf * xf, -1, keepdims=True) + LN_EPS) * g).astype(x.dtype)

def rope_tables(seq):
    inv = ROPE_THETA ** (-jnp.arange(0, ROT_DIM, 2, dtype=jnp.float32) / ROT_DIM)
    ang = jnp.arange(seq, dtype=jnp.float32)[:, None] * inv[None, :]
    return jnp.cos(ang), jnp.sin(ang)

def partial_rope(x, cos, sin):
    half = ROT_DIM // 2
    x1, x2, xp = x[..., :half], x[..., half:ROT_DIM], x[..., ROT_DIM:]
    c, s = cos.astype(x.dtype), sin.astype(x.dtype)
    return jnp.concatenate([x1 * c - x2 * s, x1 * s + x2 * c, xp], axis=-1)

def diff_attention(qa, ka, va, lam_params, sub_g, lam_init, cos, sin):
    B, S = qa.shape[:2]
    q = partial_rope(qa.transpose(0, 2, 3, 1, 4), cos, sin) * (DA_HEAD_DIM ** -0.5)
    k = partial_rope(ka.transpose(0, 2, 3, 1, 4), cos, sin)
    v = va.transpose(0, 2, 1, 3)
    lp = lam_params.astype(jnp.float32)
    lam = jnp.exp(jnp.sum(lp[0] * lp[1])) - jnp.exp(jnp.sum(lp[2] * lp[3])) + lam_init
    nb = S // Q_BLOCK
    qb = q.reshape(B, DA_HEADS, 2, nb, Q_BLOCK, DA_HEAD_DIM).transpose(3, 0, 1, 2, 4, 5)
    kpos = jnp.arange(S)

    def block(args):
        qi, i = args
        s = jnp.einsum('bhcqd,bhckd->bhcqk', qi, k).astype(jnp.float32)
        qpos = i * Q_BLOCK + jnp.arange(Q_BLOCK)
        s = jnp.where(kpos[None, :] <= qpos[:, None], s, -jnp.inf)
        pr = jax.nn.softmax(s, axis=-1)
        a = pr[:, :, 0] - lam * pr[:, :, 1]
        return jnp.einsum('bhqk,bhkd->bhqd', a.astype(v.dtype), v)

    o = lax.map(block, (qb, jnp.arange(nb)))
    o = o.transpose(1, 2, 0, 3, 4).reshape(B, DA_HEADS, S, DA_V_DIM)
    o = rms_norm(o, sub_g) * (1.0 - lam_init)
    return o.transpose(0, 2, 1, 3).reshape(B, S, DA_WIDTH)

def hgrn2(hq, hf, hi, hg, lb, out_g):
    B, S, H, dk = hq.shape
    dv = hi.shape[-1]
    f32 = jnp.float32
    q = jax.nn.silu(hq.astype(f32))
    f = lb + (1.0 - lb) * jax.nn.sigmoid(hf.astype(f32))
    kk = 1.0 - f
    logf = jnp.log(f)
    C = HG_CHUNK
    n = S // C

    def chunks(t):
        return t.reshape(B, n, C, H, t.shape[-1]).transpose(1, 0, 3, 2, 4)

    qc, kc, lc, vc = chunks(q), chunks(kk), chunks(logf), chunks(hi.astype(f32))
    b = jnp.cumsum(lc, axis=-2)
    b_last = b[..., C - 1:C, :]
    b_mid = b[..., C // 2 - 1:C // 2, :]
    a = jnp.einsum('nbhtk,nbhsk->nbhts', qc * jnp.exp(b - b_mid), kc * jnp.exp(b_mid - b))
    a = jnp.where(jnp.tril(jnp.ones((C, C), bool)), a, 0.0)
    o_intra = jnp.einsum('nbhts,nbhsv->nbhtv', a, vc)
    q_out = qc * jnp.exp(b)
    k_st = kc * jnp.exp(b_last - b)
    decay = jnp.exp(b_last[..., 0, :])

    def step(state, xs):
        qo, ks, vv, dc = xs
        o_inter = jnp.einsum('bhtk,bhkv->bhtv', qo, state)
        state = dc[..., None] * state + jnp.einsum('bhsk,bhsv->bhkv', ks, vv)
        return state, o_inter

    s0 = jnp.zeros((B, H, dk, dv), f32)
    _, o_inter = lax.scan(step, s0, (q_out, k_st, vc, decay))
    o = (o_intra + o_inter).transpose(1, 0, 3, 2, 4).reshape(B, S, H, dv)
    o = rms_norm(o, out_g) * jax.nn.silu(hg.astype(f32))
    return o.reshape(B, S, H * dv).astype(hi.dtype)

def even_mixer(x, w_in, w_out, lam_params, sub_g, lb, hg_g, lam_init, cos, sin):
    B, S, _ = x.shape
    h = x @ w_in
    sizes = (DA_QK_WIDTH, DA_QK_WIDTH, DA_WIDTH, HG_KWIDTH, HG_KWIDTH, HG_WIDTH, HG_WIDTH)
    cuts = [sum(sizes[:i + 1]) for i in range(len(sizes) - 1)]
    qa, ka, va, hq, hf, hi, hg = jnp.split(h, cuts, axis=-1)
    o_a = diff_attention(qa.reshape(B, S, DA_HEADS, 2, DA_HEAD_DIM),
                         ka.reshape(B, S, DA_HEADS, 2, DA_HEAD_DIM),
                         va.reshape(B, S, DA_HEADS, DA_V_DIM),
                         lam_params, sub_g, lam_init, cos, sin)
    o_b = hgrn2(hq.reshape(B, S, HG_HEADS, HG_KDIM), hf.reshape(B, S, HG_HEADS, HG_KDIM),
                hi.reshape(B, S, HG_HEADS, HG_VDIM), hg.reshape(B, S, HG_HEADS, HG_VDIM),
                lb.reshape(HG_HEADS, HG_KDIM), hg_g)
    return jnp.concatenate([o_a.astype(x.dtype), o_b.astype(x.dtype)], axis=-1) @ w_out

def dilated_branch(q, k, v, dil, span):
    B, H, S, hd = q.shape
    L = S // dil

    def to_res(t):
        return t.reshape(B, H, L, dil, hd).transpose(0, 1, 3, 2, 4)

    blk = span
    nb = -(-L // blk)
    pad = nb * blk - L

    def padl(t, front):
        return jnp.pad(t, ((0, 0), (0, 0), (0, 0), (front, pad), (0, 0)))

    qp = padl(to_res(q), 0).reshape(B, H, dil, nb, blk, hd)
    kp = padl(to_res(k), blk).reshape(B, H, dil, nb + 1, blk, hd)
    vp = padl(to_res(v), blk).reshape(B, H, dil, nb + 1, blk, hd)
    kw = jnp.concatenate([kp[:, :, :, :-1], kp[:, :, :, 1:]], axis=-2)
    vw = jnp.concatenate([vp[:, :, :, :-1], vp[:, :, :, 1:]], axis=-2)
    s = jnp.einsum('bhrnqd,bhrnkd->bhrnqk', qp, kw).astype(jnp.float32)
    a_idx = jnp.arange(blk)[:, None]
    c_idx = jnp.arange(2 * blk)[None, :]
    dist = blk + a_idx - c_idx
    key_idx = (jnp.arange(nb)[:, None, None] - 1) * blk + c_idx[None]
    valid = (dist >= 0)[None] & (dist <= span)[None] & (key_idx >= 0)
    s = jnp.where(valid, s, -jnp.inf)
    m = jnp.max(s, axis=-1, keepdims=True)
    e = jnp.exp(s - m)
    den = jnp.sum(e, axis=-1)
    o = jnp.einsum('bhrnqk,bhrnkd->bhrnqd', e.astype(v.dtype), vw) / den[..., None].astype(v.dtype)
    lse = m[..., 0] + jnp.log(den)
    o = o.reshape(B, H, dil, nb * blk, hd)[:, :, :, :L].transpose(0, 1, 3, 2, 4).reshape(B, H, S, hd)
    lse = lse.reshape(B, H, dil, nb * blk)[..., :L].transpose(0, 1, 3, 2).reshape(B, H, S)
    return o, lse

def odd_mixer(x, w_in, w_out, cos, sin):
    B, S, D = x.shape
    q, k, v = jnp.split(x @ w_in, 3, axis=-1)

    def heads(t):
        return t.reshape(B, S, DL_HEADS, DL_HEAD_DIM).transpose(0, 2, 1, 3)

    q = partial_rope(heads(q), cos, sin) * (DL_HEAD_DIM ** -0.5)
    k = partial_rope(heads(k), cos, sin)
    v = heads(v)
    outs, lses = [], []
    for (w, d) in DL_PAIRS:
        o, lse = dilated_branch(q, k, v, d, w // d)
        outs.append(o)
        lses.append(lse)
    wts = jax.nn.softmax(jnp.stack(lses, axis=0), axis=0)
    o = jnp.einsum('gbhs,gbhsd->bhsd', wts.astype(v.dtype), jnp.stack(outs, axis=0))
    return o.transpose(0, 2, 1, 3).reshape(B, S, D) @ w_out

def first_inputs(seed: int = 0) -> dict:
    key = jax.random.key(seed)
    ks = jax.random.split(key, 20)
    f32 = jnp.float32

    def nrm(k, shape, s):
        return jax.random.normal(k, shape, f32) * s

    def gain(k, shape):
        return 1.0 + 0.02 * jax.random.normal(k, shape, f32)

    even_in = 2 * DA_QK_WIDTH + DA_WIDTH + 2 * HG_KWIDTH + 2 * HG_WIDTH
    return {
        "x": nrm(ks[0], (BATCH, SEQ, D_MODEL), 1.0),
        "p": nrm(ks[1], (DEPTH, BATCH, SEQ, PLE_DIM), 1.0),
        "ev_w_in": nrm(ks[2], (N_EVEN, D_MODEL, even_in), D_MODEL ** -0.5),
        "ev_w_out": nrm(ks[3], (N_EVEN, DA_WIDTH + HG_WIDTH, D_MODEL), BETA * (DA_WIDTH + HG_WIDTH) ** -0.5),
        "da_lambda": nrm(ks[4], (N_EVEN, 4, DA_HEAD_DIM), 0.1),
        "da_subln_g": gain(ks[5], (N_EVEN, DA_V_DIM)),
        "hg_lb_logits": nrm(ks[6], (N_EVEN + 1, HG_KWIDTH), 0.1),
        "hg_norm_g": gain(ks[7], (N_EVEN, HG_VDIM)),
        "od_w_in": nrm(ks[8], (N_ODD, D_MODEL, 3 * D_MODEL), D_MODEL ** -0.5),
        "od_w_out": nrm(ks[9], (N_ODD, D_MODEL, D_MODEL), BETA * D_MODEL ** -0.5),
        "ln1_g": gain(ks[10], (DEPTH, D_MODEL)),
        "ln1_b": nrm(ks[11], (DEPTH, D_MODEL), 0.02),
        "ffn_w1": nrm(ks[12], (DEPTH, D_MODEL, FFN_DIM), D_MODEL ** -0.5),
        "ffn_w2": nrm(ks[13], (DEPTH, FFN_DIM, D_MODEL), BETA * FFN_DIM ** -0.5),
        "ln2_g": gain(ks[14], (DEPTH, D_MODEL)),
        "ln2_b": nrm(ks[15], (DEPTH, D_MODEL), 0.02),
        "ple_w_proj": nrm(ks[16], (DEPTH, PLE_DIM, D_MODEL), PLE_DIM ** -0.5),
        "ple_w_gate": nrm(ks[17], (DEPTH, D_MODEL, D_MODEL), D_MODEL ** -0.5),
        "ple_norm_g": gain(ks[18], (DEPTH, D_MODEL)),
    }

def first_block(x, p, ev_w_in, ev_w_out, da_lambda, da_subln_g, hg_lb_logits, hg_norm_g,
              od_w_in, od_w_out, ln1_g, ln1_b, ffn_w1, ffn_w2, ln2_g, ln2_b,
              ple_w_proj, ple_w_gate, ple_norm_g):
    S = x.shape[1]
    cos, sin = rope_tables(S)
    lb_all = jnp.cumsum(jax.nn.softmax(hg_lb_logits.astype(jnp.float32), axis=0), axis=0)
    for l in range(DEPTH):
        j = l // 2
        if l % 2 == 0:
            lam_init = 0.8 - 0.6 * math.exp(-0.3 * l)
            mix = even_mixer(x, ev_w_in[j], ev_w_out[j], da_lambda[j], da_subln_g[j],
                             lb_all[j], hg_norm_g[j], lam_init, cos, sin)
        else:
            mix = odd_mixer(x, od_w_in[j], od_w_out[j], cos, sin)
        x = layer_norm(ALPHA * x + mix, ln1_g[l], ln1_b[l])
        hdn = jnp.square(jax.nn.relu(x @ ffn_w1[l]))
        x = layer_norm(ALPHA * x + hdn @ ffn_w2[l], ln2_g[l], ln2_b[l])
        e = rms_norm(p[l] @ ple_w_proj[l], ple_norm_g[l])
        x = x + jax.nn.sigmoid(x @ ple_w_gate[l]) * e
    return x


GRID_W = 64
CTX_LEN = 256
HEAD_DIM = 64
GLA_HEADS = 4
NA_HEADS = 6
SWA_HEADS = 6
SWA_KV_HEADS = 2
GLA_W = GLA_HEADS * HEAD_DIM
NA_W = NA_HEADS * HEAD_DIM
SWA_W = SWA_HEADS * HEAD_DIM
SWA_KV_W = SWA_KV_HEADS * HEAD_DIM
MIX_WIDTH = GLA_W + NA_W + SWA_W
GLA_RANK = 16
GLA_TAU = 16.0
GLA_CHUNK = 64
NA_KH = 8
NA_KW = 16
NA_QW = 16
NA_CB = NA_KW + NA_QW
SWA_WINDOW = 128
SWA_BLOCK = 128
ROPE_THETA_2 = 10000.0
NORM_EPS = 1e-6
D_FF = -(-8 * D_MODEL // (3 * 256)) * 256
IN_SPLITS = (GLA_W, GLA_W, GLA_W, GLA_W, GLA_RANK, GLA_RANK, NA_W, NA_W, NA_W, SWA_W, SWA_KV_W, SWA_KV_W)
IN_WIDTH = sum(IN_SPLITS)


def rms_norm_2(x, g):
    xf = x.astype(jnp.float32)
    y = xf * lax.rsqrt(jnp.mean(xf * xf, axis=-1, keepdims=True) + NORM_EPS)
    return (y * g.astype(jnp.float32)).astype(x.dtype)

def split_cols(p):
    bounds = [int(b) for b in np.cumsum(IN_SPLITS)[:-1]]
    return jnp.split(p, bounds, axis=-1)

def split_heads(a, n_heads):
    return a.reshape(a.shape[:-1] + (n_heads, HEAD_DIM))

def axial_rope(n_tokens):
    t = jnp.arange(n_tokens, dtype=jnp.int32)
    row = (t // GRID_W).astype(jnp.float32)
    col = (t % GRID_W).astype(jnp.float32)
    n_freq = HEAD_DIM // 4
    inv_freq = ROPE_THETA_2 ** (-jnp.arange(n_freq, dtype=jnp.float32) / n_freq)
    ang = jnp.concatenate([row[:, None] * inv_freq, col[:, None] * inv_freq], axis=-1)
    return jnp.cos(ang), jnp.sin(ang)

def apply_rope(a, cos, sin):
    half = HEAD_DIM // 2
    af = a.astype(jnp.float32)
    a1, a2 = af[..., :half], af[..., half:]
    cs = cos[None, :, None, :]
    sn = sin[None, :, None, :]
    return jnp.concatenate([a1 * cs - a2 * sn, a1 * sn + a2 * cs], axis=-1).astype(a.dtype)

def gla_heads(a):
    B, T, _ = a.shape
    return a.reshape(B, T, GLA_HEADS, HEAD_DIM).transpose(0, 2, 1, 3)

def gla_log_decay(z_low, w2, b2):
    z = (z_low @ w2 + b2).astype(jnp.float32)
    return gla_heads(jax.nn.log_sigmoid(z) / GLA_TAU)

def gla_chunked(q, k, v, log_a, s0):
    B, H, T, dk = q.shape
    dv = v.shape[-1]
    n = T // GLA_CHUNK

    def chunks(a):
        return a.astype(jnp.float32).reshape(B, H, n, GLA_CHUNK, a.shape[-1])

    qc, kc, vc, la = chunks(q), chunks(k), chunks(v), chunks(log_a)
    b = jnp.cumsum(la, axis=3)
    b_last = b[:, :, :, -1:, :]
    q_in = qc * jnp.exp(b)
    k_in = kc * jnp.exp(-b)
    k_end = kc * jnp.exp(b_last - b)
    lower = jnp.tril(jnp.ones((GLA_CHUNK, GLA_CHUNK), dtype=bool))
    a_intra = jnp.where(lower, jnp.einsum('bhncd,bhnsd->bhncs', q_in, k_in), 0.0)
    o_intra = jnp.einsum('bhncs,bhnse->bhnce', a_intra, vc)
    chunk_state = jnp.einsum('bhnsd,bhnse->bhnde', k_end, vc)
    chunk_decay = jnp.exp(b_last[:, :, :, 0, :])

    def step(state, inp):
        dec, cs = inp
        return dec[..., None] * state + cs, state

    s_final, s_enter = lax.scan(step, s0, (jnp.moveaxis(chunk_decay, 2, 0), jnp.moveaxis(chunk_state, 2, 0)))
    o_inter = jnp.einsum('bhncd,nbhde->bhnce', q_in, s_enter)
    o = (o_intra + o_inter).reshape(B, H, T, dv).astype(v.dtype)
    return o, s_final

def gla_final_state(k, v, log_a):
    A = jnp.cumsum(log_a.astype(jnp.float32), axis=2)
    w = jnp.exp(A[:, :, -1:, :] - A)
    return jnp.einsum('bhtd,bhte->bhde', k.astype(jnp.float32) * w, v.astype(jnp.float32))

def gla_output(o, g, norm_g):
    B, H, T, dv = o.shape
    o = rms_norm_2(o.transpose(0, 2, 1, 3), norm_g.reshape(H, dv))
    return o.reshape(B, T, H * dv) * jax.nn.silu(g)

def gla_mixer(parts, parts_c, wa2_f, ba_f, wa2_b, ba_b, norm_g, need_ctx_out):
    q, k, v, g, za_f, za_b = parts
    qc, kc, vc, gc, zac_f, zac_b = parts_c
    scale = HEAD_DIM ** -0.5

    def flip(a):
        return jnp.flip(a, axis=2)

    K_c, V_c = gla_heads(kc), gla_heads(vc)
    la_cf = gla_log_decay(zac_f, wa2_f, ba_f)
    la_cb = gla_log_decay(zac_b, wa2_b, ba_b)
    if need_ctx_out:
        Q_c = gla_heads(qc) * scale
        zeros = jnp.zeros(K_c.shape[:2] + (HEAD_DIM, HEAD_DIM), jnp.float32)
        oc_f, s_f = gla_chunked(Q_c, K_c, V_c, la_cf, zeros)
        oc_b, s_b = gla_chunked(flip(Q_c), flip(K_c), flip(V_c), flip(la_cb), zeros)
        yc = gla_output(oc_f + flip(oc_b), gc, norm_g)
    else:
        s_f = gla_final_state(K_c, V_c, la_cf)
        s_b = gla_final_state(flip(K_c), flip(V_c), flip(la_cb))
        yc = None
    Q, K, V = gla_heads(q) * scale, gla_heads(k), gla_heads(v)
    o_f, _ = gla_chunked(Q, K, V, gla_log_decay(za_f, wa2_f, ba_f), s_f)
    o_b, _ = gla_chunked(flip(Q), flip(K), flip(V), flip(gla_log_decay(za_b, wa2_b, ba_b)), s_b)
    y = gla_output(o_f + flip(o_b), g, norm_g)
    return y, yc

def context_attention(qc, kc, vc, sink):
    B, L, Hq, dh = qc.shape
    Hkv = kc.shape[2]
    G = Hq // Hkv
    s = jnp.einsum('bqhgd,bkhd->bhgqk', qc.reshape(B, L, Hkv, G, dh), kc).astype(jnp.float32) * dh ** -0.5
    if sink is None:
        p = jax.nn.softmax(s, axis=-1)
    else:
        s_sink = jnp.broadcast_to(sink.astype(jnp.float32).reshape(1, Hkv, G, 1, 1), s.shape[:-1] + (1,))
        p = jax.nn.softmax(jnp.concatenate([s, s_sink], axis=-1), axis=-1)[..., :-1]
    o = jnp.einsum('bhgqk,bkhd->bqhgd', p.astype(vc.dtype), vc)
    return o.reshape(B, L, Hq * dh)

def neighborhood_attention(q, k, v, kc, vc, rpb):
    B, T, H, dh = q.shape
    rows = T // GRID_W
    kh = min(NA_KH, rows)
    ncb = GRID_W // NA_QW
    r = np.arange(rows)
    row_idx = np.clip(r - kh // 2, 0, rows - kh)[:, None] + np.arange(kh)[None, :]
    q_cols = np.arange(GRID_W).reshape(ncb, NA_QW)
    win_start = np.clip(q_cols - NA_KW // 2, 0, GRID_W - NA_KW)
    col_idx = np.clip(np.arange(ncb) * NA_QW - NA_KW // 2, 0, GRID_W - NA_CB)[:, None] + np.arange(NA_CB)[None, :]
    key_col = col_idx[:, None, :]
    valid = (key_col >= win_start[:, :, None]) & (key_col < win_start[:, :, None] + NA_KW)
    dr = row_idx - r[:, None] + NA_KH - 1
    dc = np.clip(key_col - q_cols[:, :, None] + NA_KW - 1, 0, 2 * NA_KW - 2)
    bias = rpb.astype(jnp.float32)[:, dr[:, None, None, :, None], dc[None, :, :, None, :]]
    bias = jnp.where(valid[None, None, :, :, None, :], bias, -jnp.inf)

    q_blk = q.reshape(B, rows, ncb, NA_QW, H, dh)
    k_grid = k.reshape(B, rows, GRID_W, H, dh)
    v_grid = v.reshape(B, rows, GRID_W, H, dh)
    ri = row_idx[:, None, :, None]
    ci = col_idx[None, :, None, :]
    k_blk = k_grid[:, ri, ci]
    v_blk = v_grid[:, ri, ci]
    scale = dh ** -0.5
    s_loc = jnp.einsum('brnqhd,brnkchd->bhrnqkc', q_blk, k_blk).astype(jnp.float32) * scale + bias
    n_loc = kh * NA_CB
    s_loc = s_loc.reshape(s_loc.shape[:5] + (n_loc,))
    s_ctx = jnp.einsum('brnqhd,blhd->bhrnql', q_blk, kc).astype(jnp.float32) * scale
    p = jax.nn.softmax(jnp.concatenate([s_loc, s_ctx], axis=-1), axis=-1)
    p_loc = p[..., :n_loc].reshape(p.shape[:5] + (kh, NA_CB)).astype(v.dtype)
    p_ctx = p[..., n_loc:].astype(vc.dtype)
    o = (jnp.einsum('bhrnqkc,brnkchd->brnqhd', p_loc, v_blk)
         + jnp.einsum('bhrnql,blhd->brnqhd', p_ctx, vc))
    return o.reshape(B, T, H * dh)

def sliding_window_attention(q, k, v, kc, vc, sink):
    B, T, Hq, dh = q.shape
    Hkv = k.shape[2]
    G = Hq // Hkv
    bs = SWA_BLOCK
    nb = T // bs
    qb = q.reshape(B, nb, bs, Hkv, G, dh)
    pad = ((0, 0), (bs, bs), (0, 0), (0, 0))
    kp, vp = jnp.pad(k, pad), jnp.pad(v, pad)
    idx = np.arange(nb)[:, None] * bs + np.arange(3 * bs)[None, :]
    kb, vb = kp[:, idx], vp[:, idx]
    kpos = idx - bs
    qpos = np.arange(T).reshape(nb, bs)
    valid = ((np.abs(qpos[:, :, None] - kpos[:, None, :]) <= SWA_WINDOW)
             & (kpos[:, None, :] >= 0) & (kpos[:, None, :] < T))
    scale = dh ** -0.5
    s_loc = jnp.einsum('bnqhgd,bnkhd->bhgnqk', qb, kb).astype(jnp.float32) * scale
    s_loc = jnp.where(valid, s_loc, -jnp.inf)
    s_ctx = jnp.einsum('bnqhgd,blhd->bhgnql', qb, kc).astype(jnp.float32) * scale
    s_sink = jnp.broadcast_to(sink.astype(jnp.float32).reshape(1, Hkv, G, 1, 1, 1), s_loc.shape[:-1] + (1,))
    p = jax.nn.softmax(jnp.concatenate([s_loc, s_ctx, s_sink], axis=-1), axis=-1)
    n_loc = 3 * bs
    L = kc.shape[1]
    p_loc = p[..., :n_loc].astype(v.dtype)
    p_ctx = p[..., n_loc:n_loc + L].astype(vc.dtype)
    o = (jnp.einsum('bhgnqk,bnkhd->bnqhgd', p_loc, vb)
         + jnp.einsum('bhgnql,blhd->bnqhgd', p_ctx, vc))
    return o.reshape(B, T, Hq * dh)

def token_mixers(h, hc, w_in, w_out, wa2_f, ba_f, wa2_b, ba_b, gla_norm, na_rpb, swa_sink, cos, sin, need_ctx_out):
    p = split_cols(h @ w_in)
    pc = split_cols(hc @ w_in)
    y_gla, yc_gla = gla_mixer(p[0:6], pc[0:6], wa2_f, ba_f, wa2_b, ba_b, gla_norm, need_ctx_out)
    nq, nk, nv = (split_heads(a, NA_HEADS) for a in p[6:9])
    nkc, nvc = split_heads(pc[7], NA_HEADS), split_heads(pc[8], NA_HEADS)
    y_na = neighborhood_attention(nq, nk, nv, nkc, nvc, na_rpb)
    sq = apply_rope(split_heads(p[9], SWA_HEADS), cos, sin)
    sk = apply_rope(split_heads(p[10], SWA_KV_HEADS), cos, sin)
    sv = split_heads(p[11], SWA_KV_HEADS)
    skc, svc = split_heads(pc[10], SWA_KV_HEADS), split_heads(pc[11], SWA_KV_HEADS)
    y_swa = sliding_window_attention(sq, sk, sv, skc, svc, swa_sink)
    y = jnp.concatenate([y_gla, y_na, y_swa], axis=-1) @ w_out
    if not need_ctx_out:
        return y, None
    yc_na = context_attention(split_heads(pc[6], NA_HEADS), nkc, nvc, None)
    yc_swa = context_attention(split_heads(pc[9], SWA_HEADS), skc, svc, swa_sink)
    yc = jnp.concatenate([yc_gla, yc_na, yc_swa], axis=-1) @ w_out
    return y, yc

def swiglu(h, w_gate, w_up, w_down):
    return (jax.nn.silu(h @ w_gate) * (h @ w_up)) @ w_down

def second_inputs(seed: int = 0) -> dict:
    key = jax.random.key(seed)
    ks = jax.random.split(key, 24)
    f32 = jnp.float32
    D = D_MODEL

    def nrm(k, shape, s):
        return jax.random.normal(k, shape, f32) * s

    return {
        'x': nrm(ks[0], (BATCH, SEQ, D), 1.0),
        'c': nrm(ks[1], (BATCH, D), 1.0),
        'ctx': nrm(ks[2], (BATCH, CTX_LEN, D), 1.0),
        'c_ctx': nrm(ks[3], (D,), 1.0),
        'w_mod': nrm(ks[4], (DEPTH, D, 6 * D), 0.5 * D ** -0.5),
        'b_mod': nrm(ks[5], (DEPTH, 6 * D), 0.02),
        'norm_mix': 1.0 + nrm(ks[6], (DEPTH, D), 0.05),
        'norm_ffn': 1.0 + nrm(ks[7], (DEPTH, D), 0.05),
        'w_in': nrm(ks[8], (DEPTH, D, IN_WIDTH), D ** -0.5),
        'gla_wa2_f': nrm(ks[9], (DEPTH, GLA_RANK, GLA_W), GLA_RANK ** -0.5),
        'gla_ba_f': nrm(ks[10], (DEPTH, GLA_W), 0.5),
        'gla_wa2_b': nrm(ks[11], (DEPTH, GLA_RANK, GLA_W), GLA_RANK ** -0.5),
        'gla_ba_b': nrm(ks[12], (DEPTH, GLA_W), 0.5),
        'gla_norm': 1.0 + nrm(ks[13], (DEPTH, GLA_W), 0.05),
        'na_rpb': nrm(ks[14], (DEPTH, NA_HEADS, 2 * NA_KH - 1, 2 * NA_KW - 1), 0.1),
        'swa_sink': nrm(ks[15], (DEPTH, SWA_HEADS), 0.5),
        'w_out': nrm(ks[16], (DEPTH, MIX_WIDTH, D), MIX_WIDTH ** -0.5),
        'w_gate': nrm(ks[17], (DEPTH, D, D_FF), D ** -0.5),
        'w_up': nrm(ks[18], (DEPTH, D, D_FF), D ** -0.5),
        'w_down': nrm(ks[19], (DEPTH, D_FF, D), D_FF ** -0.5),
        'final_norm': 1.0 + nrm(ks[20], (D,), 0.05),
    }

def second_block(x, c, ctx, c_ctx, w_mod, b_mod, norm_mix, norm_ffn, w_in, gla_wa2_f, gla_ba_f, gla_wa2_b, gla_ba_b,
              gla_norm, na_rpb, swa_sink, w_out, w_gate, w_up, w_down, final_norm):
    T = x.shape[1]
    cos, sin = axial_rope(T)
    s_lat = jax.nn.silu(c)
    s_ctx = jax.nn.silu(c_ctx)
    xc = ctx
    for i in range(DEPTH):
        need_ctx_out = i < DEPTH - 1
        mod = (s_lat @ w_mod[i] + b_mod[i])[:, None, :]
        mod_c = s_ctx @ w_mod[i] + b_mod[i]
        sh1, sc1, g1, sh2, sc2, g2 = jnp.split(mod, 6, axis=-1)
        sh1c, sc1c, g1c, sh2c, sc2c, g2c = jnp.split(mod_c, 6, axis=-1)
        h = rms_norm_2(x, norm_mix[i]) * (1.0 + sc1) + sh1
        hc = rms_norm_2(xc, norm_mix[i]) * (1.0 + sc1c) + sh1c
        y, yc = token_mixers(h, hc, w_in[i], w_out[i], gla_wa2_f[i], gla_ba_f[i], gla_wa2_b[i], gla_ba_b[i],
                             gla_norm[i], na_rpb[i], swa_sink[i], cos, sin, need_ctx_out)
        x = x + g1 * y
        h = rms_norm_2(x, norm_ffn[i]) * (1.0 + sc2) + sh2
        x = x + g2 * swiglu(h, w_gate[i], w_up[i], w_down[i])
        if need_ctx_out:
            xc = xc + g1c * yc
            hc = rms_norm_2(xc, norm_ffn[i]) * (1.0 + sc2c) + sh2c
            xc = xc + g2c * swiglu(hc, w_gate[i], w_up[i], w_down[i])
    return rms_norm_2(x, final_norm)


def setup_inputs(seed=0):
    out = dict(first_inputs(seed))
    for name, value in second_inputs(seed + 1).items():
        if name != "x":
            out[name + "_2"] = value
    return out


def reference(
    x, p, ev_w_in, ev_w_out, da_lambda, da_subln_g, hg_lb_logits, hg_norm_g, od_w_in, od_w_out,
    ln1_g, ln1_b, ffn_w1, ffn_w2, ln2_g, ln2_b, ple_w_proj, ple_w_gate, ple_norm_g, c_2, ctx_2,
    c_ctx_2, w_mod_2, b_mod_2, norm_mix_2, norm_ffn_2, w_in_2, gla_wa2_f_2, gla_ba_f_2,
    gla_wa2_b_2, gla_ba_b_2, gla_norm_2, na_rpb_2, swa_sink_2, w_out_2, w_gate_2, w_up_2,
    w_down_2, final_norm_2,
):
    x = first_block(
        x, p, ev_w_in, ev_w_out, da_lambda, da_subln_g, hg_lb_logits, hg_norm_g, od_w_in,
        od_w_out, ln1_g, ln1_b, ffn_w1, ffn_w2, ln2_g, ln2_b, ple_w_proj, ple_w_gate,
        ple_norm_g,
    )
    return second_block(
        x, c_2, ctx_2, c_ctx_2, w_mod_2, b_mod_2, norm_mix_2, norm_ffn_2, w_in_2, gla_wa2_f_2,
        gla_ba_f_2, gla_wa2_b_2, gla_ba_b_2, gla_norm_2, na_rpb_2, swa_sink_2, w_out_2,
        w_gate_2, w_up_2, w_down_2, final_norm_2,
    )


_drawn_inputs = setup_inputs


def setup_inputs(seed=0):
    import zlib

    import numpy as np

    out = dict(_drawn_inputs(seed))
    spreads = {}
    factors = {'da_lambda': 8.0,
     'da_subln_g': 8.0,
     'hg_lb_logits': 8.0,
     'hg_norm_g': 8.0,
     'ple_norm_g': 4.135,
     'norm_mix_2': 4.272,
     'norm_ffn_2': 3.006,
     'gla_wa2_f_2': 2.898,
     'gla_norm_2': 8.0,
     'na_rpb_2': 8.0,
     'swa_sink_2': 8.0}
    for name, (base, spread) in spreads.items():
        noise = np.random.default_rng([zlib.crc32(name.encode()), seed]).standard_normal(out[name].shape)
        drawn = base * np.exp(spread * noise) if base else spread * noise
        out[name] = jnp.asarray(drawn.astype(out[name].dtype))
    for name, factor in factors.items():
        out[name] = (out[name] * factor).astype(out[name].dtype)
    return out
```

```python
import math
from contextlib import ExitStack

import numpy as np

import concourse.bass as bass
from concourse import mybir
from concourse.alu_op_type import AluOpType as ALU

F32 = mybir.dt.float32
U32 = mybir.dt.uint32
ACT = mybir.ActivationFunctionType
AX = mybir.AxisListType

P = 128
D = 1024
DC = D // P
SEQ = 256
CTX = 256
T2 = CTX + SEQ
NQ = SEQ // P
DEPTH = 2
PLE = 256
FFN = 4 * D
DFF = 2816
CH = 64
HEADS_E = 4
HEADS_O = 16
GLA_W, NA_W, SWA_W, SWA_KV = 256, 384, 384, 128
NA_H, SWA_H, SWA_G = 6, 6, 3
GRID_W = 64
RANK = 16
ALPHA = (2 * DEPTH) ** 0.25
LAM_INIT = 0.8 - 0.6 * math.exp(0.0)
EPS1, EPS2 = 1e-5, 1e-6
HD = 64
QSCALE = HD ** -0.5
NEG = -1e30
RPB_R, RPB_C = 15, 2 * GRID_W - 1

TB = 16
RING = 5


def consts():
    p = np.arange(P)
    out = {}
    out["ident"] = np.eye(P)
    out["meanD"] = np.full((P, P), 1.0 / D)
    out["mean128"] = np.full((P, P), 1.0 / P)
    out["mean64"] = (p[:, None] // HD == p[None, :] // HD) / HD
    def rotation(half):
        r = np.zeros((P, P))
        for m in range(P):
            base, d = m // HD * HD, m % HD
            if d < half:
                r[base + d + half, m] = -1.0
            elif d < 2 * half:
                r[base + d - half, m] = 1.0
        return r
    out["rot1"], out["rot2"] = rotation(8), rotation(32)
    t = np.arange(SEQ)
    d = p % HD
    inv1 = (np.float32(500000.0) ** (-np.arange(0, 16, 2, dtype=np.float32) / np.float32(16))).astype(np.float32)
    ang1 = (t.astype(np.float32)[:, None] * inv1[None, :]).astype(np.float32)
    rot = (d < 16)[:, None]
    out["cos1"] = np.where(rot, np.cos(ang1)[:, d % 8].T, 1.0)
    out["sin1"] = np.where(rot, np.sin(ang1)[:, d % 8].T, 0.0)
    inv2 = (np.float32(10000.0) ** (-np.arange(16, dtype=np.float32) / np.float32(16))).astype(np.float32)
    row, col = (t // GRID_W).astype(np.float32), (t % GRID_W).astype(np.float32)
    ang2 = np.concatenate([row[:, None] * inv2, col[:, None] * inv2], -1).astype(np.float32)
    out["cos2"], out["sin2"] = np.cos(ang2)[:, d % 32].T, np.sin(ang2)[:, d % 32].T
    q = (np.arange(NQ)[None, :, None] * P + p[:, None, None])
    k = np.arange(SEQ)[None, None, :]
    out["causal"] = np.where(k <= q, 0.0, NEG)
    n = ((k <= q) & (q - k <= 128)) * 1.0 + ((k <= q) & ((q - k) % 4 == 0)) + ((k <= q) & ((q - k) % 16 == 0))
    out["dilated"] = np.where(n > 0, np.log(np.maximum(n, 1)), NEG)
    swa = np.where(np.abs(q - k) <= 128, 0.0, NEG)
    out["window"] = np.concatenate([np.zeros((P, NQ, CTX)), swa], -1)
    start = np.clip(q % GRID_W - 8, 0, GRID_W - 16)
    out["near"] = np.where((k % GRID_W >= start) & (k % GRID_W < start + 16), 0.0, NEG)
    s, tt = p[:, None] % CH, np.arange(CH)[None, :]
    out["before"] = (s <= tt) * 1.0
    out["after"] = (s >= tt) * 1.0
    out["cols"] = np.tile(np.array([EPS1, EPS2, 1.0, 0.0]), (P, 1))
    return {a: np.ascontiguousarray(b.reshape(P, -1).astype(np.float32)) for a, b in out.items()}


CONST = consts()

PARAMS = {}
for _n, _w in [("ln1_g", 16), ("ln1_b", 16), ("ln2_g", 16), ("ln2_b", 16), ("ple_g", 16), ("sub_g", 1), ("hg_g", 1),
               ("lb", 8), ("norm_mix", 16), ("norm_ffn", 16), ("final", 8), ("b_mod", 96), ("ba", 8), ("gla_norm", 4),
               ("sink", 12), ("lam", 256), ("cc", 16)]:
    PARAMS[_n] = (sum(w for _, w in PARAMS.values()), _w)
NPAR = sum(w for _, w in PARAMS.values())


class Queue:

    def __init__(self, nc, eng, sem):
        self.nc, self.eng, self.sem, self.n, self.seen = nc, eng, sem, 0, {}

    def wait(self, *tokens):
        for t in tokens:
            if t is None:
                continue
            sem, val, key = t
            if self.seen.get(key, 0) < val:
                self.eng.wait_ge(sem, val)
                self.seen[key] = val

    def done(self, ins):
        ins.then_inc(self.sem, 1)
        self.n += 1
        return (self.sem, self.n, id(self))

    def now(self):
        return (self.sem, self.n, id(self)) if self.n else None


class Program:
    def __init__(self, nc, ctx, io):
        self.nc, self.io = nc, io
        sb = lambda name, *shape: ctx.enter_context(nc.sbuf_tensor(name, [P, *shape], F32))
        sem = lambda name: ctx.enter_context(nc.semaphore(name))
        self.pe = Queue(nc, nc.tensor, sem("tensor_done"))
        self.act = Queue(nc, nc.scalar, sem("scalar_done"))
        self.dve = Queue(nc, nc.vector, sem("vector_done"))
        self.pool = Queue(nc, nc.gpsimd, sem("gpsimd_done"))
        self.s_tile = [sem(f"tile_loaded{i}") for i in range(RING)]
        self.s_free = sem("tile_free")
        self.s_start = [sem(f"loaded{i}") for i in range(4)]
        self.s_bias = [sem(f"bias_loaded{i}") for i in range(2)]
        self.s_wa2 = sem("wa2_loaded")
        self.s_out = sem("stored")
        self.ring = sb("ring", RING, TB * P)
        self.X = sb("X", DC, T2)
        self.H = sb("H", DC, T2)
        self.BIG = sb("BIG", 11776)
        self.SCR = sb("SCR", 5888)
        self.Tt = sb("Tt", 2, 1024)
        self.PT = sb("PT", 2, 1024)
        self.NB = sb("NB", 2, 1024)
        self.SQ = sb("SQ", 2, 512)
        self.RS = sb("RS", 512)
        self.TMP = sb("TMP", 2, 512)
        self.par = sb("par", NPAR)
        self.wa2 = sb("wa2", 256)
        self.mod = sb("mod", 2, 48, 2)
        self.gs = sb("gs", 16)
        self.small = sb("small", 64)
        self.keep = sb("keep", 1024)
        self.c = {n: sb("c_" + n, a.shape[1]) for n, a in CONST.items()}
        self.bank = [ctx.enter_context(nc.psum_tensor(f"bank{i}", [P, 512], F32)) for i in range(8)]
        self.read = [None] * 8
        self.turn = {"gemm": 0, "score": 0, "turned": 0, "out": 0}
        self.first = {"gemm": 0, "score": 2, "turned": 4, "out": 6}
        self.blocks = []
        self.tile_seen = -1
        self.freed = 0
        self.sq_read, self.rs_read, self.pt_read, self.T_read = [None, None], None, [None, None], [None, None]
        self.nb_read, self.bias_count = [None, None], [0, 0]
        self.turn_tmp = self.turn_small = self.turn_T = self.turn_PT = 0

    def col(self, name, i=0, n=1):
        o, w = PARAMS[name]
        return self.par[:, o + i:o + i + n]

    def take(self, pool):
        b = self.first[pool] + self.turn[pool] % 2
        self.turn[pool] += 1
        self.pe.wait(self.read[b])
        self.read[b] = None
        return b

    def fence(self):
        queues = [self.pe, self.act, self.dve, self.pool]
        marks = [q.now() for q in queues]
        for q in queues:
            q.wait(*marks)

    def weights(self, requests):
        at = len(self.blocks)
        self.blocks += requests
        tile, o = at // TB, at % TB
        assert o + len(requests) <= TB
        if tile > self.tile_seen:
            self.nc.tensor.wait_ge(self.s_tile[tile % RING], 16 * (tile // RING + 1))
            self.tile_seen = tile
        return self.ring[:, tile % RING, o * P:(o + len(requests)) * P]

    def matmul(self, *a, hold=False, **kw):
        mm = self.nc.tensor.matmul(*a, **kw)
        if not hold and self.freed < len(self.blocks) // TB:
            mm.then_inc(self.s_free, 1)
            self.freed += 1
        return mm

    def last_matmul(self, *a, **kw):
        return self.pe.done(self.nc.tensor.matmul(*a, **kw))

    def product(self, out, name, layer, col, kc, moving):
        for k in range(kc - 1):
            w = self.weights([(name, layer, k, col)])
            self.matmul(out, w, moving(k), start=(k == 0), stop=False)
        w = self.weights([(name, layer, kc - 1, col)])
        return self.last_matmul(out, w, moving(kc - 1), start=(kc == 1), stop=True)

    def rows_product(self, outs, name, layer, cols, kc, stationary):
        tok = None
        for k in range(kc):
            w = self.weights([(name, layer, k, c) for c in cols])
            for i, out in enumerate(outs):
                kw = dict(start=(k == 0), stop=(k == kc - 1))
                if k == kc - 1:
                    tok = self.last_matmul(out, stationary(k, i), w, **kw)
                else:
                    self.matmul(out, stationary(k, i), w, hold=(i < len(outs) - 1), **kw)
        return tok


def on(q, waits, fn, *a, **kw):
    q.wait(*waits)
    return q.done(fn(*a, **kw))


def cols(ap, n):
    return ap.unsqueeze(2)


SEQS = slice(CTX, T2)


def emit(k):
    nc, pe, act, dve, pool = k.nc, k.pe, k.act, k.dve, k.pool
    load_inputs(k)
    first_block(k)
    second_block(k)


def load_inputs(k):
    nc, io = k.nc, k.io
    s0 = k.s_start[0]
    n = 0
    order = list(CONST)
    for name in order:
        nc.scalar.dma_start(k.c[name][:, :], io[name]).then_inc(s0, 16)
        n += 16
    nc.scalar.dma_start(k.par[:, :], io["params"]).then_inc(s0, 16)
    nc.scalar.dma_start(k.X[:, :, SEQS], io["x"]).then_inc(s0, 16)
    nc.scalar.dma_start(k.X[:, :, 0:CTX], io["ctx"]).then_inc(s0, 16)
    n += 48
    for q in (k.pe, k.act, k.dve, k.pool):
        q.eng.wait_ge(s0, n)
    t = on(k.dve, [], nc.vector.memset, k.keep[:, :], 1.0)
    on(k.dve, [t], nc.vector.memset, k.keep[:, :].rearrange("p (c t) -> p c t", t=CH)[:, :, 0:1], 0.0)
    on(k.pool, [], nc.gpsimd.memset, k.NB[:, :, :], 0.0)
    k.negsink = k.small[:, 52:64]
    on(k.dve, [], nc.vector.tensor_scalar, k.negsink, k.col("sink", 0, 12), -1.0, None, ALU.mult)
    k.fence()



def mean_squares(k, chunks, stat, n, toks):
    nc = k.nc
    b = k.take("out")
    t = None
    for i, (x, tok) in enumerate(zip(chunks, toks)):
        sq = k.SQ[:, i % 2, 0:n]
        ts = on(k.act, [tok, k.sq_read[i % 2]], nc.scalar.activation, sq, x, ACT.Square)
        k.pe.wait(ts)
        t = k.sq_read[i % 2] = k.last_matmul(k.bank[b][:, 0:n], stat, sq, start=(i == 0), stop=(i == len(chunks) - 1))
    return b, t


def rsqrt_of(k, b, n, t, eps_col):
    nc = k.nc
    t = on(k.act, [t, k.rs_read], nc.scalar.activation, k.RS[:, 0:n], k.bank[b][:, 0:n], ACT.Ln,
           bias=k.c["cols"][:, eps_col:eps_col + 1])
    k.read[b] = t
    return on(k.act, [t], nc.scalar.activation, k.RS[:, 0:n], k.RS[:, 0:n], ACT.Exp, scale=-0.5)


def layer_norm(k, g, b, layer, toks):
    nc = k.nc
    bank = k.take("out")
    for i in range(DC):
        k.pe.wait(toks[i])
        args = (k.bank[bank][:, 0:SEQ], k.c["meanD"][:, :], k.X[:, i, SEQS])
        if i < DC - 1:
            k.matmul(*args, start=(i == 0), stop=False)
        else:
            t = k.last_matmul(*args, start=False, stop=True)
    centred = []
    for i in range(DC // 2):
        xs = k.X[:, 2 * i:2 * i + 2, SEQS]
        mean = k.bank[bank][:, 0:SEQ].unsqueeze(1).to_broadcast([P, 2, SEQ])
        tc = on(k.dve, [t], nc.vector.tensor_tensor, xs, xs, mean, ALU.subtract)
        centred += [tc, tc]
    k.read[bank] = centred[-1]
    b2, t = mean_squares(k, [k.X[:, i, SEQS] for i in range(DC)], k.c["meanD"][:, :], SEQ, centred)
    t = rsqrt_of(k, b2, SEQ, t, 0)
    out = []
    for i in range(DC):
        x = k.X[:, i, SEQS]
        ts = on(k.dve, [t], nc.vector.scalar_tensor_tensor, x, x, k.col(g, layer * DC + i), k.RS[:, 0:SEQ],
                ALU.mult, ALU.mult)
        out.append(on(k.act, [ts], nc.scalar.activation, x, x, ACT.Identity, bias=k.col(b, layer * DC + i)))
    k.rs_read = ts
    return out


def rms_heads(k, o, stat, g, gate, n, eps_col, toks, into):
    nc = k.nc
    out = []
    for i, x in enumerate(o):
        b, t = mean_squares(k, [x], stat, n, [toks[i]])
        t = rsqrt_of(k, b, n, t, eps_col)
        t = on(k.dve, [t], nc.vector.scalar_tensor_tensor, into[i], x, g(i), k.RS[:, 0:n], ALU.mult, ALU.mult)
        k.rs_read = t
        if gate is not None:
            t = on(k.dve, [t], nc.vector.tensor_tensor, into[i], into[i], gate(i), ALU.mult)
        out.append(t)
    return out



def rope(k, dst, rot, cos, sin, tok):
    nc = k.nc
    b = k.take("out")
    k.pe.wait(tok)
    t = k.last_matmul(k.bank[b][:, 0:SEQ], rot, dst, start=True, stop=True)
    tmp = k.TMP[:, k.turn_tmp % 2, 0:SEQ]
    k.turn_tmp += 1
    t1 = on(k.dve, [t, k.dve.now()], nc.vector.tensor_tensor, tmp, k.bank[b][:, 0:SEQ], sin, ALU.mult)
    k.read[b] = t1
    t2 = on(k.dve, [t], nc.vector.tensor_tensor, dst, dst, cos, ALU.mult)
    return on(k.dve, [t1, t2], nc.vector.tensor_tensor, dst, dst, tmp, ALU.add)



def softmax_rows(k, scores, bias, T, t_scores, start, sink=None):
    nc = k.nc
    c = 4 * (k.turn_small % 8)
    k.turn_small += 1
    nm, den, rd, es = (k.small[:, c + i:c + i + 1] for i in range(4))
    t = on(k.dve, [t_scores], nc.vector.tensor_tensor_reduce, T, scores, bias, -1.0,
           start, ALU.add, ALU.min, nm)
    t_max = t
    t = on(k.act, [t], nc.scalar.activation, T, T, ACT.Exp, bias=nm, scale=-1.0, accum_out=den)
    if sink is not None:
        ts = on(k.act, [t_max], nc.scalar.activation, es, sink, ACT.Exp, bias=nm)
        t = on(k.dve, [ts], nc.vector.tensor_tensor, den, den, es, ALU.add)
    t = on(k.dve, [t], nc.vector.reciprocal, rd, den)
    return t_max, t, rd


def turn(k, blocks, keys, PTi, toks, copy_on):
    nc = k.nc
    PT = k.PT[:, PTi, :].rearrange("p (a q) -> p a q", q=SEQ)
    k.pe.wait(*toks)
    out = []
    tp = None
    for pair in range((keys + 1) // 2):
        b = k.take("turned")
        mine = [x for x in blocks if x[0] // 2 == pair]
        for kt, qt, src in mine:
            o = (kt % 2) * SEQ + qt * P
            tp = pe_t = k.pe.done(nc.tensor.transpose(k.bank[b][:, o:o + P], src, k.c["ident"][:, :]))
        have = {kt: min(q for a, q, _ in mine if a == kt) * P for kt, _, _ in mine}
        runs = [(min(have), 0, len(have) * SEQ)] if not any(have.values()) else \
            [(kt, q0, SEQ - q0) for kt, q0 in have.items()]
        q, copy = (k.act, nc.scalar.copy) if (pair + copy_on) % 2 == 0 else (k.dve, nc.vector.tensor_copy)
        flat = k.PT[:, PTi, :]
        for kt, q0, n in runs:
            at = (kt % 2) * SEQ + q0
            t = on(q, [pe_t, k.pt_read[PTi]], copy, flat[:, kt * SEQ + q0:kt * SEQ + q0 + n], k.bank[b][:, at:at + n])
        out.append(t)
        k.read[b] = t
    return PT, out, tp


def attend(k, units):
    staged = []
    for i, u in enumerate(units):
        staged.append(scores_of(k, u, i))
        if i >= 1:
            values_of(k, units[i - 1], staged[i - 1], i - 1)
    values_of(k, units[-1], staged[-1], len(units) - 1)


def scores_of(k, u, i):
    nc = k.nc
    Ti = k.turn_T % 2
    k.turn_T += 1
    T = k.Tt[:, Ti, :]
    k.dve.wait(k.T_read[Ti])
    rows = []
    if u["prepare"] is not None:
        u["prepare"]()
    for (bank_cols, parts) in u["scores"]:
        b = k.take("score")
        for (o, n, q, kk) in parts:
            t = k.last_matmul(k.bank[b][:, o:o + n], q, kk, start=(o == 0), stop=True, skip_group_check=True)
        for (o, n, q, kk), (To, bias, start, sink) in zip(parts, bank_cols):
            t_max, t_rd, rd = softmax_rows(k, k.bank[b][:, o:o + n], bias, T[:, To:To + n], t, start, sink)
            rows.append((To, n, t_rd, rd))
        k.read[b] = t_max
    if u.get("nb") is not None:
        k.nb_read[u["nb"]] = t_max
    return Ti, rows


def values_of(k, u, staged, i):
    nc = k.nc
    Ti, rows = staged
    T = k.Tt[:, Ti, :]
    toks = []
    if u["diff"]:
        h = len(rows) // 2
        for (To, n, t, rd), (To1, _, t1, rd1) in zip(rows[:h], rows[h:]):
            ta = on(k.dve, [t], nc.vector.tensor_scalar, T[:, To:To + n], T[:, To:To + n], rd, None, ALU.mult)
            tb = on(k.dve, [t1], nc.vector.tensor_tensor, rd1, rd1, k.neglam, ALU.mult)
            toks.append(on(k.dve, [ta, tb], nc.vector.scalar_tensor_tensor, T[:, To:To + n], T[:, To1:To1 + n], rd1,
                           T[:, To:To + n], ALU.mult, ALU.add))
        rows = rows[:h]
    else:
        for (To, n, t, rd) in rows:
            toks.append(on(k.dve, [t], nc.vector.tensor_scalar, T[:, To:To + n], T[:, To:To + n], rd, None, ALU.mult))
    blocks = [(kt, qt, T[:, To + kt * P:To + (kt + 1) * P]) for qt, (To, n, _, _) in enumerate(rows) for kt in range(n // P)]
    keys = max(kt for kt, _, _ in blocks) + 1
    PTi = k.turn_PT % 2
    k.turn_PT += 1
    PT, copied, t_turned = turn(k, blocks, keys, PTi, toks, k.turn_PT % 2 if keys == 2 else 0)
    k.T_read[Ti] = t_turned
    if u["first"]:
        k.obank = k.take("out")
    out = k.bank[k.obank][u["rows"], 0:SEQ]
    k.pe.wait(*copied)
    for kt in range(keys):
        q0 = min(q for a, q, _ in blocks if a == kt) * P
        args = (out[:, q0:SEQ], u["v"](kt), PT[:, kt, q0:SEQ])
        kw = dict(start=(kt == 0), stop=(kt == keys - 1))
        if kt < keys - 1:
            k.matmul(*args, **kw)
        else:
            t = k.last_matmul(*args, **kw)
    k.pt_read[PTi] = t
    if u["last"]:
        k.read[k.obank] = on(k.act, [t], nc.scalar.copy, u["to"], k.bank[k.obank][:, 0:SEQ])
        u["tok"].append(k.read[k.obank])


BIGNUM = 3.0e38


def view(buf, off, *dims):
    n = int(np.prod(dims))
    v = buf[:, off:off + n]
    if len(dims) == 1:
        return v
    if len(dims) == 2:
        return v.rearrange("p (a b) -> p a b", b=dims[1])
    if len(dims) == 3:
        return v.rearrange("p (a b c) -> p a b c", b=dims[1], c=dims[2])
    return v.rearrange("p (a b c d) -> p a b c d", b=dims[1], c=dims[2], d=dims[3])


def project(k, name, layer, ncols, dst, scale=1.0, func=None, toks=None, kc=DC, first=0):
    nc = k.nc
    out = []
    for i in range(ncols):
        b = k.take("gemm")
        if i == 0 and toks:
            k.pe.wait(*toks)
        t = k.product(k.bank[b][:, 0:SEQ], name, layer, first + i, kc, lambda c: k.X[:, c, SEQS])
        t = on(k.act, [t], nc.scalar.activation, dst(i), k.bank[b][:, 0:SEQ], func or ACT.Copy, scale=scale)
        k.read[b] = t
        out.append(t)
    return out


def first_block(k):
    nc = k.nc
    for layer in range(DEPTH):
        if layer == 0:
            even_mixer(k)
            w_out = "ev_w_out"
        else:
            odd_mixer(k)
            w_out = "od_w_out"
        toks = residual(k, w_out, 0, lambda c: k.H[:, c, SEQS], DC)
        toks = layer_norm(k, "ln1_g", "ln1_b", layer, toks)
        hid = view(k.BIG, 0, FFN // P, SEQ)
        th = []
        for i in range(FFN // P):
            b = k.take("gemm")
            if i == 0:
                k.pe.wait(*toks)
            t = k.product(k.bank[b][:, 0:SEQ], "ffn_w1", layer, i, DC, lambda c: k.X[:, c, SEQS])
            tmp = k.TMP[:, i % 2, 0:SEQ]
            t = on(k.act, [t, th[i - 2] if i >= 2 else None], nc.scalar.activation, tmp, k.bank[b][:, 0:SEQ], ACT.Relu)
            t = on(k.dve, [t], nc.vector.scalar_tensor_tensor, hid[:, i, :], k.bank[b][:, 0:SEQ], 0.0, tmp,
                   ALU.max, ALU.mult)
            k.read[b] = t
            th.append(t)
        k.pe.wait(*th)
        toks = residual(k, "ffn_w2", layer, lambda c: hid[:, c, :], FFN // P)
        toks = layer_norm(k, "ln2_g", "ln2_b", layer, toks)
        per_layer_embedding(k, layer, toks)
        k.fence()


def residual(k, name, layer, moving, kc):
    nc, out = k.nc, []
    for i in range(DC):
        b = k.take("gemm")
        t = k.product(k.bank[b][:, 0:SEQ], name, layer, i, kc, moving)
        x = k.X[:, i, SEQS]
        t = on(k.dve, [t], nc.vector.scalar_tensor_tensor, x, x, ALPHA, k.bank[b][:, 0:SEQ], ALU.mult, ALU.add)
        k.read[b] = t
        out.append(t)
    return out


def per_layer_embedding(k, layer, toks):
    nc = k.nc
    pT, e = view(k.BIG, 8192, PLE // P, SEQ), view(k.BIG, 9216, DC, SEQ)
    k.pool.wait(k.pe.now())
    nc.gpsimd.dma_start(pT, k.io["p"][layer]).then_inc(k.s_start[1 + layer], 16)
    nc.tensor.wait_ge(k.s_start[1 + layer], 16)
    te = []
    for i in range(DC):
        b = k.take("gemm")
        t = k.product(k.bank[b][:, 0:SEQ], "ple_w_proj", layer, i, PLE // P, lambda c: pT[:, c, :])
        t = on(k.act, [t], nc.scalar.copy, e8(k, i), k.bank[b][:, 0:SEQ])
        k.read[b] = t
        te.append(t)
    b, t = mean_squares(k, [e8(k, i) for i in range(DC)], k.c["meanD"][:, :], SEQ, te)
    t = rsqrt_of(k, b, SEQ, t, 0)
    tn = [on(k.dve, [t], nc.vector.scalar_tensor_tensor, e8(k, i), e8(k, i), k.col("ple_g", layer * DC + i),
             k.RS[:, 0:SEQ], ALU.mult, ALU.mult) for i in range(DC)]
    k.rs_read = tn[-1]
    gates = []
    for i in range(DC):
        b = k.take("gemm")
        if i == 0:
            k.pe.wait(*toks)
        t = k.product(k.bank[b][:, 0:SEQ], "ple_w_gate", layer, i, DC, lambda c: k.X[:, c, SEQS])
        g = view(k.BIG, 0, DC, SEQ)[:, i, :]
        t = on(k.act, [t], nc.scalar.activation, g, k.bank[b][:, 0:SEQ], ACT.Sigmoid)
        k.read[b] = t
        gates.append(on(k.dve, [t, tn[i]], nc.vector.tensor_tensor, g, g, e8(k, i), ALU.mult))
    t_all = k.pe.now()
    for i in range(DC):
        x = k.X[:, i, SEQS]
        on(k.dve, [gates[i], t_all], nc.vector.tensor_tensor, x, x, view(k.BIG, 0, DC, SEQ)[:, i, :], ALU.add)


def e8(k, i):
    return k.SCR[:, i * SEQ:(i + 1) * SEQ]


def head_rows(h):
    return slice(HD * (h % 2), HD * (h % 2) + HD)


def even_mixer(k):
    nc = k.nc
    qT, kT = view(k.BIG, 0, 4, SEQ), view(k.BIG, 1024, 4, SEQ)
    V = view(k.BIG, 2048, NQ, 512)
    hq, hf, hg = view(k.BIG, 3072, 4, SEQ), view(k.BIG, 4096, 4, SEQ), view(k.BIG, 5120, 4, SEQ)
    HV = view(k.BIG, 6144, NQ, 512)
    tq = project(k, "ev_w_in", 0, 4, lambda i: qT[:, i, :], scale=QSCALE, first=0)
    tq = [rope(k, qT[:, i, :], k.c["rot1"][:, :], k.c["cos1"][:, :], k.c["sin1"][:, :], tq[i]) for i in range(4)]
    tk = project(k, "ev_w_in", 0, 4, lambda i: kT[:, i, :], first=4)
    tk = [rope(k, kT[:, i, :], k.c["rot1"][:, :], k.c["cos1"][:, :], k.c["sin1"][:, :], tk[i]) for i in range(4)]
    value_rows(k, "ev_w_in", 0, [8, 9, 10, 11], V, 0, lambda c, i: k.X[:, c, CTX + i * P:CTX + (i + 1) * P])
    project(k, "ev_w_in", 0, 4, lambda i: hq[:, i, :], func=ACT.Silu, first=12)
    project(k, "ev_w_in", 0, 4, lambda i: hf[:, i, :], func=ACT.Sigmoid, first=16)
    value_rows(k, "ev_w_in", 0, [20, 21, 22, 23], HV, 0, lambda c, i: k.X[:, c, CTX + i * P:CTX + (i + 1) * P])
    project(k, "ev_w_in", 0, 4, lambda i: hg[:, i, :], func=ACT.Silu, first=24)
    lp = k.col("lam", 0, 256)
    c = k.small[:, 32:40]
    t0 = on(k.dve, [], nc.vector.tensor_tensor_reduce, lp[:, 0:64], lp[:, 0:64], lp[:, 64:128], 1.0, 0.0, ALU.mult,
            ALU.add, c[:, 0:1])
    t1 = on(k.dve, [], nc.vector.tensor_tensor_reduce, lp[:, 128:192], lp[:, 128:192], lp[:, 192:256], 1.0, 0.0,
            ALU.mult, ALU.add, c[:, 1:2])
    t = on(k.act, [t0, t1], nc.scalar.activation, c[:, 2:4], c[:, 0:2], ACT.Exp)
    t = on(k.dve, [t], nc.vector.tensor_tensor, c[:, 4:5], c[:, 3:4], c[:, 2:3], ALU.subtract)
    k.neglam = c[:, 4:5]
    on(k.dve, [t], nc.vector.tensor_scalar, k.neglam, k.neglam, -LAM_INIT, None, ALU.add)
    g = c[:, 5:6]
    on(k.dve, [], nc.vector.tensor_scalar, g, k.col("sub_g"), 1.0 - LAM_INIT, None, ALU.mult)
    lb, oml = k.small[:, 40:44], k.small[:, 44:48]
    t = on(k.dve, [], nc.vector.tensor_tensor, lb, k.col("lb", 0, 4), k.col("lb", 4, 4), ALU.subtract)
    t = on(k.act, [t], nc.scalar.activation, lb, lb, ACT.Sigmoid)
    on(k.dve, [t], nc.vector.tensor_scalar, oml, lb, -1.0, 1.0, ALU.mult, ALU.add)
    k.fence()
    causal = view(k.c["causal"], 0, NQ, SEQ)
    units, toks = [], []
    for h in range(HEADS_E):
        sc = []
        for comp in range(2):
            r = slice(HD * comp, HD * comp + HD)
            parts = [(qt * SEQ, (qt + 1) * P, qT[r, h, qt * P:(qt + 1) * P], kT[r, h, 0:(qt + 1) * P]) for qt in range(NQ)]
            bank_cols = [(comp * 512 + qt * SEQ, causal[:, qt, 0:(qt + 1) * P], BIGNUM, None) for qt in range(NQ)]
            sc.append((bank_cols, parts))
        units.append(dict(prepare=None, scores=sc, diff=True, first=True, last=True, rows=slice(0, P),
                          v=lambda kt, h=h: V[:, kt, h * P:(h + 1) * P], to=k.H[:, h, SEQS], tok=toks))
    attend(k, units)
    o = [k.H[:, h, SEQS] for h in range(HEADS_E)]
    rms_heads(k, o, k.c["mean128"][:, :], lambda i: g, None, SEQ, 0, toks, o)
    k.fence()
    hgrn2(k, hq, hf, hg, HV, lb, oml)
    k.fence()


def value_rows(k, name, layer, chunks, V, off, stationary, tiles=NQ):
    nc = k.nc
    n = len(chunks) * P
    banks = [k.take(["gemm", "out"][i // 2]) for i in range(tiles)]
    t = k.rows_product([k.bank[b][:, 0:n] for b in banks], name, layer, chunks, DC, stationary)
    for i, b in enumerate(banks):
        k.read[b] = on(k.act, [t], nc.scalar.copy, V[:, i, off:off + n], k.bank[b][:, 0:n])
    return k.read[banks[-1]]


def hgrn2(k, q, f, g, V, lb, oml):
    nc = k.nc
    v1, a1 = nc.vector, nc.scalar
    W = HEADS_E * SEQ
    NC_ = SEQ // CH
    S5 = [k.SCR[:, i * W:(i + 1) * W] for i in range(5)]
    B3 = [k.BIG[:, 7168 + i * W:7168 + (i + 1) * W] for i in range(3)]
    S = view(k.BIG, 10240, HEADS_E, 3, P)
    ch = lambda x: x.rearrange("p (c t) -> p c t", t=CH)
    hd = lambda x: x.rearrange("p (h t) -> p h t", t=SEQ)
    lf, kk, b, qi, ki = S5
    qo, ks, turned = B3
    fm = hd(lf)
    qf = q.rearrange("p h t -> p (h t)")
    for h in range(HEADS_E):
        t = on(k.dve, [], v1.tensor_scalar, fm[:, h, :], f[:, h, :], oml[:, h:h + 1], lb[:, h:h + 1], ALU.mult, ALU.add)
    t = on(k.dve, [t], v1.tensor_scalar, kk, lf, -1.0, 1.0, ALU.mult, ALU.add)
    t = on(k.act, [t], a1.activation, lf, lf, ACT.Ln)
    t = on(k.dve, [t], v1.tensor_tensor_scan, b, k.keep[:, :], lf, 0.0, ALU.mult, ALU.add)
    bc = ch(b)
    mid = bc[:, :, CH // 2 - 1:CH // 2].to_broadcast([P, W // CH, CH])
    end = bc[:, :, CH - 1:CH].to_broadcast([P, W // CH, CH])
    td = on(k.dve, [t], v1.tensor_tensor, ch(lf), bc, mid, ALU.subtract)
    t1 = on(k.act, [td], a1.activation, qi, lf, ACT.Exp)
    t2 = on(k.act, [td], a1.activation, ki, lf, ACT.Exp, scale=-1.0)
    t3 = on(k.act, [t], a1.activation, qo, b, ACT.Exp)
    td = on(k.dve, [t2], v1.tensor_tensor, ch(lf), bc, end, ALU.subtract)
    t4 = on(k.act, [td], a1.activation, ks, lf, ACT.Exp, scale=-1.0)
    dc = k.SQ[:, 1, 0:W // CH]
    tdc = on(k.dve, [t3], v1.tensor_copy, dc, ch(qo)[:, :, CH - 1])
    t1 = on(k.dve, [t1], v1.tensor_tensor, qi, qi, qf, ALU.mult)
    t2 = on(k.dve, [t2], v1.tensor_tensor, ki, ki, kk, ALU.mult)
    t3 = on(k.dve, [tdc], v1.tensor_tensor, qo, qo, qf, ALU.mult)
    t4 = on(k.dve, [t4], v1.tensor_tensor, ks, ks, kk, ALU.mult)
    AT = lf.rearrange("p (a t) -> p a t", t=P)
    tz = on(k.dve, [t4], v1.memset, lf, 0.0)
    b0 = k.take("score")
    k.pe.wait(t1, t2)
    for i in range(HEADS_E * NQ):
        h, tile = i // NQ, i % NQ
        for j in range(2):
            o = tile * P + j * CH
            t = k.last_matmul(k.bank[b0][j * CH:(j + 1) * CH, i * CH:(i + 1) * CH], hd(ki)[:, h, o:o + CH],
                              hd(qi)[:, h, o:o + CH], start=True, stop=True)
    for j in range(2):
        r = slice(j * CH, (j + 1) * CH)
        mask = k.c["before"][r, :].bitcast(U32).unsqueeze(1).to_broadcast([CH, HEADS_E * NQ, CH])
        ta = on(k.dve, [t, tz], v1.copy_predicated, AT[r, :, j * CH:(j + 1) * CH], mask,
                k.bank[b0][r, :].rearrange("p (a t) -> p a t", t=CH))
    k.read[b0] = ta
    ksT = turned.rearrange("p (a h f) -> p a h f", h=HEADS_E, f=P)
    k.pe.wait(t4)
    for tile in range(NQ):
        bt = k.take("turned")
        for h in range(HEADS_E):
            t = k.pe.done(nc.tensor.transpose(k.bank[bt][:, h * P:(h + 1) * P], hd(ks)[:, h, tile * P:(tile + 1) * P],
                                              k.c["ident"][:, :]))
        k.read[bt] = tk = on(k.act, [t], a1.copy, ksT[:, tile, :, :], k.bank[bt][:, :].rearrange("p (h f) -> p h f", f=P))
    k.pe.wait(tk)
    for c in range(NC_ - 1):
        j, tile = c % 2, c // 2
        bs = k.take("score")
        r = slice(j * CH, (j + 1) * CH)
        for h in range(HEADS_E):
            t = k.last_matmul(k.bank[bs][:, h * P:(h + 1) * P], ksT[r, tile, h, :], V[r, tile, h * P:(h + 1) * P],
                              start=True, stop=True)
        for h in range(HEADS_E):
            add = k.bank[bs][:, h * P:(h + 1) * P]
            if c == 0:
                ts = on(k.dve, [t], v1.tensor_copy, S[:, h, c, :], add)
            else:
                ts = on(k.dve, [t, k.dve.now()], v1.scalar_tensor_tensor, S[:, h, c, :], S[:, h, c - 1, :],
                        dc[:, h * NC_ + c:h * NC_ + c + 1], add, ALU.mult, ALU.add)
        k.read[bs] = ts
    k.pe.wait(ta, t3, ts)
    oT = kk.rearrange("p (h t) -> p h t", t=SEQ)
    toks = []
    for h in range(HEADS_E):
        bo = k.take("out")
        vh = slice(h * P, (h + 1) * P)
        for tile in range(NQ):
            k.matmul(k.bank[bo][:, tile * P:(tile + 1) * P], V[:, tile, vh], AT[:, h * NQ + tile, :],
                     start=(tile == 0), stop=False, skip_group_check=True)
        for c in range(1, NC_):
            t = k.last_matmul(k.bank[bo][:, c * CH:(c + 1) * CH], S[:, h, c - 1, :],
                              hd(qo)[:, h, c * CH:(c + 1) * CH], start=False, stop=(c == NC_ - 1), skip_group_check=True)
        k.read[bo] = t = on(k.act, [t], a1.copy, oT[:, h, :], k.bank[bo][:, 0:SEQ])
        toks.append(t)
    rms_heads(k, [oT[:, h, :] for h in range(HEADS_E)], k.c["mean128"][:, :], lambda i: k.col("hg_g"),
              lambda i: g[:, i, :], SEQ, 0, toks, [k.H[:, 4 + h, SEQS] for h in range(HEADS_E)])


def odd_mixer(k):
    nc = k.nc
    qT, kT = view(k.BIG, 0, DC, SEQ), view(k.BIG, 2048, DC, SEQ)
    V = view(k.BIG, 4096, NQ, D)
    for dst, scale, first in ((qT, QSCALE, 0), (kT, 1.0, DC)):
        t = project(k, "od_w_in", 0, DC, lambda i: dst[:, i, :], scale=scale, first=first)
        for i in range(DC):
            rope(k, dst[:, i, :], k.c["rot1"][:, :], k.c["cos1"][:, :], k.c["sin1"][:, :], t[i])
    for half in range(2):
        value_rows(k, "od_w_in", 0, [2 * DC + 4 * half + i for i in range(4)], V, 512 * half,
                   lambda c, i: k.X[:, c, CTX + i * P:CTX + (i + 1) * P])
    k.fence()
    mask = view(k.c["dilated"], 0, NQ, SEQ)
    units, toks = [], []
    for h in range(HEADS_O):
        r, c = head_rows(h), h // 2
        parts = [(qt * SEQ, (qt + 1) * P, qT[r, c, qt * P:(qt + 1) * P], kT[r, c, 0:(qt + 1) * P]) for qt in range(NQ)]
        bank_cols = [(qt * SEQ, mask[:, qt, 0:(qt + 1) * P], BIGNUM, None) for qt in range(NQ)]
        units.append(dict(prepare=None, scores=[(bank_cols, parts)], diff=False, first=h % 2 == 0, last=h % 2 == 1,
                          rows=r, v=lambda kt, h=h: V[:, kt, h * HD:(h + 1) * HD], to=k.H[:, c, SEQS], tok=toks))
    attend(k, units)
    k.fence()



def modulations(k):
    nc = k.nc
    cc = k.col("cc", 0, 16)
    t = on(k.act, [], nc.scalar.activation, cc, cc, ACT.Silu)
    k.pe.wait(t)
    ccv = cc.rearrange("p (c s) -> p c s", s=2)
    for layer in range(DEPTH):
        b = k.take("gemm")
        for i in range(48):
            t = k.product(k.bank[b][:, 2 * i:2 * i + 2], "w_mod_2", layer, i, DC, lambda c: ccv[:, c, :])
        bias = k.col("b_mod", 48 * layer, 48).unsqueeze(2).to_broadcast([P, 48, 2])
        k.read[b] = on(k.dve, [t], nc.vector.tensor_tensor, k.mod[:, layer, :, :],
                       k.bank[b][:, 0:96].rearrange("p (c s) -> p c s", s=2), bias, ALU.add)


def modulated_norm(k, layer, norm, section, lo):
    nc = k.nc
    n = T2 - lo
    b, t = mean_squares(k, [k.X[:, i, lo:T2] for i in range(DC)], k.c["meanD"][:, :], n, [None] * DC)
    t = rsqrt_of(k, b, n, t, 1)
    sh, sc = k.mod[:, layer, section:section + DC, :], k.mod[:, layer, section + DC:section + 2 * DC, :]
    gs = k.gs[:, :].rearrange("p (c s) -> p c s", s=2)
    g = k.col(norm, layer * DC, DC).unsqueeze(2).to_broadcast([P, DC, 2])
    tg = on(k.dve, [], nc.vector.tensor_scalar, gs, sc, 1.0, None, ALU.add)
    tg = on(k.dve, [tg], nc.vector.tensor_tensor, gs, gs, g, ALU.mult)
    out = []
    for i in range(DC):
        for side in range(2):
            if side * CTX < lo:
                continue
            s = slice(side * CTX, (side + 1) * CTX)
            ts = on(k.dve, [t, tg], nc.vector.scalar_tensor_tensor, k.H[:, i, s], k.X[:, i, s], gs[:, i, side:side + 1],
                    k.RS[:, side * CTX - lo:side * CTX - lo + CTX], ALU.mult, ALU.mult)
            out.append(on(k.act, [ts], nc.scalar.activation, k.H[:, i, s], k.H[:, i, s], ACT.Identity,
                          bias=sh[:, i, side:side + 1]))
    k.rs_read = ts
    return out


def gated_residual(k, name, layer, moving, kc, gate, lo):
    nc = k.nc
    for i in range(DC):
        b = k.take("gemm")
        t = k.product(k.bank[b][:, 0:T2 - lo], name, layer, i, kc, moving)
        for side in range(2):
            if side * CTX < lo:
                continue
            s = slice(side * CTX, (side + 1) * CTX)
            t2 = on(k.dve, [t], nc.vector.scalar_tensor_tensor, k.X[:, i, s],
                    k.bank[b][:, side * CTX - lo:(side + 1) * CTX - lo], k.mod[:, layer, gate + i, side:side + 1],
                    k.X[:, i, s], ALU.mult, ALU.add)
        k.read[b] = t2


def second_block(k):
    nc = k.nc
    modulations(k)
    k.fence()
    for layer in range(DEPTH):
        lo = 0 if layer == 0 else CTX
        token_mixers(k, layer, lo)
        k.fence()
        gated_residual(k, "w_out_2", layer, lambda c: k.H[:, c, lo:T2], DC, 16, lo)
        k.fence()
        toks = modulated_norm(k, layer, "norm_ffn", 24, lo)
        k.pe.wait(*toks)
        hid = view(k.BIG, 0, DFF // P, T2 - lo)
        n = T2 - lo
        th = []
        for i in range(DFF // P):
            bg, bu = k.take("gemm"), k.take("gemm")
            tg = k.product(k.bank[bg][:, 0:n], "w_gate_2", layer, i, DC, lambda c: k.H[:, c, lo:T2])
            tmp = k.TMP[:, i % 2, 0:n]
            tg = on(k.act, [tg, th[i - 2] if i >= 2 else None], nc.scalar.activation, tmp, k.bank[bg][:, 0:n], ACT.Silu)
            k.read[bg] = tg
            tu = k.product(k.bank[bu][:, 0:n], "w_up_2", layer, i, DC, lambda c: k.H[:, c, lo:T2])
            k.read[bu] = t = on(k.dve, [tg, tu], nc.vector.tensor_tensor, hid[:, i, :], tmp, k.bank[bu][:, 0:n], ALU.mult)
            th.append(t)
        k.pe.wait(*th)
        gated_residual(k, "w_down_2", layer, lambda c: hid[:, c, :], DFF // P, 40, lo)
        k.fence()
    b, t = mean_squares(k, [k.X[:, i, SEQS] for i in range(DC)], k.c["meanD"][:, :], SEQ, [None] * DC)
    t = rsqrt_of(k, b, SEQ, t, 1)
    for i in range(DC):
        t2 = on(k.dve, [t], nc.vector.scalar_tensor_tensor, k.H[:, i, SEQS], k.X[:, i, SEQS], k.col("final", i),
                k.RS[:, 0:SEQ], ALU.mult, ALU.mult)
        k.act.wait(t2)
        nc.scalar.dma_start(k.io["out"][:, i, :], k.H[:, i, SEQS]).then_inc(k.s_out, 16)
    nc.scalar.wait_ge(k.s_out, 16 * DC)


def token_mixers(k, layer, lo):
    nc = k.nc
    toks = modulated_norm(k, layer, "norm_mix", 0, 0)
    k.pe.wait(*toks)
    gq, gk, gg = view(k.BIG, 0, 2, T2), view(k.BIG, 1024, 2, T2), view(k.BIG, 2048, 2, T2)
    z = k.BIG[:, 3072:3584]
    nq, nk = view(k.BIG, 3584, 3, T2), view(k.BIG, 5120, 3, T2)
    sq, sk = view(k.BIG, 6656, 3, T2), view(k.BIG, 8192, 1, T2)
    V = view(k.BIG, 8704, 4, 768)
    if layer == 0:
        nc.gpsimd.dma_start(k.wa2[:, :], k.io["wa2"][0]).then_inc(k.s_wa2, 16)
    else:
        nc.gpsimd.dma_start(k.wa2[:, :], k.io["wa2"][1]).then_inc(k.s_wa2, 16)
    plan = [(0, 2, gq, lo, QSCALE, ACT.Copy), (2, 2, gk, 0, 1.0, ACT.Copy), (6, 2, gg, lo, 1.0, ACT.Silu),
            (8, 1, None, 0, 1.0, ACT.Copy), (9, 3, nq, lo, QSCALE, ACT.Copy), (12, 3, nk, 0, 1.0, ACT.Copy),
            (18, 3, sq, lo, QSCALE, ACT.Copy), (21, 1, sk, 0, 1.0, ACT.Copy)]
    for first, count, dst, a, scale, func in plan:
        for i in range(count):
            b = k.take("gemm")
            d = z[:, a:T2] if dst is None else dst[:, i, a:T2]
            t = k.product(k.bank[b][:, 0:T2 - a], "w_in_2", layer, first + i, DC, lambda c: k.H[:, c, a:T2])
            k.read[b] = t = on(k.act, [t], nc.scalar.activation, d, k.bank[b][:, 0:T2 - a], func, scale=scale)
            if first >= 18:
                rope(k, dst[:, i, SEQS], k.c["rot2"][:, :], k.c["cos2"][:, :], k.c["sin2"][:, :], t)
    rows = lambda c, i: k.H[:, c, i * P:(i + 1) * P]
    value_rows(k, "w_in_2", layer, [15, 16, 17, 22], V, 256, rows, tiles=4)
    value_rows(k, "w_in_2", layer, [4, 5], V, 0, rows, tiles=4)
    k.fence()
    k.wa2_loads = 16 * (layer + 1)
    gla(k, layer, lo, gq, gk, gg, z, V)
    k.fence()
    window, near = view(k.c["window"], 0, NQ, T2), view(k.c["near"], 0, NQ, SEQ)
    zeros = window[:, 0, 0:CTX]
    swap_keys(k, sk)
    units, toks = [], []
    for kind in range(2):
        for side in ((0, 1) if layer == 0 else (1,)):
            for h in range(6):
                c, r = h // 2, head_rows(h)
                keys = CTX if side == 0 else T2
                if kind == 0:
                    q, kk, kr, vo = nq, nk[:, c, :], r, 256 + h * HD
                    bias = [k.NB[:, h % 2, qt * 512:(qt + 1) * 512] for qt in range(NQ)] if side else [zeros] * 2
                    start, sink = BIGNUM, None
                    prepare = (lambda h=h: near_bias(k, layer, h, near)) if side else None
                else:
                    kv = h // SWA_G
                    q, kr, vo = sq, r, 640 + kv * HD
                    kk = k.SK[(kv, h % 2)]
                    bias = [window[:, qt, :] for qt in range(NQ)] if side else [zeros] * 2
                    i = layer * 6 + h
                    start, sink = k.negsink[:, i:i + 1], k.col("sink", i)
                    prepare = None
                if not side:
                    bias = [zeros, zeros]
                sc = []
                for qt in range(NQ):
                    qs = q[r, c, side * CTX + qt * P:side * CTX + (qt + 1) * P]
                    sc.append(([(qt * 512, bias[qt], start, sink)], [(0, keys, qs, kk[kr, 0:keys])]))
                units.append(dict(prepare=prepare, scores=sc, diff=False, first=h % 2 == 0, last=h % 2 == 1, rows=r,
                                  nb=h % 2 if prepare else None, v=lambda kt, vo=vo: V[:, kt, vo:vo + HD],
                                  to=k.H[:, 2 + 3 * kind + c, side * CTX:(side + 1) * CTX], tok=toks))
    attend(k, units)


def swap_keys(k, sk):
    nc = k.nc
    base = sk[:, 0, :]
    other = k.SCR[:, 0:T2]
    t = on(k.dve, [], nc.vector.tensor_copy, other[0:HD, :], base[HD:P, :])
    t = on(k.dve, [], nc.vector.tensor_copy, other[HD:P, :], base[0:HD, :])
    k.pe.wait(t)
    k.SK = {(0, 0): base, (1, 1): base, (0, 1): other, (1, 0): other}


def near_bias(k, layer, h, near):
    nc = k.nc
    s = k.s_bias[h % 2]
    nb = k.NB[:, h % 2, :].rearrange("p (a b) -> p a b", b=512)
    k.pool.wait(k.nb_read[h % 2])
    for row in range(SEQ // GRID_W):
        qt, r = row // 2, slice((row % 2) * GRID_W, (row % 2 + 1) * GRID_W)
        dst = nb[r, qt, CTX:T2].rearrange("p (a b) -> p a b", b=GRID_W)
        nc.gpsimd.dma_start(dst, k.io["rpb"][layer, h, 7 - row:7 - row + SEQ // GRID_W].rearrange("a c n -> c a n")).then_inc(s, 16)
    k.bias_count[h % 2] += 64
    nc.gpsimd.wait_ge(s, k.bias_count[h % 2])
    t = on(k.pool, [], nc.gpsimd.tensor_tensor, nb[:, :, CTX:T2], nb[:, :, CTX:T2], near, ALU.add)
    k.dve.wait(t)


def gla(k, layer, lo, q, kT, g, z, V):
    nc = k.nc
    v1, a1 = nc.vector, nc.scalar
    NCH = T2 // CH
    sub = lambda i: k.SCR[:, i * T2:(i + 1) * T2]
    ch = lambda x: x.rearrange("p (c t) -> p c t", t=CH)
    nc.tensor.wait_ge(k.s_wa2, k.wa2_loads)
    c0 = lo // CH
    for d in range(2):
        for pair in range(2):
            la, b, qi, ki, ke, e = (sub(i) for i in range(6))
            keT = view(k.SCR, 3072, 4, P)
            AT = view(k.SCR, 3584, 2, 4, P)
            S = view(k.SCR, 4608, NCH - 1, P)
            dc = k.small[:, 32:40]
            rows = slice(32 * d, 32 * d + RANK)
            bz = k.take("out")
            t = k.last_matmul(k.bank[bz][:, :], k.wa2[rows, pair * P:(pair + 1) * P], z[rows, :], start=True, stop=True)
            bias = k.col("ba", (layer * 2 + d) * 2 + pair)
            k.read[bz] = t = on(k.act, [t], a1.activation, la, k.bank[bz][:, :], ACT.Identity, bias=bias)
            t1 = on(k.dve, [t], v1.scalar_tensor_tensor, b, la, -1.0, la, ALU.mult, ALU.min)
            t1 = on(k.act, [t1], a1.activation, b, b, ACT.Exp)
            t1 = on(k.act, [t1], a1.activation, b, b, ACT.Ln, bias=k.c["cols"][:, 2:3])
            t2 = on(k.dve, [t], v1.tensor_scalar, la, la, 0.0, None, ALU.min)
            t2 = on(k.dve, [t1, t2], v1.tensor_tensor, la, la, b, ALU.subtract)
            t = on(k.dve, [t2], v1.tensor_scalar, la, la, 1.0 / 16.0, None, ALU.mult)
            t = on(k.dve, [t], v1.tensor_tensor_scan, b, k.keep[:, 0:T2], la, 0.0, ALU.mult, ALU.add)
            bc = ch(b)
            if d == 1:
                t = on(k.dve, [t], v1.tensor_tensor, la, la, b, ALU.subtract)
                t = on(k.dve, [t], v1.tensor_tensor, bc, ch(la), bc[:, :, CH - 1:CH].to_broadcast([P, NCH, CH]), ALU.add)                     if False else on(k.dve, [t], v1.tensor_tensor, ch(qi), ch(la),
                                     bc[:, :, CH - 1:CH].to_broadcast([P, NCH, CH]), ALU.add)
                t = on(k.dve, [t], v1.tensor_copy, b, qi)
            edge = slice(CH - 1, CH) if d == 0 else slice(0, 1)
            end = bc[:, :, edge].to_broadcast([P, NCH, CH])
            td = on(k.dve, [t], v1.tensor_tensor, ch(la), bc, end, ALU.subtract)
            t1 = on(k.act, [t, td], a1.activation, qi, b, ACT.Exp)
            t2 = on(k.act, [t], a1.activation, ki, b, ACT.Exp, scale=-1.0)
            t3 = on(k.act, [td], a1.activation, ke, la, ACT.Exp, scale=-1.0)
            tdc = on(k.dve, [t1], v1.tensor_copy, dc, ch(qi)[:, :, edge])
            t1 = on(k.dve, [t1, tdc], v1.tensor_tensor, qi[:, lo:T2], qi[:, lo:T2], q[:, pair, lo:T2], ALU.mult)
            t2 = on(k.dve, [t2], v1.tensor_tensor, ki, ki, kT[:, pair, :], ALU.mult)
            t3 = on(k.dve, [t3], v1.tensor_tensor, ke, ke, kT[:, pair, :], ALU.mult)
            bt = k.take("turned")
            k.pe.wait(t3)
            for tile in range(4):
                t = k.pe.done(nc.tensor.transpose(k.bank[bt][:, tile * P:(tile + 1) * P], ke[:, tile * P:(tile + 1) * P],
                                                  k.c["ident"][:, :]))
            k.read[bt] = tk = on(k.act, [t], a1.copy, keT, k.bank[bt][:, :].rearrange("p (a f) -> p a f", f=P))
            tz = on(k.dve, [], v1.memset, AT, 0.0)
            k.pe.wait(t1, t2)
            for hh in range(2):
                r = slice(hh * HD, (hh + 1) * HD)
                b0 = k.take("score")
                for tile in range(lo // P, 4):
                    for j in range(2):
                        o = tile * P + j * CH
                        t = k.last_matmul(k.bank[b0][j * CH:(j + 1) * CH, tile * CH:(tile + 1) * CH], ki[r, o:o + CH],
                                          qi[r, o:o + CH], start=True, stop=True)
                for j in range(2):
                    s = slice(j * CH, (j + 1) * CH)
                    n = 4 - lo // P
                    mask = k.c["before" if d == 0 else "after"][s, :].bitcast(U32).unsqueeze(1).to_broadcast([CH, n, CH])
                    ta = on(k.dve, [t, tz], v1.copy_predicated, AT[s, hh, lo // P:4, j * CH:(j + 1) * CH], mask,
                            k.bank[b0][s, lo // 2:256].rearrange("p (a t) -> p a t", t=CH))
                k.read[b0] = ta
            k.pe.wait(tk)
            order = list(range(NCH)) if d == 0 else [3, 2, 1, 0, 7, 6, 5, 4]
            banks = [k.take("out"), k.take("out")]
            for c in order[:-1]:
                j, tile = c % 2, c // 2
                s = slice(j * CH, (j + 1) * CH)
                t = k.last_matmul(k.bank[banks[j]][:, tile * P:(tile + 1) * P], keT[s, tile, :],
                                  V[s, tile, pair * P:(pair + 1) * P], start=True, stop=True)
            enter = {}
            for n, c in enumerate(order[:-1]):
                j, tile = c % 2, c // 2
                add = k.bank[banks[j]][:, tile * P:(tile + 1) * P]
                if n == 0:
                    ts = on(k.dve, [t], v1.tensor_copy, S[:, n, :], add)
                else:
                    ts = on(k.dve, [t, ts], v1.scalar_tensor_tensor, S[:, n, :], S[:, n - 1, :], dc[:, c:c + 1], add,
                            ALU.mult, ALU.add)
                enter[order[n + 1]] = n
            k.read[banks[0]] = k.read[banks[1]] = ts
            k.pe.wait(ta, ts)
            bo = k.take("gemm")
            for hh in range(2):
                r = slice(hh * HD, (hh + 1) * HD)
                for tile in range(lo // P, 4):
                    k.matmul(k.bank[bo][r, tile * P:(tile + 1) * P], V[:, tile, pair * P + hh * HD:pair * P + (hh + 1) * HD],
                             AT[:, hh, tile, :], start=(tile == lo // P), stop=False, skip_group_check=True)
            for hh in range(2):
                r = slice(hh * HD, (hh + 1) * HD)
                for c in range(c0, NCH):
                    if c in enter:
                        t = k.last_matmul(k.bank[bo][r, c * CH:(c + 1) * CH], S[r, enter[c], hh * HD:(hh + 1) * HD],
                                          qi[r, c * CH:(c + 1) * CH], start=False, stop=True, skip_group_check=True)
            dst = k.H[:, pair, lo:T2]
            if d == 0:
                t = on(k.act, [t], a1.copy, dst, k.bank[bo][:, lo:T2])
            else:
                t = on(k.dve, [t], v1.tensor_tensor, dst, dst, k.bank[bo][:, lo:T2], ALU.add)
            k.read[bo] = t
            k.fence()
    o = [k.H[:, p, lo:T2] for p in range(2)]
    rms_heads(k, o, k.c["mean64"][:, :], lambda i: k.col("gla_norm", layer * 2 + i), lambda i: g[:, i, lo:T2],
              T2 - lo, 1, [None, None], o)


def load_stream(k, tiles):
    nc = k.nc
    stream = k.io["stream"]
    assert tiles % RING == 0
    for s in range(RING):
        nc.sync.dma_start(k.ring[:, s, :], stream[s]).then_inc(k.s_tile[s], 16)
    with nc.sync.Fori(1, tiles // RING) as i:
        for s in range(RING):
            nc.sync.wait_ge(k.s_free, i * RING + (s - RING + 1))
            nc.sync.dma_start(k.ring[:, s, :], stream[bass.ds(i * RING + s, 1)].rearrange("a p n -> (a p) n")) \
                .then_inc(k.s_tile[s], 16)



def kernel(**inputs):
    import numpy as _np
    import concourse.bacc as _bacc
    from concourse import mybir as _mybir
    from concourse.bass_utils import run_bass_kernel_spmd as _run

    nc = _bacc.Bacc("TRN2", target_bir_lowering=False, num_devices=1)
    arrays, io = {}, {}

    def give(name, a):
        a = _np.ascontiguousarray(a)
        arrays["in_" + name] = a
        io[name] = nc.dram_tensor("in_" + name, a.shape, _mybir.dt.from_np(a.dtype), kind="ExternalInput").ap()

    x = {n: _np.asarray(a) for n, a in inputs.items()}
    chunked = lambda a: a.reshape(*a.shape[:-1], a.shape[-1] // P, P)
    feat = lambda a: chunked(a.reshape(-1)).T
    toks = lambda a: _np.transpose(chunked(a), (2, 1, 0))
    for n, a in CONST.items():
        give(n, a)
    rows = lambda a: _np.broadcast_to(a.reshape(1, -1), (P, a.size))
    par = {"ln1_g": feat(x["ln1_g"]), "ln1_b": feat(x["ln1_b"]), "ln2_g": feat(x["ln2_g"]), "ln2_b": feat(x["ln2_b"]),
           "ple_g": feat(x["ple_norm_g"]), "sub_g": feat(x["da_subln_g"]), "hg_g": feat(x["hg_norm_g"]),
           "lb": feat(x["hg_lb_logits"]), "norm_mix": feat(x["norm_mix_2"]), "norm_ffn": feat(x["norm_ffn_2"]),
           "final": feat(x["final_norm_2"]), "b_mod": feat(x["b_mod_2"]),
           "ba": feat(_np.stack([x["gla_ba_f_2"], x["gla_ba_b_2"]], 1)), "gla_norm": feat(x["gla_norm_2"]),
           "sink": rows(x["swa_sink_2"]), "lam": rows(x["da_lambda"]),
           "cc": _np.stack([feat(x["c_ctx_2"]), feat(x["c_2"])], 2).reshape(P, 16)}
    give("params", _np.concatenate([par[n] for n in PARAMS], 1))
    give("x", toks(x["x"][0]))
    give("ctx", toks(x["ctx_2"][0]))
    give("p", _np.stack([toks(x["p"][l, 0]) for l in range(DEPTH)]))
    wa2 = _np.zeros((DEPTH, P, GLA_W), _np.float32)
    wa2[:, 0:RANK] = x["gla_wa2_f_2"]
    wa2[:, 32:32 + RANK] = x["gla_wa2_b_2"]
    give("wa2", wa2)
    rpb = _np.zeros((DEPTH, NA_H, RPB_R, RPB_C), _np.float32)
    rpb[..., GRID_W - 16:GRID_W + 15] = x["na_rpb_2"]
    give("rpb", _np.lib.stride_tricks.sliding_window_view(rpb, GRID_W, axis=-1)[..., ::-1, :])
    W = {n: x[n] for n in ("ev_w_in", "ev_w_out", "od_w_in", "od_w_out", "ffn_w1", "ffn_w2", "ple_w_proj", "ple_w_gate",
                           "w_mod_2", "w_out_2", "w_gate_2", "w_up_2", "w_down_2")}
    w = x["w_in_2"]
    low = _np.zeros((DEPTH, D, P), _np.float32)
    low[..., 0:RANK] = w[..., 1024:1024 + RANK]
    low[..., 32:32 + RANK] = w[..., 1024 + RANK:1024 + 2 * RANK]
    W["w_in_2"] = _np.concatenate([w[..., :1024], low, w[..., 1024 + 2 * RANK:]], -1)
    n_blocks = sum(a.size for a in W.values()) // (P * P)
    tiles = -(-n_blocks // (TB * RING)) * RING
    give("stream", _np.zeros((tiles, P, TB * P), _np.float32))
    io["out"] = nc.dram_tensor("out_0", (P, DC, SEQ), _mybir.dt.float32, kind="ExternalOutput").ap()
    k = build(nc, io, tiles)
    assert len(k.blocks) == n_blocks, (len(k.blocks), n_blocks)
    stream = arrays["in_stream"]
    for i, (name, layer, kc, col) in enumerate(k.blocks):
        stream[i // TB, :, i % TB * P:(i % TB + 1) * P] = W[name][layer, kc * P:(kc + 1) * P, col * P:(col + 1) * P]
    r = _run(nc, [arrays], core_ids=[0])
    out = r.results[0]["out_0"]
    return _np.ascontiguousarray(_np.transpose(out, (2, 1, 0))).reshape(1, SEQ, D)


def build(nc, io, tiles):
    ctx = ExitStack()
    with ctx:
        k = Program(nc, ctx, io)
        load_stream(k, tiles)
        emit(k)
        for s in k.s_tile:
            nc.tensor.wait_ge(s, 16 * tiles // RING)
    return k
```

```python
import math
from contextlib import ExitStack

import numpy as np

import concourse.bass as bass
from concourse import mybir
from concourse.alu_op_type import AluOpType as ALU

F32 = mybir.dt.float32
F32R = mybir.dt.float32r
U32 = mybir.dt.uint32
ACT = mybir.ActivationFunctionType
AX = mybir.AxisListType

P = 128
D = 1024
DC = D // P
SEQ = 256
CTX = 256
T2 = CTX + SEQ
NQ = SEQ // P
DEPTH = 2
PLE = 256
FFN = 4 * D
DFF = 2816
CH = 64
HEADS_E = 4
HEADS_O = 16
GLA_W, NA_W, SWA_W, SWA_KV = 256, 384, 384, 128
NA_H, SWA_H, SWA_G = 6, 6, 3
GRID_W = 64
RANK = 16
ALPHA = (2 * DEPTH) ** 0.25
LAM_INIT = 0.8 - 0.6 * math.exp(0.0)
EPS1, EPS2 = 1e-5, 1e-6
HD = 64
QSCALE = HD ** -0.5
NEG = -1e30
RPB_R, RPB_C = 15, 2 * GRID_W - 1

TB = 8
RING = 6
SPLIT = 4
AHEAD = 2


def consts():
    p = np.arange(P)
    out = {}
    out["ident"] = np.eye(P)
    out["meanD"] = np.full((P, P), 1.0 / D)
    out["mean128"] = np.full((P, P), 1.0 / P)
    out["mean64"] = (p[:, None] // HD == p[None, :] // HD) / HD
    def rotation(half):
        r = np.zeros((P, P))
        for m in range(P):
            base, d = m // HD * HD, m % HD
            if d < half:
                r[base + d + half, m] = -1.0
            elif d < 2 * half:
                r[base + d - half, m] = 1.0
        return r
    out["rot1"], out["rot2"] = rotation(8), rotation(32)
    t = np.arange(SEQ)
    d = p % HD
    inv1 = (np.float32(500000.0) ** (-np.arange(0, 16, 2, dtype=np.float32) / np.float32(16))).astype(np.float32)
    ang1 = (t.astype(np.float32)[:, None] * inv1[None, :]).astype(np.float32)
    rot = (d < 16)[:, None]
    out["cos1"] = np.where(rot, np.cos(ang1)[:, d % 8].T, 1.0)
    out["sin1"] = np.where(rot, np.sin(ang1)[:, d % 8].T, 0.0)
    inv2 = (np.float32(10000.0) ** (-np.arange(16, dtype=np.float32) / np.float32(16))).astype(np.float32)
    row, col = (t // GRID_W).astype(np.float32), (t % GRID_W).astype(np.float32)
    ang2 = np.concatenate([row[:, None] * inv2, col[:, None] * inv2], -1).astype(np.float32)
    out["cos2"], out["sin2"] = np.cos(ang2)[:, d % 32].T, np.sin(ang2)[:, d % 32].T
    q = (np.arange(NQ)[None, :, None] * P + p[:, None, None])
    k = np.arange(SEQ)[None, None, :]
    out["causal"] = np.where(k <= q, 0.0, NEG)
    n = ((k <= q) & (q - k <= 128)) * 1.0 + ((k <= q) & ((q - k) % 4 == 0)) + ((k <= q) & ((q - k) % 16 == 0))
    out["dilated"] = np.where(n > 0, np.log(np.maximum(n, 1)), NEG)
    swa = np.where(np.abs(q - k) <= 128, 0.0, NEG)
    out["window"] = np.concatenate([np.zeros((P, NQ, CTX)), swa], -1)
    start = np.clip(q % GRID_W - 8, 0, GRID_W - 16)
    out["near"] = np.where((k % GRID_W >= start) & (k % GRID_W < start + 16), 0.0, NEG)
    s, tt = p[:, None] % CH, np.arange(CH)[None, :]
    out["before"] = (s <= tt) * 1.0
    out["after"] = (s >= tt) * 1.0
    out["cols"] = np.tile(np.array([EPS1, EPS2, 1.0, 0.0]), (P, 1))
    return {a: np.ascontiguousarray(b.reshape(P, -1).astype(np.float32)) for a, b in out.items()}


CONST = consts()

PARAMS = {}
for _n, _w in [("ln1_g", 16), ("ln1_b", 16), ("ln2_g", 16), ("ln2_b", 16), ("ple_g", 16), ("sub_g", 1), ("hg_g", 1),
               ("lb", 8), ("norm_mix", 16), ("norm_ffn", 16), ("final", 8), ("b_mod", 96), ("ba", 8), ("gla_norm", 4),
               ("sink", 12), ("lam", 256), ("cc", 16)]:
    PARAMS[_n] = (sum(w for _, w in PARAMS.values()), _w)
NPAR = sum(w for _, w in PARAMS.values())


class Queue:

    def __init__(self, nc, eng, sem):
        self.nc, self.eng, self.sem, self.n, self.seen = nc, eng, sem, 0, {}

    def wait(self, *tokens):
        for t in tokens:
            if t is None:
                continue
            sem, val, key = t
            if self.seen.get(key, 0) < val:
                self.eng.wait_ge(sem, val)
                self.seen[key] = val

    def done(self, ins):
        ins.then_inc(self.sem, 1)
        self.n += 1
        return (self.sem, self.n, id(self))

    def now(self):
        return (self.sem, self.n, id(self)) if self.n else None


class Program:
    def __init__(self, nc, ctx, io):
        self.nc, self.io, self.ctx = nc, io, ctx
        sb = self.sb
        sem = lambda name: ctx.enter_context(nc.semaphore(name))
        self.pe = Queue(nc, nc.tensor, sem("tensor_done"))
        self.act = Queue(nc, nc.scalar, sem("scalar_done"))
        self.dve = Queue(nc, nc.vector, sem("vector_done"))
        self.pool = Queue(nc, nc.gpsimd, sem("gpsimd_done"))
        self.s_tile = [sem(f"tile_loaded{i}") for i in range(RING)]
        self.s_high = sem("tile_high_split")
        self.s_low = sem("tile_low_split")
        self.s_free = sem("tile_used")
        self.s_start = [sem(f"loaded{i}") for i in range(4)]
        self.s_bias = [sem(f"bias_loaded{i}") for i in range(2)]
        self.s_wa2 = sem("wa2_loaded")
        self.s_out = sem("stored")
        self.ring = sb(ctx, "ring", RING, TB * P)
        self.high = sb(ctx, "high", SPLIT, TB * P, dt=F32R)
        self.low = sb(ctx, "low", SPLIT, TB * P, dt=F32R)
        self.X = sb(ctx, "X", DC, T2)
        self.XH = sb(ctx, "XH", DC, T2, dt=F32R)
        self.XL = sb(ctx, "XL", DC, T2, dt=F32R)
        self.SQ = sb(ctx, "SQ", 2, 512)
        self.RS = sb(ctx, "RS", 512)
        self.TMP = sb(ctx, "TMP", 2, 512)
        self.par = sb(ctx, "par", NPAR)
        self.wa2 = sb(ctx, "wa2", 256)
        self.mod = sb(ctx, "mod", 2, 48, 2)
        self.gs = sb(ctx, "gs", 16)
        self.small = sb(ctx, "small", 112)
        self.keep = sb(ctx, "keep", 512)
        self.c = {}
        self.load_consts(ctx, ["ident", "meanD", "mean128", "mean64", "before", "after", "cols"], 0)
        self.bank = [ctx.enter_context(nc.psum_tensor(f"bank{i}", [P, 512], F32)) for i in range(8)]
        self.read = [None] * 8
        self.turn = {"gemm": 0, "score": 0, "turned": 0, "out": 0}
        self.first = {"gemm": 0, "score": 2, "turned": 4, "out": 6}
        self.blocks = []
        self.tile_seen, self.split, self.freed = -1, 0, 0
        self.sq_read, self.rs_read, self.pt_read, self.T_read = [None] * 2, None, [None] * 2, [None] * 3
        self.tmp_read, self.xh_read, self.hid_read = [None] * 2, None, None
        self.nb_read, self.bias_count = [None, None], [0, 0]
        self.turn_tmp = self.turn_small = self.turn_T = self.turn_PT = self.turn_sq = 0
        self.filler = None

    def sb(self, ctx, name, *shape, dt=F32):
        return ctx.enter_context(self.nc.sbuf_tensor(name, [P, *shape], dt))

    def load_consts(self, ctx, names, s):
        for name in names:
            self.c[name] = self.sb(ctx, f"c{s}_{name}", CONST[name].shape[1])
            self.nc.scalar.dma_start(self.c[name][:, :], self.io[name]).then_inc(self.s_start[s], 16)
        self.n_loads = 16 * len(names)

    def fill(self, us):
        while self.filler is not None and us > 0:
            try:
                us -= next(self.filler)
            except StopIteration:
                self.filler = None

    def drain_filler(self):
        self.fill(1e9)

    def col(self, name, i=0, n=1):
        o, w = PARAMS[name]
        return self.par[:, o + i:o + i + n]

    def take(self, pool):
        b = self.first[pool] + self.turn[pool] % 2
        self.turn[pool] += 1
        self.pe.wait(self.read[b])
        self.read[b] = None
        return b

    def fence(self):
        queues = [self.pe, self.act, self.dve, self.pool]
        marks = [q.now() for q in queues]
        for q in queues:
            q.wait(*marks)

    def split_tile(self, t):
        nc, r, o = self.nc, t % RING, t % SPLIT
        raw, high, low = self.ring[:, r, :], self.high[:, o, :], self.low[:, o, :]
        nc.scalar.wait_ge(self.s_tile[r], 16 * (t // RING + 1))
        if t >= SPLIT:
            nc.scalar.wait_ge(self.s_free, t - SPLIT + 1)
        nc.scalar.copy(high, raw).then_inc(self.s_high, 1)
        nc.vector.wait_ge(self.s_high, t + 1)
        nc.vector.tensor_tensor(low, raw, high.bitcast(F32), ALU.subtract).then_inc(self.s_low, 1)

    def weights(self, requests):
        at = len(self.blocks)
        self.blocks += requests
        tile, o = at // TB, at % TB
        assert o + len(requests) <= TB
        if tile > self.tile_seen:
            while self.split <= min(tile + AHEAD, self.tiles - 1):
                assert self.split < SPLIT or self.freed >= self.split - SPLIT + 1, (self.split, self.freed)
                self.split_tile(self.split)
                self.split += 1
            self.nc.tensor.wait_ge(self.s_low, tile + 1)
            self.tile_seen = tile
        s = slice(o * P, (o + len(requests)) * P)
        return self.high[:, tile % SPLIT, s], self.low[:, tile % SPLIT, s]

    def matmul(self, *a, hold=False, **kw):
        mm = self.nc.tensor.matmul(*a, **kw)
        done = len(self.blocks) // TB if not hold else (len(self.blocks) - 1) // TB
        if self.freed < done:
            mm.then_inc(self.s_free, 1)
            self.freed += 1
        return mm

    def last_matmul(self, *a, **kw):
        return self.pe.done(self.nc.tensor.matmul(*a, **kw))

    def product(self, out, name, layer, col, ks, moving):
        n = len(ks)
        for i, c in enumerate(ks):
            wh, wl = self.weights([(name, layer, c, col)])
            xh, xl = moving(c)
            self.matmul(out, wh, xh, hold=True, start=(i == 0), stop=False)
            self.matmul(out, wh, xl, hold=True, start=False, stop=False)
            if i < n - 1:
                self.matmul(out, wl, xh, start=False, stop=False)
            else:
                return self.last_matmul(out, wl, xh, start=False, stop=True)

    def rows_product(self, outs, name, layer, cols, kc, stationary):
        tok = None
        for k in range(kc):
            wh, wl = self.weights([(name, layer, k, c) for c in cols])
            for i, out in enumerate(outs):
                xh, xl = stationary(k, i)
                self.matmul(out, xh, wh, hold=True, start=(k == 0), stop=False)
                self.matmul(out, xl, wh, hold=True, start=False, stop=False)
                if k == kc - 1:
                    tok = self.last_matmul(out, xh, wl, start=False, stop=True)
                else:
                    self.matmul(out, xh, wl, hold=(i < len(outs) - 1), start=False, stop=False)
        return tok


def on(q, waits, fn, *a, **kw):
    q.wait(*waits)
    return q.done(fn(*a, **kw))


def cols(ap, n):
    return ap.unsqueeze(2)


SEQS = slice(CTX, T2)
LNEXP = "natural_log_exp_and_others"


def emit(k):
    nc = k.nc
    load_inputs(k)
    first_block(k)
    second_block(k)


def load_inputs(k):
    nc, io = k.nc, k.io
    s0 = k.s_start[0]
    n = k.n_loads
    nc.scalar.dma_start(k.par[:, :], io["params"]).then_inc(s0, 16)
    nc.scalar.dma_start(k.X[:, :, SEQS], io["x"]).then_inc(s0, 16)
    nc.scalar.dma_start(k.X[:, :, 0:CTX], io["ctx"]).then_inc(s0, 16)
    n += 48
    for q in (k.pe, k.act, k.dve, k.pool):
        q.eng.wait_ge(s0, n)
    t = on(k.dve, [], nc.vector.memset, k.keep[:, :], 1.0)
    on(k.dve, [t], nc.vector.memset, k.keep[:, :].rearrange("p (c t) -> p c t", t=CH)[:, :, 0:1], 0.0)
    k.negsink = k.small[:, 100:112]
    on(k.dve, [], nc.vector.tensor_scalar, k.negsink, k.col("sink", 0, 12), -1.0, None, ALU.mult)
    k.x_toks = [split(k, k.X[:, i, SEQS], i, SEQS) for i in range(DC)]


def split(k, src, i, s, waits=(), high=None, low=None):
    nc = k.nc
    xh, xl = (k.XH[:, i, s], k.XL[:, i, s]) if high is None else (high, low)
    th = on(k.act, [*waits, k.xh_read], nc.scalar.copy, xh, src)
    return on(k.dve, [*waits, th], nc.vector.tensor_tensor, xl, src, xh.bitcast(F32), ALU.subtract)


def moving_x(k, toks, s=SEQS):
    def get(c):
        k.pe.wait(toks[c] if isinstance(toks, list) else toks)
        return k.XH[:, c, s], k.XL[:, c, s]
    return get


def rows_x(k, toks):
    def get(c, tile):
        k.pe.wait(toks[c] if isinstance(toks, list) else toks)
        s = slice(tile * P, (tile + 1) * P)
        return k.XH[:, c, s], k.XL[:, c, s]
    return get



def mean_squares(k, chunks, stat, n, toks):
    nc = k.nc
    b = k.take("out")
    t = None
    for i, (x, tok) in enumerate(zip(chunks, toks)):
        j = k.turn_sq % 2
        k.turn_sq += 1
        sq = k.SQ[:, j, 0:n]
        ts = on(k.act, [tok, k.sq_read[j]], nc.scalar.activation, sq, x, ACT.Square)
        k.pe.wait(ts)
        t = k.sq_read[j] = k.last_matmul(k.bank[b][:, 0:n], stat, sq, start=(i == 0), stop=(i == len(chunks) - 1))
    return b, t


def rsqrt_of(k, b, n, t, eps_col):
    nc = k.nc
    t = on(k.act, [t, k.rs_read], nc.scalar.activation, k.RS[:, 0:n], k.bank[b][:, 0:n], ACT.Ln,
           bias=k.c["cols"][:, eps_col:eps_col + 1])
    k.read[b] = t
    return on(k.act, [t], nc.scalar.activation, k.RS[:, 0:n], k.RS[:, 0:n], ACT.Exp, scale=-0.5)


def layer_norm(k, g, b, layer, toks):
    nc = k.nc
    bank = k.take("out")
    for i in range(DC):
        k.pe.wait(toks[i])
        args = (k.bank[bank][:, 0:SEQ], k.c["meanD"][:, :], k.X[:, i, SEQS])
        if i < DC - 1:
            k.matmul(*args, start=(i == 0), stop=False)
        else:
            t = k.last_matmul(*args, start=False, stop=True)
    k.fill(1.5)
    centred = []
    for i in range(DC // 2):
        xs = k.X[:, 2 * i:2 * i + 2, SEQS]
        mean = k.bank[bank][:, 0:SEQ].unsqueeze(1).to_broadcast([P, 2, SEQ])
        tc = on(k.dve, [t], nc.vector.tensor_tensor, xs, xs, mean, ALU.subtract)
        centred += [tc, tc]
    k.read[bank] = centred[-1]
    b2, t = mean_squares(k, [k.X[:, i, SEQS] for i in range(DC)], k.c["meanD"][:, :], SEQ, centred)
    k.fill(5)
    t = rsqrt_of(k, b2, SEQ, t, 0)
    out = []
    for i in range(DC):
        x, bias = k.X[:, i, SEQS], k.col(b, layer * DC + i)
        xh, xl = k.XH[:, i, SEQS], k.XL[:, i, SEQS]
        ts = on(k.dve, [t], nc.vector.scalar_tensor_tensor, x, x, k.col(g, layer * DC + i), k.RS[:, 0:SEQ],
                ALU.mult, ALU.mult)
        th = on(k.act, [ts, k.xh_read], nc.scalar.activation, xh, x, ACT.Identity, bias=bias)
        tl = on(k.dve, [th], nc.vector.scalar_tensor_tensor, xl, x, bias, xh.bitcast(F32), ALU.add, ALU.subtract)
        k.x_ready[i] = on(k.pool, [tl], nc.gpsimd.tensor_scalar, x, x, bias, None, ALU.add)
        out.append(tl)
    k.rs_read = ts
    return out


def rms_heads(k, o, stat, g, gate, n, eps_col, toks, chunk, s):
    nc = k.nc
    out = []
    for i, x in enumerate(o):
        b, t = mean_squares(k, [x], stat, n, [toks[i]])
        k.fill(1.5)
        t = rsqrt_of(k, b, n, t, eps_col)
        t = on(k.dve, [t], nc.vector.scalar_tensor_tensor, x, x, g(i), k.RS[:, 0:n], ALU.mult, ALU.mult)
        k.rs_read = t
        if gate is not None:
            t = on(k.dve, [t], nc.vector.tensor_tensor, x, x, gate(i), ALU.mult)
        out.append(split(k, x, chunk + i, s, [t]))
    return out



def rope(k, dst, rot, cos, sin, tok):
    nc = k.nc
    b = k.take("out")
    k.pe.wait(tok)
    t = k.last_matmul(k.bank[b][:, 0:SEQ], rot, dst, start=True, stop=True)
    tmp = k.TMP[:, k.turn_tmp % 2, 0:SEQ]
    k.turn_tmp += 1
    t1 = on(k.dve, [t, k.dve.now()], nc.vector.tensor_tensor, tmp, k.bank[b][:, 0:SEQ], sin, ALU.mult)
    k.read[b] = t1
    t2 = on(k.dve, [t], nc.vector.tensor_tensor, dst, dst, cos, ALU.mult)
    return on(k.dve, [t1, t2], nc.vector.tensor_tensor, dst, dst, tmp, ALU.add)



def softmax_rows(k, scores, bias, T, t_scores, start, sink=None):
    nc = k.nc
    c = 4 * (k.turn_small % 12)
    k.turn_small += 1
    nm, den, rd, es = (k.small[:, c + i:c + i + 1] for i in range(4))
    t = on(k.dve, [t_scores], nc.vector.tensor_tensor_reduce, T, scores, bias, -1.0,
           start, ALU.add, ALU.min, nm)
    t_max = t
    t = on(k.act, [t], nc.scalar.activation, T, T, ACT.Exp, bias=nm, scale=-1.0, accum_out=den)
    if sink is not None:
        ts = on(k.act, [t_max], nc.scalar.activation, es, sink, ACT.Exp, bias=nm)
        t = on(k.dve, [ts], nc.vector.tensor_tensor, den, den, es, ALU.add)
    t = on(k.dve, [t], nc.vector.reciprocal, rd, den)
    return t_max, t, rd


def turn(k, blocks, keys, PTi, toks, copy_on):
    nc = k.nc
    PT = k.PT[:, PTi, :].rearrange("p (a q) -> p a q", q=SEQ)
    k.pe.wait(*toks)
    out = []
    tp = None
    for pair in range((keys + 1) // 2):
        b = k.take("turned")
        mine = [x for x in blocks if x[0] // 2 == pair]
        for kt, qt, src in mine:
            o = (kt % 2) * SEQ + qt * P
            tp = pe_t = k.pe.done(nc.tensor.transpose(k.bank[b][:, o:o + P], src, k.c["ident"][:, :]))
        have = {kt: min(q for a, q, _ in mine if a == kt) * P for kt, _, _ in mine}
        runs = [(min(have), 0, len(have) * SEQ)] if not any(have.values()) else \
            [(kt, q0, SEQ - q0) for kt, q0 in have.items()]
        q, copy = (k.act, nc.scalar.copy) if (pair + copy_on) % 2 == 0 else (k.dve, nc.vector.tensor_copy)
        flat = k.PT[:, PTi, :]
        for kt, q0, n in runs:
            at = (kt % 2) * SEQ + q0
            t = on(q, [pe_t, k.pt_read[PTi]], copy, flat[:, kt * SEQ + q0:kt * SEQ + q0 + n], k.bank[b][:, at:at + n])
        out.append(t)
        k.read[b] = t
    return PT, out, tp


LAG = 2


def attend(k, units, fill=0.0):
    staged = []
    for i in range(len(units) + LAG):
        if i < len(units):
            staged.append(scores_of(k, units[i], i))
        if i >= LAG:
            k.fill(fill)
            values_of(k, units[i - LAG], staged[i - LAG], i - LAG)


def scores_of(k, u, i):
    nc = k.nc
    Ti = k.turn_T % 3
    k.turn_T += 1
    T = k.Tt[:, Ti, :]
    k.dve.wait(k.T_read[Ti])
    rows = []
    if u["prepare"] is not None:
        u["prepare"]()
    for (bank_cols, parts) in u["scores"]:
        b = k.take("score")
        for (o, n, q, kk) in parts:
            t = k.last_matmul(k.bank[b][:, o:o + n], q, kk, start=(o == 0), stop=True, skip_group_check=True)
        for (o, n, q, kk), (To, bias, start, sink) in zip(parts, bank_cols):
            t_max, t_rd, rd = softmax_rows(k, k.bank[b][:, o:o + n], bias, T[:, To:To + n], t, start, sink)
            rows.append((To, n, t_rd, rd))
        k.read[b] = t_max
    if u.get("nb") is not None:
        k.nb_read[u["nb"]] = t_max
    return Ti, rows


def values_of(k, u, staged, i):
    nc = k.nc
    Ti, rows = staged
    T = k.Tt[:, Ti, :]
    toks = []
    if u["diff"]:
        h = len(rows) // 2
        for (To, n, t, rd), (To1, _, t1, rd1) in zip(rows[:h], rows[h:]):
            ta = on(k.dve, [t], nc.vector.tensor_scalar, T[:, To:To + n], T[:, To:To + n], rd, None, ALU.mult)
            tb = on(k.dve, [t1], nc.vector.tensor_tensor, rd1, rd1, k.neglam, ALU.mult)
            toks.append(on(k.dve, [ta, tb], nc.vector.scalar_tensor_tensor, T[:, To:To + n], T[:, To1:To1 + n], rd1,
                           T[:, To:To + n], ALU.mult, ALU.add))
        rows = rows[:h]
    else:
        for (To, n, t, rd) in rows:
            toks.append(on(k.dve, [t], nc.vector.tensor_scalar, T[:, To:To + n], T[:, To:To + n], rd, None, ALU.mult))
    blocks = [(kt, qt, T[:, To + kt * P:To + (kt + 1) * P]) for qt, (To, n, _, _) in enumerate(rows) for kt in range(n // P)]
    keys = max(kt for kt, _, _ in blocks) + 1
    PTi = k.turn_PT % 2
    k.turn_PT += 1
    PT, copied, t_turned = turn(k, blocks, keys, PTi, toks, k.turn_PT % 2 if keys == 2 else 0)
    k.T_read[Ti] = t_turned
    if u["first"]:
        k.obank = k.take("out")
    out = k.bank[k.obank][u["rows"], 0:SEQ]
    k.pe.wait(*copied)
    for kt in range(keys):
        q0 = min(q for a, q, _ in blocks if a == kt) * P
        args = (out[:, q0:SEQ], u["v"](kt), PT[:, kt, q0:SEQ])
        kw = dict(start=(kt == 0), stop=(kt == keys - 1))
        if kt < keys - 1:
            k.matmul(*args, **kw)
        else:
            t = k.last_matmul(*args, **kw)
    k.pt_read[PTi] = t
    if u["last"]:
        if u["fp32"] is not None:
            k.read[k.obank] = on(k.act, [t], nc.scalar.copy, u["fp32"], k.bank[k.obank][:, 0:SEQ])
        else:
            k.read[k.obank] = split(k, k.bank[k.obank][:, 0:SEQ], *u["to"], [t])
        u["tok"].append(k.read[k.obank])


BIGNUM = 3.0e38


def view(buf, off, *dims):
    n = int(np.prod(dims))
    v = buf[:, off:off + n]
    if len(dims) == 1:
        return v
    if len(dims) == 2:
        return v.rearrange("p (a b) -> p a b", b=dims[1])
    if len(dims) == 3:
        return v.rearrange("p (a b c) -> p a b c", b=dims[1], c=dims[2])
    return v.rearrange("p (a b c d) -> p a b c d", b=dims[1], c=dims[2], d=dims[3])


def project(k, name, layer, ncols, dst, toks, scale=1.0, func=None, first=0):
    nc = k.nc
    out = []
    for i in range(ncols):
        b = k.take("gemm")
        t = k.product(k.bank[b][:, 0:SEQ], name, layer, first + i, range(DC), moving_x(k, toks))
        t = on(k.act, [t], nc.scalar.activation, dst(i), k.bank[b][:, 0:SEQ], func or ACT.Copy, scale=scale)
        k.read[b] = t
        out.append(t)
    return out


def scope_end(k):
    marks = [q.now() for q in (k.pe, k.act, k.dve, k.pool)]
    for q in (k.act, k.dve, k.pool):
        q.wait(*marks)
    k.scope_marks = marks


def first_block(k):
    nc = k.nc
    with ExitStack() as filler_scope:
        ch, cl = (k.sb(filler_scope, "c_" + n, DC, P, dt=F32R) for n in ("high_part", "low_part"))
        k.filler = modulations(k, ch, cl, k.sb(filler_scope, "mod_rows", 2, 512))
        k.x_ready = [None] * DC
        toks = k.x_toks
        for layer in range(DEPTH):
            if layer == 0:
                mixed = even_mixer(k, toks)
                w_out = "ev_w_out"
            else:
                mixed = odd_mixer(k, toks)
                w_out = "od_w_out"
            toks = residual(k, w_out, 0, moving_x(k, mixed), range(DC), ALPHA)
            k.xh_read = k.pe.now()
            toks = layer_norm(k, "ln1_g", "ln1_b", layer, toks)
            toks = ffn1(k, layer, toks)
            toks = layer_norm(k, "ln2_g", "ln2_b", layer, toks)
            toks = per_layer_embedding(k, layer, toks)
            scope_end(k)
        k.drain_filler()
        k.fence()


def ffn1(k, layer, toks):
    nc = k.nc
    half = FFN // P // 2
    with ExitStack() as scope:
        hh, hl = (k.sb(scope, f"hidden_{n}{layer}", half, SEQ, dt=F32R) for n in ("high", "low"))
        hid_read = None
        for part in range(2):
            th = []
            for i in range(half):
                b = k.take("gemm")
                t = k.product(k.bank[b][:, 0:SEQ], "ffn_w1", layer, part * half + i, range(DC), moving_x(k, toks))
                j = i % 2
                sq = k.TMP[:, j, 0:SEQ]
                t1 = on(k.act, [t, k.tmp_read[j]], nc.scalar.activation, sq, k.bank[b][:, 0:SEQ], ACT.Relu)
                t2 = on(k.dve, [t1], nc.vector.tensor_tensor, sq, sq, sq, ALU.mult)
                k.read[b] = t1
                t3 = on(k.act, [t2, hid_read], nc.scalar.copy, hh[:, i, :], sq)
                t4 = on(k.dve, [t3], nc.vector.tensor_tensor, hl[:, i, :], sq, hh[:, i, :].bitcast(F32), ALU.subtract)
                k.tmp_read[j] = t4
                th.append(t4)
            k.fill(2.5)

            def moving(c):
                k.pe.wait(th[c - part * half])
                return hh[:, c - part * half, :], hl[:, c - part * half, :]

            out = residual(k, "ffn_w2", layer, moving, range(part * half, (part + 1) * half), ALPHA if part == 0 else 1.0)
            hid_read = k.pe.now()
        k.xh_read = hid_read
        scope_end(k)
    return out


def residual(k, name, layer, moving, ks, alpha):
    nc, out = k.nc, []
    for i in range(DC):
        b = k.take("gemm")
        t = k.product(k.bank[b][:, 0:SEQ], name, layer, i, ks, moving)
        x = k.X[:, i, SEQS]
        t = on(k.dve, [t, k.x_ready[i]], nc.vector.scalar_tensor_tensor, x, x, alpha, k.bank[b][:, 0:SEQ],
               ALU.mult, ALU.add)
        k.read[b] = k.x_ready[i] = t
        out.append(t)
    return out


def per_layer_embedding(k, layer, toks):
    nc = k.nc
    with ExitStack() as scope:
        pT = k.sb(scope, f"pT{layer}", PLE // P, SEQ)
        ph, pl = (k.sb(scope, f"p_{n}{layer}", PLE // P, SEQ, dt=F32R) for n in ("high", "low"))
        e = k.sb(scope, f"e{layer}", DC, SEQ)
        gate = k.sb(scope, f"gate{layer}", DC, SEQ)
        k.pool.wait(*k.scope_marks)
        nc.gpsimd.dma_start(pT[:, :, :], k.io["p"][layer]).then_inc(k.s_start[1], 16)
        for q in (k.act, k.dve):
            q.eng.wait_ge(k.s_start[1], 16 * (layer + 1))
        tp = [split(k, pT[:, i, :], 0, None, [], ph[:, i, :], pl[:, i, :]) for i in range(PLE // P)]

        def moving(c):
            k.pe.wait(tp[c])
            return ph[:, c, :], pl[:, c, :]

        te = []
        for i in range(DC):
            b = k.take("gemm")
            t = k.product(k.bank[b][:, 0:SEQ], "ple_w_proj", layer, i, range(PLE // P), moving)
            k.read[b] = t = on(k.act, [t], nc.scalar.copy, e[:, i, :], k.bank[b][:, 0:SEQ])
            te.append(t)
        b, t = mean_squares(k, [e[:, i, :] for i in range(DC)], k.c["meanD"][:, :], SEQ, te)
        t = rsqrt_of(k, b, SEQ, t, 0)
        tn = [on(k.dve, [t], nc.vector.scalar_tensor_tensor, e[:, i, :], e[:, i, :], k.col("ple_g", layer * DC + i),
                 k.RS[:, 0:SEQ], ALU.mult, ALU.mult) for i in range(DC)]
        k.rs_read = tn[-1]
        gates = []
        for i in range(DC):
            b = k.take("gemm")
            t = k.product(k.bank[b][:, 0:SEQ], "ple_w_gate", layer, i, range(DC), moving_x(k, toks))
            g = gate[:, i, :]
            k.read[b] = t = on(k.act, [t], nc.scalar.activation, g, k.bank[b][:, 0:SEQ], ACT.Sigmoid)
            gates.append(on(k.dve, [t, tn[i]], nc.vector.tensor_tensor, g, g, e[:, i, :], ALU.mult))
        k.xh_read = k.pe.now()
        out = []
        nc.scalar.preload_act_table_set(LNEXP)
        for i in range(DC):
            x = k.X[:, i, SEQS]
            t = k.x_ready[i] = on(k.dve, [gates[i], k.x_ready[i]], nc.vector.tensor_tensor, x, x, gate[:, i, :], ALU.add)
            if layer == 0:
                out.append(split(k, x, i, SEQS, [t]))
        scope_end(k)
    return out


def head_rows(h):
    return slice(HD * (h % 2), HD * (h % 2) + HD)


def even_mixer(k, toks):
    nc = k.nc
    with ExitStack() as scope:
        sb = lambda n, *shape: k.sb(scope, "even_" + n, *shape)
        qT, kT, V = sb("q", 4, SEQ), sb("k", 4, SEQ), sb("v", NQ, 512)
        hq, hf, hg, HV = sb("hq", 4, SEQ), sb("hf", 4, SEQ), sb("hg", 4, SEQ), sb("hv", NQ, 512)
        k.load_consts(scope, ["causal", "cos1", "sin1", "rot1"], 2)
        for q in (k.pe, k.dve):
            q.eng.wait_ge(k.s_start[2], k.n_loads)
        c = k.small[:, 48:56]
        g = c[:, 5:6]
        lb, oml = k.small[:, 56:60], k.small[:, 60:64]
        rot = (k.c["rot1"][:, :], k.c["cos1"][:, :], k.c["sin1"][:, :])
        tq = project(k, "ev_w_in", 0, 4, lambda i: qT[:, i, :], toks, scale=QSCALE, first=0)
        tk = project(k, "ev_w_in", 0, 4, lambda i: kT[:, i, :], toks, first=4)
        tq = [rope(k, qT[:, i, :], *rot, tq[i]) for i in range(4)]
        project(k, "ev_w_in", 0, 4, lambda i: hq[:, i, :], toks, func=ACT.Silu, first=12)
        tk = [rope(k, kT[:, i, :], *rot, tk[i]) for i in range(4)]
        project(k, "ev_w_in", 0, 4, lambda i: hg[:, i, :], toks, func=ACT.Silu, first=24)
        project(k, "ev_w_in", 0, 4, lambda i: hf[:, i, :], toks, func=ACT.Sigmoid, first=16)
        t = on(k.dve, [], nc.vector.tensor_tensor, lb, k.col("lb", 0, 4), k.col("lb", 4, 4), ALU.subtract)
        t = on(k.act, [t], nc.scalar.activation, lb, lb, ACT.Sigmoid)
        on(k.dve, [t], nc.vector.tensor_scalar, oml, lb, -1.0, 1.0, ALU.mult, ALU.add)
        nc.scalar.preload_act_table_set(LNEXP)
        lp = k.col("lam", 0, 256)
        t0 = on(k.dve, [], nc.vector.tensor_tensor_reduce, lp[:, 0:64], lp[:, 0:64], lp[:, 64:128], 1.0, 0.0, ALU.mult,
                ALU.add, c[:, 0:1])
        t1 = on(k.dve, [], nc.vector.tensor_tensor_reduce, lp[:, 128:192], lp[:, 128:192], lp[:, 192:256], 1.0, 0.0,
                ALU.mult, ALU.add, c[:, 1:2])
        t = on(k.act, [t0, t1], nc.scalar.activation, c[:, 2:4], c[:, 0:2], ACT.Exp)
        t = on(k.dve, [t], nc.vector.tensor_tensor, c[:, 4:5], c[:, 3:4], c[:, 2:3], ALU.subtract)
        k.neglam = c[:, 4:5]
        on(k.dve, [t], nc.vector.tensor_scalar, k.neglam, k.neglam, -LAM_INIT, None, ALU.add)
        on(k.dve, [], nc.vector.tensor_scalar, g, k.col("sub_g"), 1.0 - LAM_INIT, None, ALU.mult)
        value_rows(k, "ev_w_in", 0, [8, 9, 10, 11], V, 0, rows_x(k, toks), range(2, 4))
        value_rows(k, "ev_w_in", 0, [20, 21, 22, 23], HV, 0, rows_x(k, toks), range(2, 4))
        k.xh_read = k.pe.now()
        k.fill(3)
        k.fence()
        with ExitStack() as inner:
            attention_buffers(k, inner, "da")
            o = k.sb(inner, "da_o", HEADS_E, SEQ)
            causal = view(k.c["causal"], 0, NQ, SEQ)
            units, done = [], []
            for h in range(HEADS_E):
                sc = []
                for comp in range(2):
                    r = slice(HD * comp, HD * comp + HD)
                    parts = [(qt * SEQ, (qt + 1) * P, qT[r, h, qt * P:(qt + 1) * P], kT[r, h, 0:(qt + 1) * P])
                             for qt in range(NQ)]
                    bank_cols = [(comp * 512 + qt * SEQ, causal[:, qt, 0:(qt + 1) * P], BIGNUM, None)
                                 for qt in range(NQ)]
                    sc.append((bank_cols, parts))
                units.append(dict(prepare=None, scores=sc, diff=True, first=True, last=True, rows=slice(0, P),
                                  v=lambda kt, h=h: V[:, kt, h * P:(h + 1) * P], fp32=o[:, h, :], tok=done))
            attend(k, units, 3.0)
            mixed = rms_heads(k, [o[:, h, :] for h in range(HEADS_E)], k.c["mean128"][:, :], lambda i: g, None, SEQ, 0,
                              done, 0, SEQS)
            scope_end(k)
        with ExitStack() as inner:
            mixed += hgrn2(k, inner, hq, hf, hg, HV, lb, oml)
            scope_end(k)
    return mixed


def attention_buffers(k, scope, name):
    k.Tt = k.sb(scope, name + "_scores", 3, 1024)
    k.PT = k.sb(scope, name + "_turned", 2, 1024)
    k.T_read, k.pt_read = [None] * 3, [None] * 2


def value_rows(k, name, layer, chunks, V, off, stationary, tiles):
    nc = k.nc
    n = len(chunks) * P
    banks = [k.take(["gemm", "out"][i // 2]) for i in range(len(tiles))]
    t = k.rows_product([k.bank[b][:, 0:n] for b in banks], name, layer, chunks, DC,
                       lambda c, i: stationary(c, tiles[i]))
    for i, b in enumerate(banks):
        k.read[b] = on(k.act, [t], nc.scalar.copy, V[:, i, off:off + n], k.bank[b][:, 0:n])
    return k.read[banks[-1]]


def hgrn2(k, scope, q, f, g, V, lb, oml):
    nc = k.nc
    v1, a1 = nc.vector, nc.scalar
    W = HEADS_E * SEQ
    NC_ = SEQ // CH
    S5 = [k.sb(scope, f"hgrn_a{i}", W)[:, :] for i in range(5)]
    B3 = [k.sb(scope, f"hgrn_b{i}", W)[:, :] for i in range(3)]
    S = k.sb(scope, "hgrn_state", HEADS_E, 3, P)
    ch = lambda x: x.rearrange("p (c t) -> p c t", t=CH)
    hd = lambda x: x.rearrange("p (h t) -> p h t", t=SEQ)
    lf, kk, b, qi, ki = S5
    qo, ks, turned = B3
    fm = hd(lf)
    qf = q[:, :, :].rearrange("p h t -> p (h t)")
    for h in range(HEADS_E):
        t = on(k.dve, [], v1.tensor_scalar, fm[:, h, :], f[:, h, :], oml[:, h:h + 1], lb[:, h:h + 1], ALU.mult, ALU.add)
    t = on(k.dve, [t], v1.tensor_scalar, kk, lf, -1.0, 1.0, ALU.mult, ALU.add)
    t = on(k.act, [t], a1.activation, lf, lf, ACT.Ln)
    for i in range(2):
        s = slice(i * 512, (i + 1) * 512)
        t2 = on(k.dve, [t], v1.tensor_tensor_scan, b[:, s], k.keep[:, :], lf[:, s], 0.0, ALU.mult, ALU.add)
    t = t2
    k.fill(8)
    bc = ch(b)
    mid = bc[:, :, CH // 2 - 1:CH // 2].to_broadcast([P, W // CH, CH])
    end = bc[:, :, CH - 1:CH].to_broadcast([P, W // CH, CH])
    td = on(k.dve, [t], v1.tensor_tensor, ch(lf), bc, mid, ALU.subtract)
    t1 = on(k.act, [td], a1.activation, qi, lf, ACT.Exp)
    t2 = on(k.act, [td], a1.activation, ki, lf, ACT.Exp, scale=-1.0)
    t3 = on(k.act, [t], a1.activation, qo, b, ACT.Exp)
    td = on(k.dve, [t2], v1.tensor_tensor, ch(lf), bc, end, ALU.subtract)
    t4 = on(k.act, [td], a1.activation, ks, lf, ACT.Exp, scale=-1.0)
    dc = k.small[:, 64:64 + W // CH]
    tdc = on(k.dve, [t3], v1.tensor_copy, dc, ch(qo)[:, :, CH - 1])
    t1 = on(k.dve, [t1], v1.tensor_tensor, qi, qi, qf, ALU.mult)
    t2 = on(k.dve, [t2], v1.tensor_tensor, ki, ki, kk, ALU.mult)
    t3 = on(k.dve, [tdc], v1.tensor_tensor, qo, qo, qf, ALU.mult)
    t4 = on(k.dve, [t4], v1.tensor_tensor, ks, ks, kk, ALU.mult)
    k.fill(5)
    AT = lf.rearrange("p (a t) -> p a t", t=P)
    tz = on(k.dve, [t4], v1.memset, lf, 0.0)
    b0 = k.take("score")
    k.pe.wait(t1, t2)
    for i in range(HEADS_E * NQ):
        h, tile = i // NQ, i % NQ
        for j in range(2):
            o = tile * P + j * CH
            t = k.last_matmul(k.bank[b0][j * CH:(j + 1) * CH, i * CH:(i + 1) * CH], hd(ki)[:, h, o:o + CH],
                              hd(qi)[:, h, o:o + CH], start=True, stop=True)
    for j in range(2):
        r = slice(j * CH, (j + 1) * CH)
        mask = k.c["before"][r, :].bitcast(U32).unsqueeze(1).to_broadcast([CH, HEADS_E * NQ, CH])
        ta = on(k.dve, [t, tz], v1.copy_predicated, AT[r, :, j * CH:(j + 1) * CH], mask,
                k.bank[b0][r, :].rearrange("p (a t) -> p a t", t=CH))
    k.read[b0] = ta
    ksT = turned.rearrange("p (a h f) -> p a h f", h=HEADS_E, f=P)
    k.pe.wait(t4)
    for tile in range(NQ):
        bt = k.take("turned")
        for h in range(HEADS_E):
            t = k.pe.done(nc.tensor.transpose(k.bank[bt][:, h * P:(h + 1) * P], hd(ks)[:, h, tile * P:(tile + 1) * P],
                                              k.c["ident"][:, :]))
        k.read[bt] = tk = on(k.act, [t], a1.copy, ksT[:, tile, :, :], k.bank[bt][:, :].rearrange("p (h f) -> p h f", f=P))
    k.pe.wait(tk)
    for c in range(NC_ - 1):
        j, tile = c % 2, c // 2
        bs = k.take("score")
        r = slice(j * CH, (j + 1) * CH)
        for h in range(HEADS_E):
            t = k.last_matmul(k.bank[bs][:, h * P:(h + 1) * P], ksT[r, tile, h, :], V[r, tile, h * P:(h + 1) * P],
                              start=True, stop=True)
        for h in range(HEADS_E):
            add = k.bank[bs][:, h * P:(h + 1) * P]
            if c == 0:
                ts = on(k.dve, [t], v1.tensor_copy, S[:, h, c, :], add)
            else:
                ts = on(k.dve, [t, k.dve.now()], v1.scalar_tensor_tensor, S[:, h, c, :], S[:, h, c - 1, :],
                        dc[:, h * NC_ + c:h * NC_ + c + 1], add, ALU.mult, ALU.add)
        k.read[bs] = ts
    k.fill(5)
    k.pe.wait(ta, t3, ts)
    oT = kk.rearrange("p (h t) -> p h t", t=SEQ)
    toks = []
    for h in range(HEADS_E):
        bo = k.take("out")
        vh = slice(h * P, (h + 1) * P)
        for tile in range(NQ):
            k.matmul(k.bank[bo][:, tile * P:(tile + 1) * P], V[:, tile, vh], AT[:, h * NQ + tile, :],
                     start=(tile == 0), stop=False, skip_group_check=True)
        for c in range(1, NC_):
            t = k.last_matmul(k.bank[bo][:, c * CH:(c + 1) * CH], S[:, h, c - 1, :],
                              hd(qo)[:, h, c * CH:(c + 1) * CH], start=False, stop=(c == NC_ - 1), skip_group_check=True)
        k.read[bo] = t = on(k.act, [t], a1.copy, oT[:, h, :], k.bank[bo][:, 0:SEQ])
        toks.append(t)
    return rms_heads(k, [oT[:, h, :] for h in range(HEADS_E)], k.c["mean128"][:, :], lambda i: k.col("hg_g"),
                     lambda i: g[:, i, :], SEQ, 0, toks, 4, SEQS)


def odd_mixer(k, toks):
    nc = k.nc
    with ExitStack() as scope:
        qT, kT = k.sb(scope, "odd_q", DC, SEQ), k.sb(scope, "odd_k", DC, SEQ)
        V = k.sb(scope, "odd_v", NQ, D)
        for q in (k.act,):
            q.wait(*k.scope_marks)
        k.load_consts(scope, ["dilated", "cos1", "sin1", "rot1"], 3)
        for q in (k.pe, k.dve):
            q.eng.wait_ge(k.s_start[3], k.n_loads)
        rot = (k.c["rot1"][:, :], k.c["cos1"][:, :], k.c["sin1"][:, :])
        tq = project(k, "od_w_in", 0, DC, lambda i: qT[:, i, :], toks, scale=QSCALE, first=0)
        tk = project(k, "od_w_in", 0, DC, lambda i: kT[:, i, :], toks, first=DC)
        for i in range(DC):
            rope(k, qT[:, i, :], *rot, tq[i])
            k.fill(0.5)
        for half in range(2):
            value_rows(k, "od_w_in", 0, [2 * DC + 4 * half + i for i in range(4)], V, 512 * half, rows_x(k, toks),
                       range(2, 4))
            for i in range(4 * half, 4 * half + 4):
                rope(k, kT[:, i, :], *rot, tk[i])
        k.xh_read = k.pe.now()
        k.fill(3)
        k.fence()
        attention_buffers(k, scope, "odd")
        mask = view(k.c["dilated"], 0, NQ, SEQ)
        units, done = [], []
        for h in range(HEADS_O):
            r, c = head_rows(h), h // 2
            parts = [(qt * SEQ, (qt + 1) * P, qT[r, c, qt * P:(qt + 1) * P], kT[r, c, 0:(qt + 1) * P])
                     for qt in range(NQ)]
            bank_cols = [(qt * SEQ, mask[:, qt, 0:(qt + 1) * P], BIGNUM, None) for qt in range(NQ)]
            units.append(dict(prepare=None, scores=[(bank_cols, parts)], diff=False, first=h % 2 == 0, last=h % 2 == 1,
                              rows=r, v=lambda kt, h=h: V[:, kt, h * HD:(h + 1) * HD], fp32=None, to=(c, SEQS),
                              tok=done))
        attend(k, units, 2.5)
        scope_end(k)
    return done



def modulations(k, ch, cl, row):
    nc = k.nc
    cc = k.col("cc", 0, 16)
    t = on(k.act, [], nc.scalar.activation, cc, cc, ACT.Silu)
    ccv = cc.rearrange("p (c s) -> p c s", s=2)
    t0 = on(k.dve, [], nc.vector.memset, ch[:, :, :].bitcast(F32), 0.0)
    t1 = on(k.dve, [], nc.vector.memset, cl[:, :, :].bitcast(F32), 0.0)
    t = on(k.act, [t, t0], nc.scalar.copy, ch[:, :, 0:2], ccv)
    ready = on(k.dve, [t, t1], nc.vector.tensor_tensor, cl[:, :, 0:2], ccv, ch[:, :, 0:2].bitcast(F32), ALU.subtract)
    row_read = [None, None]
    for layer in range(DEPTH):
        for i in range(12):
            k.pe.wait(ready)
            b = k.take("gemm")
            out = k.bank[b][:, 0:512]
            for c in range(DC):
                wh, wl = k.weights([("w_mod_2", layer, c, 4 * i + j) for j in range(4)])
                k.matmul(out, ch[:, c, :], wh, hold=True, start=(c == 0), stop=False)
                k.matmul(out, cl[:, c, :], wh, hold=True, start=False, stop=False)
                if c < DC - 1:
                    k.matmul(out, ch[:, c, :], wl, start=False, stop=False)
                else:
                    t = k.last_matmul(out, ch[:, c, :], wl, start=False, stop=True)
            k.read[b] = t = on(k.act, [t, row_read[i % 2]], nc.scalar.copy, row[0:2, i % 2, :], k.bank[b][0:2, :])
            yield 5.3
            b = k.take("gemm")
            k.pe.wait(t)
            for j in range(4):
                t = k.pe.done(nc.tensor.transpose(k.bank[b][:, 2 * j:2 * j + 2], row[0:2, i % 2, j * P:(j + 1) * P],
                                                  k.c["ident"][0:2, 0:2]))
            row_read[i % 2] = t
            bias = k.col("b_mod", 48 * layer + 4 * i, 4).unsqueeze(2).to_broadcast([P, 4, 2])
            k.read[b] = on(k.dve, [t], nc.vector.tensor_tensor, k.mod[:, layer, 4 * i:4 * i + 4, :],
                           k.bank[b][:, 0:8].rearrange("p (c s) -> p c s", s=2), bias, ALU.add)
            yield 0.5


def modulated_norm(k, layer, norm, section, lo, toks):
    nc = k.nc
    n = T2 - lo
    b, t = mean_squares(k, [k.X[:, i, lo:T2] for i in range(DC)], k.c["meanD"][:, :], n, toks)
    t = rsqrt_of(k, b, n, t, 1)
    sh, sc = k.mod[:, layer, section:section + DC, :], k.mod[:, layer, section + DC:section + 2 * DC, :]
    gs = k.gs[:, :].rearrange("p (c s) -> p c s", s=2)
    g = k.col(norm, layer * DC, DC).unsqueeze(2).to_broadcast([P, DC, 2])
    tg = on(k.dve, [], nc.vector.tensor_scalar, gs, sc, 1.0, None, ALU.add)
    tg = on(k.dve, [tg], nc.vector.tensor_tensor, gs, gs, g, ALU.mult)
    out = []
    for i in range(DC):
        for side in range(2):
            if side * CTX < lo:
                continue
            s = slice(side * CTX, (side + 1) * CTX)
            j = k.turn_tmp % 4
            k.turn_tmp += 1
            tmp = k.TMP[:, j // 2, (j % 2) * CTX:(j % 2 + 1) * CTX]
            shift, xh, xl = sh[:, i, side:side + 1], k.XH[:, i, s], k.XL[:, i, s]
            ts = on(k.dve, [t, tg], nc.vector.scalar_tensor_tensor, tmp, k.X[:, i, s], gs[:, i, side:side + 1],
                    k.RS[:, side * CTX - lo:side * CTX - lo + CTX], ALU.mult, ALU.mult)
            th = on(k.act, [ts, k.xh_read], nc.scalar.activation, xh, tmp, ACT.Identity, bias=shift)
            tl = on(k.dve, [th], nc.vector.scalar_tensor_tensor, xl, tmp, shift, xh.bitcast(F32), ALU.add, ALU.subtract)
        out.append(tl)
    k.rs_read = ts
    return out


def gated_residual(k, name, layer, moving, ks, gate, lo):
    nc = k.nc
    out = []
    for i in range(DC):
        b = k.take("gemm")
        t = k.product(k.bank[b][:, 0:T2 - lo], name, layer, i, ks, moving)
        for side in range(2):
            if side * CTX < lo:
                continue
            s = slice(side * CTX, (side + 1) * CTX)
            t2 = on(k.dve, [t], nc.vector.scalar_tensor_tensor, k.X[:, i, s],
                    k.bank[b][:, side * CTX - lo:(side + 1) * CTX - lo], k.mod[:, layer, gate + i, side:side + 1],
                    k.X[:, i, s], ALU.mult, ALU.add)
        k.read[b] = t2
        out.append(t2)
    return out


def second_block(k):
    nc = k.nc
    toks = [None] * DC
    for layer in range(DEPTH):
        lo = 0 if layer == 0 else CTX
        mixed = token_mixers(k, layer, lo, toks)
        toks = gated_residual(k, "w_out_2", layer, moving_x(k, mixed, slice(lo, T2)), range(DC), 16, lo)
        k.xh_read = k.pe.now()
        toks = modulated_norm(k, layer, "norm_ffn", 24, lo, toks)
        toks = swiglu(k, layer, lo, toks)
    b, t = mean_squares(k, [k.X[:, i, SEQS] for i in range(DC)], k.c["meanD"][:, :], SEQ, toks)
    t = rsqrt_of(k, b, SEQ, t, 1)
    with ExitStack() as scope:
        y = k.sb(scope, "y", DC, SEQ)
        for i in range(DC):
            t2 = on(k.dve, [t], nc.vector.scalar_tensor_tensor, y[:, i, :], k.X[:, i, SEQS], k.col("final", i),
                    k.RS[:, 0:SEQ], ALU.mult, ALU.mult)
            k.act.wait(t2)
            nc.scalar.dma_start(k.io["out"][:, i, :], y[:, i, :]).then_inc(k.s_out, 16)
        nc.scalar.wait_ge(k.s_out, 16 * DC)


def swiglu(k, layer, lo, toks):
    nc = k.nc
    n, half = T2 - lo, DFF // P // 2
    with ExitStack() as scope:
        hh, hl = (k.sb(scope, f"hidden2_{x}{layer}", half, n, dt=F32R) for x in ("high", "low"))
        hid_read = None
        for part in range(2):
            th = []
            for i in range(half):
                col = part * half + i
                bg, bu = k.take("gemm"), k.take("gemm")
                tg = k.product(k.bank[bg][:, 0:n], "w_gate_2", layer, col, range(DC), moving_x(k, toks, slice(lo, T2)))
                j = i % 2
                tmp = k.TMP[:, j, 0:n]
                k.read[bg] = tg = on(k.act, [tg, k.tmp_read[j]], nc.scalar.activation, tmp, k.bank[bg][:, 0:n], ACT.Silu)
                tu = k.product(k.bank[bu][:, 0:n], "w_up_2", layer, col, range(DC), moving_x(k, toks, slice(lo, T2)))
                k.read[bu] = t = on(k.dve, [tg, tu], nc.vector.tensor_tensor, tmp, tmp, k.bank[bu][:, 0:n], ALU.mult)
                t = on(k.act, [t, hid_read], nc.scalar.copy, hh[:, i, :], tmp)
                t = on(k.dve, [t], nc.vector.tensor_tensor, hl[:, i, :], tmp, hh[:, i, :].bitcast(F32), ALU.subtract)
                k.tmp_read[j] = t
                th.append(t)

            def moving(c):
                k.pe.wait(th[c - part * half])
                return hh[:, c - part * half, :], hl[:, c - part * half, :]

            if part == 1:
                nc.scalar.preload_act_table_set(LNEXP)
            out = gated_residual(k, "w_down_2", layer, moving, range(part * half, (part + 1) * half), 40, lo)
            hid_read = k.pe.now()
        k.xh_read = hid_read
        scope_end(k)
    return out


def project2(k, layer, plan, toks):
    nc = k.nc
    for first, count, dst, a, scale, func, rotate in plan:
        if first is None:
            value_rows(k, "w_in_2", layer, count, dst, a, rows_x(k, toks), range(4))
            yield 10
            continue
        for i in range(count):
            b = k.take("gemm")
            d = dst[:, i, a:T2]
            t = k.product(k.bank[b][:, 0:T2 - a], "w_in_2", layer, first + i, range(DC), moving_x(k, toks, slice(a, T2)))
            k.read[b] = t = on(k.act, [t], nc.scalar.activation, d, k.bank[b][:, 0:T2 - a], func, scale=scale)
            if rotate:
                yield 2.6 * (T2 - a) / 256
                rope(k, dst[:, i, SEQS], k.c["rot2"][:, :], k.c["cos2"][:, :], k.c["sin2"][:, :], t)
            yield 2.6 * (T2 - a) / 256


def token_mixers(k, layer, lo, toks):
    nc = k.nc
    toks = modulated_norm(k, layer, "norm_mix", 0, 0, toks)
    with ExitStack() as scope:
        sb = lambda n, *shape: k.sb(scope, f"{n}{layer}", *shape)
        nq, nk, sq, sk = sb("nq", 3, T2), sb("nk", 3, T2), sb("sq", 3, T2), sb("sk", 1, T2)
        V = sb("v2", 4, 512)
        k.load_consts(scope, ["cos2", "sin2", "rot2", "window", "near"], 2 + layer)
        loads = k.n_loads + 64
        for q in (k.pe, k.dve, k.pool):
            q.eng.wait_ge(k.s_start[2 + layer], loads)
        if layer == 0:
            k.pool.wait(k.pe.now())
        nc.gpsimd.dma_start(k.wa2[:, :], k.io["wa2"][layer]).then_inc(k.s_wa2, 16)
        with ExitStack() as inner:
            g2 = lambda n, *shape: k.sb(inner, f"{n}{layer}", *shape)
            gq, gk, gg, z = g2("gq", 2, T2), g2("gk", 2, T2), g2("gg", 2, T2), g2("z", 1, T2)
            GV, o = g2("gv", 4, 256), g2("go", 2, T2)
            for _ in project2(k, layer, [(6, 2, gg, lo, 1.0, ACT.Silu, False)], toks):
                pass
            nc.scalar.preload_act_table_set(LNEXP)
            plan = [(8, 1, z, 0, 1.0, ACT.Copy, False), (0, 2, gq, lo, QSCALE, ACT.Copy, False),
                    (2, 2, gk, 0, 1.0, ACT.Copy, False), (None, [4, 5], GV, 0, None, None, None)]
            for _ in project2(k, layer, plan, toks):
                pass
            k.wa2_loads = 16 * (layer + 1)
            k.filler = project2(k, layer, [(9, 3, nq, lo, QSCALE, ACT.Copy, False), (12, 3, nk, 0, 1.0, ACT.Copy, False),
                                           (18, 3, sq, lo, QSCALE, ACT.Copy, True), (21, 1, sk, 0, 1.0, ACT.Copy, True),
                                           (None, [15, 16, 17, 22], V, 0, None, None, None)], toks)
            gla(k, inner, layer, lo, gq, gk, z, GV, o)
            k.drain_filler()
            k.xh_read = k.pe.now()
            mixed = rms_heads(k, [o[:, p, lo:T2] for p in range(2)], k.c["mean64"][:, :],
                              lambda i: k.col("gla_norm", layer * 2 + i), lambda i: gg[:, i, lo:T2],
                              T2 - lo, 1, [None, None], 0, slice(lo, T2))
            k.fence()
        attention_buffers(k, scope, f"mix{layer}")
        k.NB = sb("nb", 2, 1024)
        k.nb_read = [on(k.pool, [], nc.gpsimd.memset, k.NB[:, :, :], 0.0)] * 2
        k.SW = sb("swapped", T2)
        window, near = view(k.c["window"], 0, NQ, T2), view(k.c["near"], 0, NQ, SEQ)
        zeros = window[:, 0, 0:CTX]
        swap_keys(k, sk)
        units, done = [], []
        for kind in range(2):
            for side in ((0, 1) if layer == 0 else (1,)):
                for h in range(6):
                    c, r = h // 2, head_rows(h)
                    keys = CTX if side == 0 else T2
                    prepare, nb = None, None
                    if kind == 0:
                        q, kk, vo = nq, nk[:, c, :], h * HD
                        start, sink = BIGNUM, None
                        if side:
                            prepare, nb = (lambda h=h: near_bias(k, layer, h, near)), h % 2
                            bias = [k.NB[:, h % 2, qt * 512:(qt + 1) * 512] for qt in range(NQ)]
                    else:
                        kv = h // SWA_G
                        q, kk, vo = sq, k.SK[(kv, h % 2)], 384 + kv * HD
                        start, sink = k.negsink[:, layer * 6 + h:layer * 6 + h + 1], k.col("sink", layer * 6 + h)
                        bias = [window[:, qt, :] for qt in range(NQ)]
                    if not side:
                        bias = [zeros, zeros]
                    sc = []
                    for qt in range(NQ):
                        qs = q[r, c, side * CTX + qt * P:side * CTX + (qt + 1) * P]
                        sc.append(([(qt * 512, bias[qt], start, sink)], [(0, keys, qs, kk[r, 0:keys])]))
                    units.append(dict(prepare=prepare, scores=sc, diff=False, first=h % 2 == 0, last=h % 2 == 1, rows=r,
                                      nb=nb, v=lambda kt, vo=vo: V[:, kt, vo:vo + HD], fp32=None,
                                      to=(2 + 3 * kind + c, slice(side * CTX, (side + 1) * CTX)), tok=done))
        attend(k, units)
        k.fence()
    return [None] * DC


def swap_keys(k, sk):
    nc = k.nc
    base = sk[:, 0, :]
    other = k.SW[:, :]
    t = on(k.dve, [], nc.vector.tensor_copy, other[0:HD, :], base[HD:P, :])
    t = on(k.dve, [], nc.vector.tensor_copy, other[HD:P, :], base[0:HD, :])
    k.pe.wait(t)
    k.SK = {(0, 0): base, (1, 1): base, (0, 1): other, (1, 0): other}


def near_bias(k, layer, h, near):
    nc = k.nc
    s = k.s_bias[h % 2]
    nb = k.NB[:, h % 2, :].rearrange("p (a b) -> p a b", b=512)
    k.pool.wait(k.nb_read[h % 2])
    for row in range(SEQ // GRID_W):
        qt, r = row // 2, slice((row % 2) * GRID_W, (row % 2 + 1) * GRID_W)
        dst = nb[r, qt, CTX:T2].rearrange("p (a b) -> p a b", b=GRID_W)
        nc.gpsimd.dma_start(dst, k.io["rpb"][layer, h, 7 - row:7 - row + SEQ // GRID_W].rearrange("a c n -> c a n")).then_inc(s, 16)
    k.bias_count[h % 2] += 64
    nc.gpsimd.wait_ge(s, k.bias_count[h % 2])
    t = on(k.pool, [], nc.gpsimd.tensor_tensor, nb[:, :, CTX:T2], nb[:, :, CTX:T2], near, ALU.add)
    k.dve.wait(t)


def gla(k, scope, layer, lo, q, kT, z, V, o):
    nc = k.nc
    v1, a1 = nc.vector, nc.scalar
    NCH = T2 // CH
    scr = [k.sb(scope, f"gla{layer}_{i}", T2) for i in range(6)]
    keT_, AT_, S_ = (k.sb(scope, f"gla{layer}_{n}", *s) for n, s in
                     (("keT", (4, P)), ("A", (2, 4, P)), ("state", (NCH - 1, P))))
    ch = lambda x: x.rearrange("p (c t) -> p c t", t=CH)
    nc.tensor.wait_ge(k.s_wa2, k.wa2_loads)
    c0 = lo // CH
    for d in range(2):
        for pair in range(2):
            la, b, qi, ki, ke, e = (x[:, :] for x in scr)
            keT, AT, S = keT_[:, :, :], AT_[:, :, :, :], S_[:, :, :]
            dc = k.small[:, 80:80 + NCH]
            rows = slice(32 * d, 32 * d + RANK)
            bz = k.take("out")
            t = k.last_matmul(k.bank[bz][:, :], k.wa2[rows, pair * P:(pair + 1) * P], z[rows, 0, :], start=True, stop=True)
            bias = k.col("ba", (layer * 2 + d) * 2 + pair)
            k.read[bz] = t = on(k.act, [t], a1.activation, la, k.bank[bz][:, :], ACT.Identity, bias=bias)
            t1 = on(k.dve, [t], v1.scalar_tensor_tensor, b, la, -1.0, la, ALU.mult, ALU.min)
            t1 = on(k.act, [t1], a1.activation, b, b, ACT.Exp)
            t1 = on(k.act, [t1], a1.activation, b, b, ACT.Ln, bias=k.c["cols"][:, 2:3])
            t2 = on(k.dve, [t], v1.tensor_scalar, la, la, 0.0, None, ALU.min)
            t2 = on(k.dve, [t1, t2], v1.tensor_tensor, la, la, b, ALU.subtract)
            t = on(k.dve, [t2], v1.tensor_scalar, la, la, 1.0 / 16.0, None, ALU.mult)
            t = on(k.dve, [t], v1.tensor_tensor_scan, b, k.keep[:, 0:T2], la, 0.0, ALU.mult, ALU.add)
            bc = ch(b)
            if d == 1:
                t = on(k.dve, [t], v1.tensor_tensor, la, la, b, ALU.subtract)
                t = on(k.dve, [t], v1.tensor_tensor, ch(qi), ch(la), bc[:, :, CH - 1:CH].to_broadcast([P, NCH, CH]), ALU.add)
                t = on(k.dve, [t], v1.tensor_copy, b, qi)
            edge = slice(CH - 1, CH) if d == 0 else slice(0, 1)
            end = bc[:, :, edge].to_broadcast([P, NCH, CH])
            td = on(k.dve, [t], v1.tensor_tensor, ch(la), bc, end, ALU.subtract)
            t1 = on(k.act, [t, td], a1.activation, qi, b, ACT.Exp)
            t2 = on(k.act, [t], a1.activation, ki, b, ACT.Exp, scale=-1.0)
            t3 = on(k.act, [td], a1.activation, ke, la, ACT.Exp, scale=-1.0)
            tdc = on(k.dve, [t1], v1.tensor_copy, dc, ch(qi)[:, :, edge])
            t1 = on(k.dve, [t1, tdc], v1.tensor_tensor, qi[:, lo:T2], qi[:, lo:T2], q[:, pair, lo:T2], ALU.mult)
            t2 = on(k.dve, [t2], v1.tensor_tensor, ki, ki, kT[:, pair, :], ALU.mult)
            t3 = on(k.dve, [t3], v1.tensor_tensor, ke, ke, kT[:, pair, :], ALU.mult)
            k.fill(16)
            bt = k.take("turned")
            k.pe.wait(t3)
            for tile in range(4):
                t = k.pe.done(nc.tensor.transpose(k.bank[bt][:, tile * P:(tile + 1) * P], ke[:, tile * P:(tile + 1) * P],
                                                  k.c["ident"][:, :]))
            k.read[bt] = tk = on(k.act, [t], a1.copy, keT, k.bank[bt][:, :].rearrange("p (a f) -> p a f", f=P))
            tz = on(k.dve, [], v1.memset, AT, 0.0)
            k.pe.wait(t1, t2)
            for hh in range(2):
                r = slice(hh * HD, (hh + 1) * HD)
                b0 = k.take("score")
                for tile in range(lo // P, 4):
                    for j in range(2):
                        at = tile * P + j * CH
                        t = k.last_matmul(k.bank[b0][j * CH:(j + 1) * CH, tile * CH:(tile + 1) * CH], ki[r, at:at + CH],
                                          qi[r, at:at + CH], start=True, stop=True)
                for j in range(2):
                    s = slice(j * CH, (j + 1) * CH)
                    n = 4 - lo // P
                    mask = k.c["before" if d == 0 else "after"][s, :].bitcast(U32).unsqueeze(1).to_broadcast([CH, n, CH])
                    ta = on(k.dve, [t, tz], v1.copy_predicated, AT[s, hh, lo // P:4, j * CH:(j + 1) * CH], mask,
                            k.bank[b0][s, lo // 2:256].rearrange("p (a t) -> p a t", t=CH))
                k.read[b0] = ta
            k.pe.wait(tk)
            order = list(range(NCH)) if d == 0 else [3, 2, 1, 0, 7, 6, 5, 4]
            banks = [k.take("out"), k.take("out")]
            for c in order[:-1]:
                j, tile = c % 2, c // 2
                s = slice(j * CH, (j + 1) * CH)
                t = k.last_matmul(k.bank[banks[j]][:, tile * P:(tile + 1) * P], keT[s, tile, :],
                                  V[s, tile, pair * P:(pair + 1) * P], start=True, stop=True)
            enter = {}
            for n, c in enumerate(order[:-1]):
                j, tile = c % 2, c // 2
                add = k.bank[banks[j]][:, tile * P:(tile + 1) * P]
                if n == 0:
                    ts = on(k.dve, [t], v1.tensor_copy, S[:, n, :], add)
                else:
                    ts = on(k.dve, [t, ts], v1.scalar_tensor_tensor, S[:, n, :], S[:, n - 1, :], dc[:, c:c + 1], add,
                            ALU.mult, ALU.add)
                enter[order[n + 1]] = n
            k.read[banks[0]] = k.read[banks[1]] = ts
            k.fill(8)
            k.pe.wait(ta, ts)
            bo = k.take("turned")
            for hh in range(2):
                r = slice(hh * HD, (hh + 1) * HD)
                for tile in range(lo // P, 4):
                    k.matmul(k.bank[bo][r, tile * P:(tile + 1) * P], V[:, tile, pair * P + hh * HD:pair * P + (hh + 1) * HD],
                             AT[:, hh, tile, :], start=(tile == lo // P), stop=False, skip_group_check=True)
            for hh in range(2):
                r = slice(hh * HD, (hh + 1) * HD)
                for c in range(c0, NCH):
                    if c in enter:
                        t = k.last_matmul(k.bank[bo][r, c * CH:(c + 1) * CH], S[r, enter[c], hh * HD:(hh + 1) * HD],
                                          qi[r, c * CH:(c + 1) * CH], start=False, stop=True, skip_group_check=True)
            dst = o[:, pair, lo:T2]
            if d == 0:
                t = on(k.act, [t], a1.copy, dst, k.bank[bo][:, lo:T2])
            else:
                t = on(k.dve, [t], v1.tensor_tensor, dst, dst, k.bank[bo][:, lo:T2], ALU.add)
            k.read[bo] = t
            k.fence()

def load_stream(k, tiles):
    nc = k.nc
    stream = k.io["stream"]
    k.tiles = tiles
    assert tiles % RING == 0
    for s in range(RING):
        nc.sync.dma_start(k.ring[:, s, :], stream[s]).then_inc(k.s_tile[s], 16)
    with nc.sync.Fori(1, tiles // RING) as i:
        for s in range(RING):
            nc.sync.wait_ge(k.s_low, i * RING + (s - RING + 1))
            nc.sync.dma_start(k.ring[:, s, :], stream[bass.ds(i * RING + s, 1)].rearrange("a p n -> (a p) n")) \
                .then_inc(k.s_tile[s], 16)



def kernel(**inputs):
    import numpy as _np
    import concourse.bacc as _bacc
    from concourse import mybir as _mybir
    from concourse.bass_utils import run_bass_kernel_spmd as _run

    nc = _bacc.Bacc("TRN2", target_bir_lowering=False, num_devices=1)
    arrays, io = {}, {}

    def give(name, a):
        a = _np.ascontiguousarray(a)
        arrays["in_" + name] = a
        io[name] = nc.dram_tensor("in_" + name, a.shape, _mybir.dt.from_np(a.dtype), kind="ExternalInput").ap()

    x = {n: _np.asarray(a) for n, a in inputs.items()}
    chunked = lambda a: a.reshape(*a.shape[:-1], a.shape[-1] // P, P)
    feat = lambda a: chunked(a.reshape(-1)).T
    toks = lambda a: _np.transpose(chunked(a), (2, 1, 0))
    for n, a in CONST.items():
        give(n, a)
    rows = lambda a: _np.broadcast_to(a.reshape(1, -1), (P, a.size))
    par = {"ln1_g": feat(x["ln1_g"]), "ln1_b": feat(x["ln1_b"]), "ln2_g": feat(x["ln2_g"]), "ln2_b": feat(x["ln2_b"]),
           "ple_g": feat(x["ple_norm_g"]), "sub_g": feat(x["da_subln_g"]), "hg_g": feat(x["hg_norm_g"]),
           "lb": feat(x["hg_lb_logits"]), "norm_mix": feat(x["norm_mix_2"]), "norm_ffn": feat(x["norm_ffn_2"]),
           "final": feat(x["final_norm_2"]), "b_mod": feat(x["b_mod_2"]),
           "ba": feat(_np.stack([x["gla_ba_f_2"], x["gla_ba_b_2"]], 1)), "gla_norm": feat(x["gla_norm_2"]),
           "sink": rows(x["swa_sink_2"]), "lam": rows(x["da_lambda"]),
           "cc": _np.stack([feat(x["c_ctx_2"]), feat(x["c_2"])], 2).reshape(P, 16)}
    give("params", _np.concatenate([par[n] for n in PARAMS], 1))
    give("x", toks(x["x"][0]))
    give("ctx", toks(x["ctx_2"][0]))
    give("p", _np.stack([toks(x["p"][l, 0]) for l in range(DEPTH)]))
    wa2 = _np.zeros((DEPTH, P, GLA_W), _np.float32)
    wa2[:, 0:RANK] = x["gla_wa2_f_2"]
    wa2[:, 32:32 + RANK] = x["gla_wa2_b_2"]
    give("wa2", wa2)
    rpb = _np.zeros((DEPTH, NA_H, RPB_R, RPB_C), _np.float32)
    rpb[..., GRID_W - 16:GRID_W + 15] = x["na_rpb_2"]
    give("rpb", _np.lib.stride_tricks.sliding_window_view(rpb, GRID_W, axis=-1)[..., ::-1, :])
    W = {n: x[n] for n in ("ev_w_in", "ev_w_out", "od_w_in", "od_w_out", "ffn_w1", "ffn_w2", "ple_w_proj", "ple_w_gate",
                           "w_mod_2", "w_out_2", "w_gate_2", "w_up_2", "w_down_2")}
    w = x["w_in_2"]
    low = _np.zeros((DEPTH, D, P), _np.float32)
    low[..., 0:RANK] = w[..., 1024:1024 + RANK]
    low[..., 32:32 + RANK] = w[..., 1024 + RANK:1024 + 2 * RANK]
    W["w_in_2"] = _np.concatenate([w[..., :1024], low, w[..., 1024 + 2 * RANK:]], -1)
    n_blocks = sum(a.size for a in W.values()) // (P * P)
    tiles = -(-n_blocks // (TB * RING)) * RING
    give("stream", _np.zeros((tiles, P, TB * P), _np.float32))
    io["out"] = nc.dram_tensor("out_0", (P, DC, SEQ), _mybir.dt.float32, kind="ExternalOutput").ap()
    k = build(nc, io, tiles)
    assert len(k.blocks) == n_blocks, (len(k.blocks), n_blocks)
    stream = arrays["in_stream"]
    for i, (name, layer, kc, col) in enumerate(k.blocks):
        stream[i // TB, :, i % TB * P:(i % TB + 1) * P] = W[name][layer, kc * P:(kc + 1) * P, col * P:(col + 1) * P]
    r = _run(nc, [arrays], core_ids=[0])
    out = r.results[0]["out_0"]
    return _np.ascontiguousarray(_np.transpose(out, (2, 1, 0))).reshape(1, SEQ, D)


def build(nc, io, tiles):
    ctx = ExitStack()
    with ctx:
        k = Program(nc, ctx, io)
        load_stream(k, tiles)
        emit(k)
        for s in k.s_tile:
            nc.tensor.wait_ge(s, 16 * tiles // RING)
        nc.tensor.wait_ge(k.s_low, k.split)
    return k
```

```python
import math
from contextlib import ExitStack

import numpy as np

import concourse.bass as bass
from concourse import mybir
from concourse.alu_op_type import AluOpType as ALU

F32 = mybir.dt.float32
F32R = mybir.dt.float32r
U32 = mybir.dt.uint32
ACT = mybir.ActivationFunctionType
AX = mybir.AxisListType

P = 128
D = 1024
DC = D // P
SEQ = 256
CTX = 256
T2 = CTX + SEQ
NQ = SEQ // P
DEPTH = 2
PLE = 256
FFN = 4 * D
DFF = 2816
CH = 64
HEADS_E = 4
HEADS_O = 16
GLA_W, NA_W, SWA_W, SWA_KV = 256, 384, 384, 128
NA_H, SWA_H, SWA_G = 6, 6, 3
GRID_W = 64
RANK = 16
ALPHA = (2 * DEPTH) ** 0.25
LAM_INIT = 0.8 - 0.6 * math.exp(0.0)
EPS1, EPS2 = 1e-5, 1e-6
HD = 64
QSCALE = HD ** -0.5
NEG = -1e30
RPB_R, RPB_C = 15, 2 * GRID_W - 1

TB = 8
RING = 5
SPLIT = 4
AHEAD = 3


def consts():
    p = np.arange(P)
    out = {}
    out["ident"] = np.eye(P)
    out["meanD"] = np.full((P, P), 1.0 / D)
    out["mean128"] = np.full((P, P), 1.0 / P)
    out["mean64"] = (p[:, None] // HD == p[None, :] // HD) / HD
    def rotation(half):
        r = np.zeros((P, P))
        for m in range(P):
            base, d = m // HD * HD, m % HD
            if d < half:
                r[base + d + half, m] = -1.0
            elif d < 2 * half:
                r[base + d - half, m] = 1.0
        return r
    out["rot1"], out["rot2"] = rotation(8), rotation(32)
    t = np.arange(SEQ)
    d = p % HD
    inv1 = (np.float32(500000.0) ** (-np.arange(0, 16, 2, dtype=np.float32) / np.float32(16))).astype(np.float32)
    ang1 = (t.astype(np.float32)[:, None] * inv1[None, :]).astype(np.float32)
    rot = (d < 16)[:, None]
    out["cos1"] = np.where(rot, np.cos(ang1)[:, d % 8].T, 1.0)
    out["sin1"] = np.where(rot, np.sin(ang1)[:, d % 8].T, 0.0)
    inv2 = (np.float32(10000.0) ** (-np.arange(16, dtype=np.float32) / np.float32(16))).astype(np.float32)
    row, col = (t // GRID_W).astype(np.float32), (t % GRID_W).astype(np.float32)
    ang2 = np.concatenate([row[:, None] * inv2, col[:, None] * inv2], -1).astype(np.float32)
    out["cos2"], out["sin2"] = np.cos(ang2)[:, d % 32].T, np.sin(ang2)[:, d % 32].T
    q = (np.arange(NQ)[None, :, None] * P + p[:, None, None])
    k = np.arange(SEQ)[None, None, :]
    out["causal"] = np.where(k <= q, 0.0, NEG)
    n = ((k <= q) & (q - k <= 128)) * 1.0 + ((k <= q) & ((q - k) % 4 == 0)) + ((k <= q) & ((q - k) % 16 == 0))
    out["dilated"] = np.where(n > 0, np.log(np.maximum(n, 1)), NEG)
    swa = np.where(np.abs(q - k) <= 128, 0.0, NEG)
    out["window"] = np.concatenate([np.zeros((P, NQ, CTX)), swa], -1)
    start = np.clip(q % GRID_W - 8, 0, GRID_W - 16)
    out["near"] = np.where((k % GRID_W >= start) & (k % GRID_W < start + 16), 0.0, NEG)
    s, tt = p[:, None] % CH, np.arange(CH)[None, :]
    out["before"] = (s <= tt) * 1.0
    out["after"] = (s >= tt) * 1.0
    out["cols"] = np.tile(np.array([EPS1, EPS2, 1.0, 0.0]), (P, 1))
    return {a: np.ascontiguousarray(b.reshape(P, -1).astype(np.float32)) for a, b in out.items()}


CONST = consts()

PARAMS = {}
for _n, _w in [("ln1_g", 16), ("ln1_b", 16), ("ln2_g", 16), ("ln2_b", 16), ("ple_g", 16), ("sub_g", 1), ("hg_g", 1),
               ("lb", 8), ("norm_mix", 16), ("norm_ffn", 16), ("final", 8), ("b_mod", 96), ("ba", 8), ("gla_norm", 4),
               ("sink", 12), ("lam", 256), ("cc", 16)]:
    PARAMS[_n] = (sum(w for _, w in PARAMS.values()), _w)
NPAR = sum(w for _, w in PARAMS.values())


GLOBAL_CONSTS = ["ident", "meanD", "mean128", "mean64", "before", "after", "cols"]


class Queue:

    def __init__(self, nc, eng, sem):
        self.nc, self.eng, self.sem, self.n, self.seen = nc, eng, sem, 0, {}

    def wait(self, *tokens):
        for t in tokens:
            if t is None:
                continue
            sem, val, key = t
            if self.seen.get(key, 0) < val:
                self.eng.wait_ge(sem, val)
                self.seen[key] = val

    def done(self, ins):
        ins.then_inc(self.sem, 1)
        self.n += 1
        return (self.sem, self.n, id(self))

    def now(self):
        return (self.sem, self.n, id(self)) if self.n else None


class Program:
    def __init__(self, nc, ctx, io):
        self.nc, self.io, self.ctx = nc, io, ctx
        sb = self.sb
        sem = lambda name: ctx.enter_context(nc.semaphore(name))
        self.pe = Queue(nc, nc.tensor, sem("tensor_done"))
        self.act = Queue(nc, nc.scalar, sem("scalar_done"))
        self.dve = Queue(nc, nc.vector, sem("vector_done"))
        self.pool = Queue(nc, nc.gpsimd, sem("gpsimd_done"))
        self.s_tile = [sem(f"tile_loaded{i}") for i in range(RING)]
        self.s_high = sem("tile_high_split")
        self.s_low = sem("tile_low_split")
        self.s_free = sem("tile_used")
        self.s_x = [sem(f"x_loaded{i}") for i in range(2)]
        self.s_start = [sem(f"loaded{i}") for i in range(4)]
        self.s_bias = [sem(f"bias_loaded{i}") for i in range(2)]
        self.s_wa2 = sem("wa2_loaded")
        self.s_out = sem("stored")
        self.ring = sb(ctx, "ring", RING, TB * P)
        self.high = sb(ctx, "high", SPLIT, TB * P, dt=F32R)
        self.low = sb(ctx, "low", SPLIT, TB * P, dt=F32R)
        self.X = sb(ctx, "X", DC, T2)
        self.XH = sb(ctx, "XH", DC, T2, dt=F32R)
        self.XL = sb(ctx, "XL", DC, T2, dt=F32R)
        self.SQ = sb(ctx, "SQ", 2, 512)
        self.RS = sb(ctx, "RS", 2, 512)
        self.TMP = sb(ctx, "TMP", 4 * SEQ)
        self.par = sb(ctx, "par", NPAR)
        self.wa2 = sb(ctx, "wa2", 256)
        self.mod = sb(ctx, "mod", 2, 48, 2)
        self.gs = sb(ctx, "gs", 16)
        self.small = sb(ctx, "small", 112)
        self.keep = sb(ctx, "keep", 512)
        self.c = {}
        for name in GLOBAL_CONSTS:
            self.c[name] = sb(ctx, "c_" + name, CONST[name].shape[1])
        self.bank = [ctx.enter_context(nc.psum_tensor(f"bank{i}", [P, 512], F32)) for i in range(8)]
        self.read = [None] * 8
        self.turn = {"gemm": 0, "score": 0, "turned": 0, "out": 0}
        self.first = {"gemm": 0, "score": 2, "turned": 4, "out": 6}
        self.blocks = []
        self.tile_seen, self.split, self.freed = -1, 0, 0
        self.sq_read, self.rs_read, self.pt_read, self.T_read = [None] * 2, [None] * 2, [None] * 2, [None] * 3
        self.tmp_read, self.xh_read = [None] * 4, None
        self.nb_read, self.bias_count = [None, None], [0, 0]
        self.turn_tmp = self.turn_PT = self.turn_sq = 0
        self.sq_owner = [None] * 2
        self.fillers, self.output = [], None
        self.n_loads = [0] * 4

    def sb(self, ctx, name, *shape, dt=F32):
        return ctx.enter_context(self.nc.sbuf_tensor(name, [P, *shape], dt))

    def load_consts(self, ctx, names, s, waits=()):
        self.pool.wait(*waits)
        for name in names:
            self.c[name] = self.sb(ctx, f"c{s}_{name}", CONST[name].shape[1])
            self.nc.gpsimd.dma_start(self.c[name][:, :], self.io[name]).then_inc(self.s_start[s], 16)
            self.n_loads[s] += 16
        self.const_waits = {id(q): (self.s_start[s], self.n_loads[s]) for q in (self.pe, self.dve, self.pool)}

    def need_consts(self, *queues):
        for q in queues or (self.pe, self.dve, self.pool):
            if id(q) in self.const_waits:
                q.eng.wait_ge(*self.const_waits.pop(id(q)))

    def fill(self, us, of=None):
        while self.fillers and us > 0 and (of is None or self.fillers[0] in of):
            try:
                us -= next(self.fillers[0])
            except StopIteration:
                self.fillers.pop(0)

    def finish(self, filler):
        while filler in self.fillers:
            self.fill(0.01)

    def scratch(self, n):
        w = n // SEQ
        self.turn_tmp = (self.turn_tmp + w - 1) // w * w
        parts = [(self.turn_tmp + j) % 4 for j in range(w)]
        self.turn_tmp += w

        def read(token):
            for part in parts:
                self.tmp_read[part] = token

        return self.TMP[:, parts[0] * SEQ:parts[0] * SEQ + n], [self.tmp_read[part] for part in parts], read

    def col(self, name, i=0, n=1):
        o, w = PARAMS[name]
        return self.par[:, o + i:o + i + n]

    def take(self, pool):
        b = self.first[pool] + self.turn[pool] % 2
        self.turn[pool] += 1
        self.pe.wait(self.read[b])
        self.read[b] = None
        return b

    def split_tile(self, t):
        nc, r, o = self.nc, t % RING, t % SPLIT
        raw, high, low = self.ring[:, r, :], self.high[:, o, :], self.low[:, o, :]
        nc.scalar.wait_ge(self.s_tile[r], 16 * (t // RING + 1))
        if t >= SPLIT:
            nc.scalar.wait_ge(self.s_free, t - SPLIT + 1)
        nc.scalar.copy(high, raw).then_inc(self.s_high, 1)
        nc.vector.wait_ge(self.s_high, t + 1)
        nc.vector.tensor_tensor(low, raw, high.bitcast(F32), ALU.subtract).then_inc(self.s_low, 1)

    def weights(self, requests):
        at = len(self.blocks)
        self.blocks += requests
        tile, o = at // TB, at % TB
        assert o + len(requests) <= TB
        while self.split <= min(tile + AHEAD, self.tiles - 1) and self.freed >= self.split - SPLIT + 1:
            self.split_tile(self.split)
            self.split += 1
        assert self.split > tile
        if tile > self.tile_seen:
            self.nc.tensor.wait_ge(self.s_low, tile + 1)
            self.tile_seen = tile
        s = slice(o * P, (o + len(requests)) * P)
        return self.high[:, tile % SPLIT, s], self.low[:, tile % SPLIT, s]

    def matmul(self, *a, hold=False, **kw):
        mm = self.nc.tensor.matmul(*a, **kw)
        done = len(self.blocks) // TB if not hold else (len(self.blocks) - 1) // TB
        if self.freed < done:
            mm.then_inc(self.s_free, 1)
            self.freed += 1
        return mm

    def last_matmul(self, *a, **kw):
        return self.pe.done(self.nc.tensor.matmul(*a, **kw))

    def product(self, out, name, layer, col, ks, moving):
        return self.products([out], [(name, layer, col)], ks, moving)[0]

    def products(self, outs, columns, ks, moving):
        n, tokens = len(ks), []
        for i, c in enumerate(ks):
            for out, (name, layer, col) in zip(outs, columns):
                wh, wl = self.weights([(name, layer, c, col)])
                xh, xl = moving(c)
                self.matmul(out, wh, xh, hold=True, start=(i == 0), stop=False)
                self.matmul(out, wh, xl, hold=True, start=False, stop=False)
                if i < n - 1:
                    self.matmul(out, wl, xh, start=False, stop=False)
                else:
                    tokens.append(self.last_matmul(out, wl, xh, start=False, stop=True))
        return tokens

    def rows_product(self, outs, name, layer, cols, kc, stationary):
        tok = None
        for k in range(kc):
            wh, wl = self.weights([(name, layer, k, c) for c in cols])
            for i, out in enumerate(outs):
                xh, xl = stationary(k, i)
                self.matmul(out, xh, wh, hold=True, start=(k == 0), stop=False)
                self.matmul(out, xl, wh, hold=True, start=False, stop=False)
                if k == kc - 1:
                    tok = self.last_matmul(out, xh, wl, start=False, stop=True)
                else:
                    self.matmul(out, xh, wl, hold=(i < len(outs) - 1), start=False, stop=False)
        return tok


def on(q, waits, fn, *a, **kw):
    q.wait(*waits)
    return q.done(fn(*a, **kw))


SEQS = slice(CTX, T2)
LNEXP = "natural_log_exp_and_others"


def emit(k):
    nc = k.nc
    load_inputs(k)
    with ExitStack() as scope:
        cs, rows = k.sb(scope, "conditions", DC, P, dt=F32R), k.sb(scope, "mod_rows", 2, 512)
        first, second = (modulations(k, layer, cs, rows) for layer in range(DEPTH))
        k.fillers = [first, context_norm(k), second]
        mean = first_block(k, cs)
        k.finish(second)
    second_block(k, mean)


def load_inputs(k):
    nc = k.nc
    for q in (k.act, k.dve):
        q.eng.wait_ge(k.s_x[0], 16)
    k.x_toks = [split_x(k, i, []) for i in range(DC // 2)]
    for q in (k.act, k.dve):
        q.eng.wait_ge(k.s_x[1], 16)
    k.x_toks += [split_x(k, i, []) for i in range(DC // 2, DC)]


def prepare_constants(k):
    nc = k.nc
    for q in (k.pe, k.act, k.dve, k.pool):
        q.eng.wait_ge(k.s_start[0], k.n_loads[0])
    t = on(k.dve, [], nc.vector.memset, k.keep[:, :], 1.0)
    on(k.dve, [t], nc.vector.memset, k.keep[:, :].rearrange("p (c t) -> p c t", t=CH)[:, :, 0:1], 0.0)
    k.negsink = k.small[:, 100:112]
    on(k.dve, [], nc.vector.tensor_scalar, k.negsink, k.col("sink", 0, 12), -1.0, None, ALU.mult)


def split(k, src, waits, high, low):
    nc = k.nc
    th = on(k.act, [*waits, k.xh_read], nc.scalar.copy, high, src)
    return on(k.dve, [*waits, th], nc.vector.tensor_tensor, low, src, high.bitcast(F32), ALU.subtract)


def split_x(k, i, waits):
    return split(k, k.X[:, i, SEQS], waits, k.XH[:, i, SEQS], k.XL[:, i, SEQS])


def moving_x(k, toks, s=SEQS):
    def get(c):
        k.pe.wait(toks[c] if isinstance(toks, list) else toks)
        return k.XH[:, c, s], k.XL[:, c, s]
    return get


def rows_x(k, toks):
    def get(c, tile):
        k.pe.wait(toks[c] if isinstance(toks, list) else toks)
        s = slice(tile * P, (tile + 1) * P)
        return k.XH[:, c, s], k.XL[:, c, s]
    return get



class Mean:

    def __init__(self, k, n, stat, count=DC, square=True, pool="out"):
        self.k, self.n, self.stat, self.square, self.count = k, n, stat, square, count
        self.bank, self.added, self.summed, self.waiting = k.take(pool), 0, 0, None
        self.token = None

    def add(self, x, tok):
        k = self.k
        if self.square:
            j = k.turn_sq % 2
            k.turn_sq += 1
            if k.sq_owner[j] is not None:
                k.sq_owner[j].flush()
            k.sq_owner[j] = self
            sq = k.SQ[:, j, 0:self.n]
            tok = on(k.act, [tok, k.sq_read[j]], k.nc.scalar.activation, sq if len(x.shape) == 2 else
                     sq.rearrange("p (a t) -> p a t", t=SEQ), x, ACT.Square)
            x = sq
            self.flush()
            self.waiting = (x, tok, j)
        else:
            self.flush()
            self.waiting = (x, tok, None)

    def flush(self):
        k = self.k
        if self.waiting is None:
            return
        x, tok, j = self.waiting
        self.waiting = None
        k.pe.wait(tok)
        self.token = k.last_matmul(k.bank[self.bank][:, 0:self.n], self.stat, x, start=(self.summed == 0),
                                   stop=(self.summed == self.count - 1))
        self.summed += 1
        if j is not None:
            k.sq_read[j] = self.token

    def end(self):
        self.flush()
        assert self.summed == self.count
        return self.bank, self.token


class SlowMean:

    def __init__(self, k, n, stat, square=True, r=0):
        self.k, self.n, self.stat, self.square = k, n, stat, square
        self.sum, self.r, self.first, self.token, self.added = k.RS[:, r, 0:n], r, None, None, 0

    def add(self, x, tok):
        k, nc = self.k, self.k.nc
        free = k.rs_read[self.r]
        if self.square and self.added == 0:
            self.token = on(k.act, [tok, free], nc.scalar.activation, self.sum, x, ACT.Square)
        elif self.square:
            j = k.turn_sq % 2
            k.turn_sq += 1
            if k.sq_owner[j] is not None:
                k.sq_owner[j].flush()
                k.sq_owner[j] = None
            sq = k.SQ[:, j, 0:self.n]
            t = on(k.act, [tok, k.sq_read[j]], nc.scalar.activation, sq, x, ACT.Square)
            k.sq_read[j] = self.token = on(k.dve, [t, self.token], nc.vector.tensor_tensor, self.sum, self.sum, sq,
                                           ALU.add)
        elif self.added == 0:
            self.first = (x, tok)
        elif self.added == 1:
            self.token = on(k.dve, [self.first[1], tok, free], nc.vector.tensor_tensor, self.sum, self.first[0], x,
                            ALU.add)
        else:
            self.token = on(k.dve, [tok, self.token], nc.vector.tensor_tensor, self.sum, self.sum, x, ALU.add)
        self.added += 1

    def end(self):
        k = self.k
        b = k.take("out")
        k.pe.wait(self.token)
        return b, k.last_matmul(k.bank[b][:, 0:self.n], self.stat, self.sum, start=True, stop=True)


def rsqrt_of(k, mean, eps_col, r=0):
    nc = k.nc
    b, t = mean.end()
    rs = k.RS[:, r, 0:mean.n]
    k.read[b] = t = on(k.act, [t, k.rs_read[r]], nc.scalar.activation, rs, k.bank[b][:, 0:mean.n], ACT.Ln,
                       bias=k.c["cols"][:, eps_col:eps_col + 1])
    return on(k.act, [t], nc.scalar.activation, rs, rs, ACT.Exp, scale=-0.5)


def layer_norm(k, g, b, layer, mean):
    nc = k.nc
    bank, t = mean.end()
    k.fill(1)
    squares = Mean(k, SEQ, k.c["meanD"][:, :])
    for i in range(DC // 2):
        xs = k.X[:, 2 * i:2 * i + 2, SEQS]
        m = k.bank[bank][:, 0:SEQ].unsqueeze(1).to_broadcast([P, 2, SEQ])
        k.read[bank] = tc = on(k.dve, [t], nc.vector.tensor_tensor, xs, xs, m, ALU.subtract)
        squares.add(k.X[:, 2 * i, SEQS], tc)
        squares.add(k.X[:, 2 * i + 1, SEQS], tc)
    t = rsqrt_of(k, squares, 0)
    k.fill(5)
    out = []
    started = []

    def finish_chunk():
        i, x, bias, ts = started.pop(0)
        xh, xl = k.XH[:, i, SEQS], k.XL[:, i, SEQS]
        th = on(k.act, [ts, k.xh_read], nc.scalar.activation, xh, x, ACT.Identity, bias=bias)
        tl = on(k.dve, [th], nc.vector.scalar_tensor_tensor, xl, x, bias, xh.bitcast(F32), ALU.add, ALU.subtract)
        k.x_ready[i] = on(k.pool, [tl], nc.gpsimd.tensor_scalar, x, x, bias, None, ALU.add)
        out.append(tl)

    for i in range(DC):
        x = k.X[:, i, SEQS]
        ts = on(k.dve, [t], nc.vector.scalar_tensor_tensor, x, x, k.col(g, layer * DC + i), k.RS[:, 0, 0:SEQ],
                ALU.mult, ALU.mult)
        if len(started) == 2:
            finish_chunk()
        started.append((i, x, k.col(b, layer * DC + i), ts))
    while started:
        finish_chunk()
    k.rs_read[0] = ts
    return out


def rms_heads(k, o, stat, g, gates, eps_col, toks, high, low, between=None):
    nc = k.nc
    means, out = [], []
    for x, t in zip(o, toks):
        means.append(Mean(k, math.prod(x.shape[1:]), stat, count=1))
        means[-1].add(x, t)
    means[-1].flush()
    ready = [rsqrt_of(k, m, eps_col, i) for i, m in enumerate(means)]
    if between is None:
        k.fill(4)
    else:
        between()
    for i, x in enumerate(o):
        rs = k.RS[:, i, 0:means[i].n]
        if len(x.shape) == 3:
            rs = rs.rearrange("p (a t) -> p a t", t=SEQ)
        t = on(k.dve, [ready[i]], nc.vector.scalar_tensor_tensor, x, x, g(i), rs, ALU.mult, ALU.mult)
        k.rs_read[i] = t
        if gates is not None:
            t = on(k.dve, [t], nc.vector.tensor_tensor, x, x, gates[i], ALU.mult)
        out.append(split(k, x, [t], high[i], low[i]))
    return out



def rope(k, dst, rot, tok):
    nc = k.nc
    k.need_consts()
    b = k.take("gemm")
    k.pe.wait(tok)
    t = k.last_matmul(k.bank[b][:, 0:SEQ], rot[0], dst, start=True, stop=True)
    tmp, free, read = k.scratch(SEQ)
    t1 = on(k.dve, [t, *free], nc.vector.tensor_tensor, tmp, k.bank[b][:, 0:SEQ], rot[2], ALU.mult)
    k.read[b] = t1
    t2 = on(k.dve, [t], nc.vector.tensor_tensor, dst, dst, rot[1], ALU.mult)
    t = on(k.dve, [t1, t2], nc.vector.tensor_tensor, dst, dst, tmp, ALU.add)
    read(t)
    return t



def turn(k, blocks, PTi, toks, copy_on):
    nc = k.nc
    k.pe.wait(*toks)
    out = []
    for pair in sorted({kt // 2 for kt, _, _ in blocks}):
        b = k.take("turned")
        mine = [x for x in blocks if x[0] // 2 == pair]
        for kt, qt, src in mine:
            o = (kt % 2) * SEQ + qt * P
            t_turned = k.pe.done(nc.tensor.transpose(k.bank[b][:, o:o + P], src, k.c["ident"][:, :]))
        have = {kt: min(q for a, q, _ in mine if a == kt) * P for kt, _, _ in mine}
        runs = [(min(have), 0, len(have) * SEQ)] if not any(have.values()) else \
            [(kt, q0, SEQ - q0) for kt, q0 in have.items()]
        q, copy = (k.act, nc.scalar.copy) if (pair + copy_on) % 2 == 0 else (k.dve, nc.vector.tensor_copy)
        for kt, q0, n in runs:
            at = (kt % 2) * SEQ + q0
            t = on(q, [t_turned, k.pt_read[PTi]], copy, k.PT[:, PTi, kt * SEQ + q0:kt * SEQ + q0 + n],
                   k.bank[b][:, at:at + n])
        out.append(t)
        k.read[b] = t
    return out, t_turned


def attend(k, units, fill=0.0, of=None):
    n = len(units)
    for step in range(n + 2):
        if step < n:
            scores_of(k, units[step], step)
        if 1 <= step <= n:
            normalise(k, units[step - 1])
        if step < n:
            exponentials(k, units[step])
        store_output(k)
        k.fill(fill, of)
        if 1 <= step <= n:
            transposes_of(k, units[step - 1])
        if step >= 2:
            values_of(k, units[step - 2])
    store_output(k)


def scores_of(k, u, i):
    nc = k.nc
    u["T"] = i % 3
    c = 16 * (i % 3)
    u["nm"], u["den"], u["rd"], u["es"] = (k.small[:, c + 4 * j:c + 4 * j + 4] for j in range(4))
    if u["prepare"] is not None:
        k.pe.wait(*(u["prepare"]() or []))
    u["done"] = []
    for bank_cols, parts in u["scores"]:
        b = k.take("score")
        for (o, n, q, kk) in parts:
            t = k.last_matmul(k.bank[b][:, o:o + n], q, kk, start=(o == 0), stop=True, skip_group_check=True)
        u["done"].append((b, t))


def exponentials(k, u):
    nc = k.nc
    T = k.Tt[:, u["T"], :]
    k.dve.wait(k.T_read[u["T"]])
    if u.get("nb") is not None:
        k.dve.wait(k.nb_ready[u["nb"]])
    rows, j = [], 0
    for (bank_cols, parts), (b, t) in zip(u["scores"], u["done"]):
        for (o, n, _, _), (To, bias, start, sink) in zip(parts, bank_cols):
            t_max = on(k.dve, [t], nc.vector.tensor_tensor_reduce, T[:, To:To + n], k.bank[b][:, o:o + n], bias, -1.0,
                       start, ALU.add, ALU.min, u["nm"][:, j:j + 1])
            rows.append((To, n, j, t_max))
            j += 1
        k.read[b] = t_max
    if u.get("nb") is not None:
        k.nb_read[u["nb"]] = t_max
    for To, n, j, t_max in rows:
        u["exp"] = on(k.act, [t_max], nc.scalar.activation, T[:, To:To + n], T[:, To:To + n], ACT.Exp,
                      bias=u["nm"][:, j:j + 1], scale=-1.0, accum_out=u["den"][:, j:j + 1])
    u["sink"] = sink
    if sink is not None:
        u["exp"] = on(k.act, [t_max], nc.scalar.activation, u["es"][:, 0:j + 1], u["nm"][:, 0:j + 1], ACT.Exp,
                      bias=sink)
    u["rows"] = rows


def normalise(k, u):
    nc = k.nc
    T, rows, rd = k.Tt[:, u["T"], :], u["rows"], u["rd"]
    n_rows, t = len(rows), u["exp"]
    if u["sink"] is not None:
        t = on(k.dve, [t], nc.vector.tensor_tensor, u["den"][:, 0:n_rows], u["den"][:, 0:n_rows], u["es"][:, 0:n_rows],
               ALU.add)
    t = on(k.dve, [t], nc.vector.reciprocal, rd[:, 0:n_rows], u["den"][:, 0:n_rows])
    first = rows[:len(rows) // 2] if u["diff"] else rows
    scaled = [on(k.dve, [t], nc.vector.tensor_scalar, T[:, To:To + n], T[:, To:To + n], rd[:, j:j + 1], None, ALU.mult)
              for To, n, j, _ in first]
    if u["diff"]:
        h = len(first)
        t = on(k.dve, [t], nc.vector.tensor_scalar, rd[:, h:2 * h], rd[:, h:2 * h], k.neglam, None, ALU.mult)
        scaled = [on(k.dve, [t, ts], nc.vector.scalar_tensor_tensor, T[:, To:To + n], T[:, To1:To1 + n],
                     rd[:, j1:j1 + 1], T[:, To:To + n], ALU.mult, ALU.add)
                  for (To, n, _, _), (To1, _, j1, _), ts in zip(first, rows[h:], scaled)]
    u["scaled"] = scaled
    u["blocks"] = [(kt, qt, T[:, To + kt * P:To + (kt + 1) * P])
                   for qt, (To, n, _, _) in enumerate(first) for kt in range(n // P)]


def transposes_of(k, u):
    u["PT"] = k.turn_PT % 2
    k.turn_PT += 1
    u["copied"], k.T_read[u["T"]] = turn(k, u["blocks"], u["PT"], u["scaled"], k.turn_PT)


def values_of(k, u):
    nc = k.nc
    PT = k.PT[:, u["PT"], :].rearrange("p (a q) -> p a q", q=SEQ)
    if u["first"]:
        k.obank = k.take("out")
    out = k.bank[k.obank][u["at"], 0:SEQ]
    k.pe.wait(*u["copied"])
    keys = max(kt for kt, _, _ in u["blocks"]) + 1
    for kt in range(keys):
        q0 = min(q for a, q, _ in u["blocks"] if a == kt) * P
        args = (out[:, q0:SEQ], u["v"](kt), PT[:, kt, q0:SEQ])
        kw = dict(start=(kt == 0), stop=(kt == keys - 1))
        if kt < keys - 1:
            k.matmul(*args, **kw)
        else:
            t = k.last_matmul(*args, **kw)
    k.pt_read[u["PT"]] = t
    if u["last"]:
        k.output = (u, k.obank, t)


def store_output(k):
    if k.output is None:
        return
    u, b, t = k.output
    k.output = None
    u["tok"].append(u["store"](k.bank[b][:, 0:SEQ], t))
    k.read[b] = u["tok"][-1]


BIGNUM = 3.0e38


def view(buf, a, b):
    return buf[:, :].rearrange("p (a b) -> p a b", a=a, b=b)


def projections(k, name, layer, plan, toks, early=False):
    nc = k.nc
    rotate = None
    for first, *entry in plan:
        if first is None:
            value_rows(k, name, layer, *entry, toks)
            yield 2.6 * len(entry[0]) / 2 * len(entry[-1]) / 2
            continue
        dsts, s, scale, func, rot, part = entry
        n, done = s.stop - s.start, 0
        while done < len(dsts):
            group = range(done, min(done + (2 if early else 1), len(dsts)))
            early, done = False, group.stop
            banks = [k.take("gemm") for _ in group]
            toks_out = k.products([k.bank[b][:, 0:n] for b in banks], [(name, layer, first + i) for i in group],
                                  range(DC), moving_x(k, toks, s))
            for i, b, t in zip(group, banks, toks_out):
                dst = dsts[i]
                k.read[b] = t = on(k.act, [t], nc.scalar.activation, dst, k.bank[b][:, 0:n], func, scale=scale)
                if rotate is not None:
                    rope(k, *rotate)
                rotate = (part(dst), rot, t) if rot is not None else None
            yield 2.6 * n / 256 * len(group)
    if rotate is not None:
        rope(k, *rotate)
        yield 0.4


def scope_end(k):
    marks = [q.now() for q in (k.pe, k.act, k.dve, k.pool)]
    for q in (k.act, k.dve, k.pool):
        q.wait(*marks)
    k.scope_marks = marks


def first_block(k, cs):
    nc = k.nc
    k.x_ready = [None] * DC
    toks = k.x_toks
    for layer in range(DEPTH):
        if layer == 0:
            mean = even_mixer(k, toks, cs)
        else:
            mean = odd_mixer(k, toks)
        toks = layer_norm(k, "ln1_g", "ln1_b", layer, mean)
        mean = ffn1(k, layer, toks)
        with ExitStack() as scope:
            embedding, e = per_layer_embedding(k, scope, layer)
            toks = layer_norm(k, "ln2_g", "ln2_b", layer, mean)
            k.finish(embedding)
            toks, mean = add_embedding(k, scope, layer, e, toks)
            scope_end(k)
    return mean


def ffn1(k, layer, toks):
    nc = k.nc
    half = FFN // P // 2
    with ExitStack() as scope:
        hh, hl = (k.sb(scope, f"hidden_{n}{layer}", half, SEQ, dt=F32R) for n in ("high", "low"))
        hid_read = None
        for part in range(2):
            th = []
            products = []
            for i in range(half):
                if not products:
                    group = [i, i + 1] if (part, i) == (0, 0) else [i]
                    banks = [k.take("gemm") for _ in group]
                    products = list(zip(banks, k.products([k.bank[b][:, 0:SEQ] for b in banks],
                                                          [("ffn_w1", layer, part * half + j) for j in group],
                                                          range(DC), moving_x(k, toks))))
                b, t = products.pop(0)
                sq, free, read = k.scratch(SEQ)
                t1 = on(k.act, [t, *free], nc.scalar.activation, sq, k.bank[b][:, 0:SEQ], ACT.Relu)
                k.read[b] = t1
                t2 = on(k.dve, [t1], nc.vector.tensor_tensor, sq, sq, sq, ALU.mult)
                t3 = on(k.act, [t2, hid_read], nc.scalar.copy, hh[:, i, :], sq)
                t4 = on(k.dve, [t3], nc.vector.tensor_tensor, hl[:, i, :], sq, hh[:, i, :].bitcast(F32), ALU.subtract)
                read(t4)
                th.append(t4)

            def moving(c):
                k.pe.wait(th[c - part * half])
                return hh[:, c - part * half, :], hl[:, c - part * half, :]

            mean = SlowMean(k, SEQ, k.c["meanD"][:, :], square=False) if part == 1 else None
            residual(k, "ffn_w2", layer, moving, range(part * half, (part + 1) * half), ALPHA if part == 0 else 1.0,
                     mean)
            hid_read = k.pe.now()
        k.xh_read = hid_read
        scope_end(k)
    return mean


def residual(k, name, layer, moving, ks, alpha, mean):
    nc = k.nc
    for i in range(DC):
        b = k.take("gemm")
        t = k.product(k.bank[b][:, 0:SEQ], name, layer, i, ks, moving)
        x = k.X[:, i, SEQS]
        t = on(k.dve, [t, k.x_ready[i]], nc.vector.scalar_tensor_tensor, x, x, alpha, k.bank[b][:, 0:SEQ],
               ALU.mult, ALU.add)
        k.read[b] = k.x_ready[i] = t
        if mean is not None:
            mean.add(x, t)


def per_layer_embedding(k, scope, layer):
    pT = k.sb(scope, f"pT{layer}", PLE // P, SEQ)
    ph, pl = (k.sb(scope, f"p_{n}{layer}", PLE // P, SEQ, dt=F32R) for n in ("high", "low"))
    e = k.sb(scope, f"e{layer}", DC, SEQ)
    k.pool.wait(*k.scope_marks)
    k.nc.gpsimd.dma_start(pT[:, :, :], k.io["p"][layer]).then_inc(k.s_start[1], 16)
    filler = embedding(k, layer, pT, ph, pl, e)
    k.fillers.insert(0, filler)
    return filler, e


def embedding(k, layer, pT, ph, pl, e):
    nc = k.nc
    for q in (k.act, k.dve):
        q.eng.wait_ge(k.s_start[1], 16 * (layer + 1))
    tp = [split(k, pT[:, i, :], [], ph[:, i, :], pl[:, i, :]) for i in range(PLE // P)]

    def moving(c):
        k.pe.wait(tp[c])
        return ph[:, c, :], pl[:, c, :]

    mean = SlowMean(k, SEQ, k.c["meanD"][:, :], r=1)
    for i in range(DC):
        b = k.take("gemm")
        t = k.product(k.bank[b][:, 0:SEQ], "ple_w_proj", layer, i, range(PLE // P), moving)
        k.read[b] = t = on(k.act, [t], nc.scalar.copy, e[:, i, :], k.bank[b][:, 0:SEQ])
        mean.add(e[:, i, :], t)
        yield 1.1
    t = rsqrt_of(k, mean, 0, 1)
    for i in range(DC):
        k.rs_read[1] = on(k.dve, [t], nc.vector.scalar_tensor_tensor, e[:, i, :], e[:, i, :],
                          k.col("ple_g", layer * DC + i), k.RS[:, 1, 0:SEQ], ALU.mult, ALU.mult)


def add_embedding(k, scope, layer, e, toks):
    nc = k.nc
    gate = k.sb(scope, f"gate{layer}", DC, SEQ)
    gates = []
    for i in range(DC):
        b = k.take("gemm")
        t = k.product(k.bank[b][:, 0:SEQ], "ple_w_gate", layer, i, range(DC), moving_x(k, toks))
        g = gate[:, i, :]
        k.read[b] = t = on(k.act, [t], nc.scalar.activation, g, k.bank[b][:, 0:SEQ], ACT.Sigmoid)
        t = on(k.dve, [t, k.rs_read[1]], nc.vector.tensor_tensor, g, g, e[:, i, :], ALU.mult)
        gates.append(on(k.dve, [t, k.x_ready[i]], nc.vector.tensor_tensor, g, g, k.X[:, i, SEQS], ALU.add))
    k.xh_read = k.pe.now()
    nc.scalar.preload_act_table_set(LNEXP)
    out = []
    mean = Mean(k, SEQ, k.c["meanD"][:, :]) if layer == DEPTH - 1 else None
    for i in range(DC):
        x = k.X[:, i, SEQS]
        k.x_ready[i] = tx = on(k.pool, [gates[i]], nc.gpsimd.tensor_copy, x, gate[:, i, :])
        if mean is None:
            out.append(split(k, gate[:, i, :], [gates[i]], k.XH[:, i, SEQS], k.XL[:, i, SEQS]))
        else:
            mean.add(gate[:, i, :], gates[i])
    if mean is not None:
        mean.flush()
    return out, mean


def head_rows(h):
    return slice(HD * (h % 2), HD * (h % 2) + HD)


def even_mixer(k, toks, cs):
    nc = k.nc
    with ExitStack() as scope:
        sb = lambda n, *shape: k.sb(scope, "even_" + n, *shape)
        qT, kT, V = sb("q", 4, SEQ), sb("k", 4, SEQ), sb("v", NQ, 512)
        hq, hf, hg, HV = sb("hq", 4, SEQ), sb("hf", 4, SEQ), sb("hg", 4, SEQ), sb("hv", NQ, 512)
        k.load_consts(scope, ["causal", "cos1", "sin1", "rot1"], 2)
        c = k.small[:, 48:56]
        g = c[:, 5:6]
        rot = (k.c["rot1"][:, :], k.c["cos1"][:, :], k.c["sin1"][:, :])
        chunks = lambda buf: [buf[:, i, :] for i in range(4)]
        whole = lambda dst: dst
        n = 0
        for _ in projections(k, "ev_w_in", 0, [(0, chunks(qT), SEQS, QSCALE, ACT.Copy, rot, whole),
                                               (4, chunks(kT), SEQS, 1.0, ACT.Copy, rot, whole),
                                               (None, [8, 9, 10, 11], V, 0, range(2, 4))], toks, early=True):
            if n == 0:
                prepare_constants(k)
                split_conditions(k, cs)
            n += 1
        rest = projections(k, "ev_w_in", 0, [(12, chunks(hq), SEQS, 1.0, ACT.Copy, None, None),
                                             (24, chunks(hg), SEQS, 1.0, ACT.Copy, None, None),
                                             (16, chunks(hf), SEQS, 1.0, ACT.Copy, None, None),
                                             (None, [20, 21, 22, 23], HV, 0, range(2, 4))], toks)
        k.fillers.insert(0, rest)
        lp = k.col("lam", 0, 256)
        t0 = on(k.dve, [], nc.vector.tensor_tensor_reduce, lp[:, 0:64], lp[:, 0:64], lp[:, 64:128], 1.0, 0.0, ALU.mult,
                ALU.add, c[:, 0:1])
        t1 = on(k.dve, [], nc.vector.tensor_tensor_reduce, lp[:, 128:192], lp[:, 128:192], lp[:, 192:256], 1.0, 0.0,
                ALU.mult, ALU.add, c[:, 1:2])
        t = on(k.act, [t0, t1], nc.scalar.activation, c[:, 2:4], c[:, 0:2], ACT.Exp)
        t = on(k.dve, [t], nc.vector.tensor_tensor, c[:, 4:5], c[:, 3:4], c[:, 2:3], ALU.subtract)
        k.neglam = c[:, 4:5]
        t = on(k.dve, [t], nc.vector.tensor_scalar, k.neglam, k.neglam, -LAM_INIT, None, ALU.add)
        t_g = on(k.dve, [], nc.vector.tensor_scalar, g, k.col("sub_g"), 1.0 - LAM_INIT, None, ALU.mult)
        k.dve.wait(t_g)
        k.pe.wait(k.dve.now(), k.act.now())
        with ExitStack() as inner:
            attention_buffers(k, inner, "da")
            o = k.sb(inner, "da_o", HEADS_E, SEQ)
            causal = view(k.c["causal"], NQ, SEQ)
            units, done = [], []
            for h in range(HEADS_E):
                sc = []
                for comp in range(2):
                    r = slice(HD * comp, HD * comp + HD)
                    parts = [(qt * SEQ, (qt + 1) * P, qT[r, h, qt * P:(qt + 1) * P], kT[r, h, 0:(qt + 1) * P])
                             for qt in range(NQ)]
                    bank_cols = [(comp * 512 + qt * SEQ, causal[:, qt, 0:(qt + 1) * P], BIGNUM, None)
                                 for qt in range(NQ)]
                    sc.append((bank_cols, parts))
                units.append(dict(prepare=None, scores=sc, diff=True, first=True, last=True, at=slice(0, P),
                                  v=lambda kt, h=h: V[:, kt, h * P:(h + 1) * P], tok=done,
                                  store=lambda bank, t, h=h: on(k.act, [t], nc.scalar.copy, o[:, h, :], bank)))
            attend(k, units, 7.0, [rest])
            k.finish(rest)
            k.xh_read = k.pe.now()
            flat = lambda buf: buf[:, :, :].rearrange("p h t -> p (h t)")
            lb, oml = k.small[:, 56:60], k.small[:, 60:64]
            t = on(k.dve, [], nc.vector.tensor_tensor, lb, k.col("lb", 0, 4), k.col("lb", 4, 4), ALU.subtract)
            on(k.act, [], nc.scalar.activation, flat(hq), flat(hq), ACT.Silu)
            on(k.act, [], nc.scalar.activation, flat(hg), flat(hg), ACT.Silu)
            t = on(k.act, [t], nc.scalar.activation, lb, lb, ACT.Sigmoid)
            t_f = on(k.act, [], nc.scalar.activation, flat(hf), flat(hf), ACT.Sigmoid)
            t = on(k.dve, [t], nc.vector.tensor_scalar, oml, lb, -1.0, 1.0, ALU.mult, ALU.add)
            nc.scalar.preload_act_table_set(LNEXP)
            k.dve.wait(t, t_f)
            pairs = [slice(0, 2), slice(2, 4)]
            mixed = rms_heads(k, [o[:, s, :] for s in pairs], k.c["mean128"][:, :], lambda i: g, None, 0,
                              [done[1], done[3]], [k.XH[:, s, SEQS] for s in pairs], [k.XL[:, s, SEQS] for s in pairs])
            scope_end(k)
        with ExitStack() as inner:
            mixed += hgrn2(k, inner, hq, hf, hg, HV, lb, oml)
            scope_end(k)
        mean = SlowMean(k, SEQ, k.c["meanD"][:, :], square=False)
        residual(k, "ev_w_out", 0, moving_x(k, [t for t in mixed for _ in range(2)]), range(DC), ALPHA, mean)
        k.xh_read = k.pe.now()
    return mean


def attention_buffers(k, scope, name):
    k.Tt = k.sb(scope, name + "_scores", 3, 1024)
    k.PT = k.sb(scope, name + "_turned", 2, 1024)
    k.T_read, k.pt_read = [None] * 3, [None] * 2


def value_rows(k, name, layer, chunks, V, off, tiles, toks):
    nc = k.nc
    n = len(chunks) * P
    stationary = rows_x(k, toks)
    banks = [k.take(["gemm", "out"][i // 2]) for i in range(len(tiles))]
    t = k.rows_product([k.bank[b][:, 0:n] for b in banks], name, layer, chunks, DC,
                       lambda c, i: stationary(c, tiles[i]))
    for i, b in enumerate(banks):
        k.read[b] = on(k.act, [t], nc.scalar.copy, V[:, i, off:off + n], k.bank[b][:, 0:n])
    k.value_tok = k.read[banks[-1]]


def hgrn2(k, scope, q, f, g, V, lb, oml):
    W = HEADS_E * SEQ
    full = [k.sb(scope, f"hgrn_{name}", W) for name in
            ("log_decay", "k", "sum", "q_in", "k_in", "q_out", "k_out", "k_turned")]
    S = k.sb(scope, "hgrn_state", HEADS_E, 3, P)
    flat = lambda x: x[:, :, :].rearrange("p h t -> p (h t)")
    halves, out = [], []
    for half in range(2):
        s = slice(half * W // 2, (half + 1) * W // 2)
        part = [x[:, s] for x in full]
        decays = hgrn_decays(k, half, part, flat(q)[:, s], flat(f)[:, s], lb, oml)
        halves.append((part, decays))
    for _ in halves[0][1]:
        k.fill(3)
    for half, (part, _) in enumerate(halves):
        ahead = halves[1][1] if half == 0 else iter(())
        out += hgrn_heads(k, half, part, S, V, g, ahead)
    return out


def hgrn_decays(k, half, part, q, f, lb, oml):
    nc = k.nc
    v1, a1 = nc.vector, nc.scalar
    W = HEADS_E * SEQ // 2
    lf, kk, b, qi, ki, qo, ks, _ = part
    ch = lambda x: x.rearrange("p (c t) -> p c t", t=CH)
    for i in range(2):
        h, s = 2 * half + i, slice(i * SEQ, (i + 1) * SEQ)
        t = on(k.dve, [], v1.tensor_scalar, lf[:, s], f[:, s], oml[:, h:h + 1], lb[:, h:h + 1], ALU.mult, ALU.add)
    t = on(k.dve, [t], v1.tensor_scalar, kk, lf, -1.0, 1.0, ALU.mult, ALU.add)
    t = on(k.act, [t], a1.activation, lf, lf, ACT.Ln)
    yield
    t = on(k.dve, [t], v1.tensor_tensor_scan, b, k.keep[:, :], lf, 0.0, ALU.mult, ALU.add)
    mid = ch(b)[:, :, CH // 2 - 1:CH // 2].to_broadcast([P, W // CH, CH])
    end = ch(b)[:, :, CH - 1:CH].to_broadcast([P, W // CH, CH])
    td = on(k.dve, [t], v1.tensor_tensor, ch(lf), ch(b), mid, ALU.subtract)
    te = on(k.dve, [t], v1.tensor_tensor, ch(ks), ch(b), end, ALU.subtract)
    t1 = on(k.act, [td], a1.activation, qi, lf, ACT.Exp)
    t2 = on(k.act, [td], a1.activation, ki, lf, ACT.Exp, scale=-1.0)
    t4 = on(k.act, [te], a1.activation, ks, ks, ACT.Exp, scale=-1.0)
    t3 = on(k.act, [t], a1.activation, qo, b, ACT.Exp)
    yield
    dc = k.small[:, 64 + 8 * half:72 + 8 * half]
    t1 = on(k.dve, [t1], v1.tensor_tensor, qi, qi, q, ALU.mult)
    t2 = on(k.dve, [t2], v1.tensor_tensor, ki, ki, kk, ALU.mult)
    t4 = on(k.dve, [t4], v1.tensor_tensor, ks, ks, kk, ALU.mult)
    tdc = on(k.dve, [t3], v1.tensor_copy, dc, ch(qo)[:, :, CH - 1])
    t3 = on(k.dve, [tdc], v1.tensor_tensor, qo, qo, q, ALU.mult)
    on(k.dve, [t3], v1.memset, lf, 0.0)
    yield


def hgrn_heads(k, half, part, S, V, g, ahead):
    nc = k.nc
    v1, a1 = nc.vector, nc.scalar
    n_chunks = SEQ // CH
    lf, kk, b, qi, ki, qo, ks, turned = part
    hd = lambda x: x.rearrange("p (h t) -> p h t", t=SEQ)
    dc = k.small[:, 64 + 8 * half:72 + 8 * half]
    k.pe.wait(k.dve.now())
    AT = lf.rearrange("p (a t) -> p a t", t=P)
    b0 = k.take("score")
    for i in range(2 * NQ):
        h, tile = i // NQ, i % NQ
        for j in range(2):
            at = tile * P + j * CH
            t = k.last_matmul(k.bank[b0][j * CH:(j + 1) * CH, i * CH:(i + 1) * CH], hd(ki)[:, h, at:at + CH],
                              hd(qi)[:, h, at:at + CH], start=True, stop=True)
    for j in range(2):
        r = slice(j * CH, (j + 1) * CH)
        mask = k.c["before"][r, :].bitcast(U32).unsqueeze(1).to_broadcast([CH, 2 * NQ, CH])
        ta = on(k.dve, [t], v1.copy_predicated, AT[r, :, j * CH:(j + 1) * CH], mask,
                k.bank[b0][r, 0:2 * NQ * CH].rearrange("p (a t) -> p a t", t=CH))
    k.read[b0] = ta
    ksT = turned.rearrange("p (a h f) -> p a h f", h=2, f=P)
    bt = k.take("turned")
    for tile in range(NQ):
        for h in range(2):
            i = tile * 2 + h
            t = k.pe.done(nc.tensor.transpose(k.bank[bt][:, i * P:(i + 1) * P], hd(ks)[:, h, tile * P:(tile + 1) * P],
                                              k.c["ident"][:, :]))
    k.read[bt] = tk = on(k.act, [t], a1.copy, turned, k.bank[bt][:, :])
    next(ahead, None)
    k.fill(3)
    k.pe.wait(tk)
    for c in range(n_chunks - 1):
        j, tile = c % 2, c // 2
        bs = k.take("score")
        r = slice(j * CH, (j + 1) * CH)
        for h in range(2):
            vh = slice((2 * half + h) * P, (2 * half + h + 1) * P)
            t = k.last_matmul(k.bank[bs][:, h * P:(h + 1) * P], ksT[r, tile, h, :], V[r, tile, vh], start=True,
                              stop=True)
        for h in range(2):
            add, state = k.bank[bs][:, h * P:(h + 1) * P], S[:, 2 * half + h, :, :]
            if c == 0:
                ts = on(k.dve, [t], v1.tensor_copy, state[:, c, :], add)
            else:
                ts = on(k.dve, [t, k.dve.now()], v1.scalar_tensor_tensor, state[:, c, :], state[:, c - 1, :],
                        dc[:, h * n_chunks + c:h * n_chunks + c + 1], add, ALU.mult, ALU.add)
        k.read[bs] = ts
    next(ahead, None)
    k.fill(3)
    k.pe.wait(ta, ts)
    oT = hd(kk)
    bo = k.take("turned")
    for h in range(2):
        vh = slice((2 * half + h) * P, (2 * half + h + 1) * P)
        for tile in range(NQ):
            k.matmul(k.bank[bo][:, h * SEQ + tile * P:h * SEQ + (tile + 1) * P], V[:, tile, vh],
                     AT[:, h * NQ + tile, :], start=(h == 0 and tile == 0), stop=False, skip_group_check=True)
        for c in range(1, n_chunks):
            at = h * SEQ + c * CH
            t = k.last_matmul(k.bank[bo][:, at:at + CH], S[:, 2 * half + h, c - 1, :], qo[:, at:at + CH],
                              start=False, stop=(c == n_chunks - 1), skip_group_check=True)
    k.read[bo] = t = on(k.act, [t], a1.copy, kk, k.bank[bo][:, :])
    next(ahead, None)
    s, mixed = slice(2 * half, 2 * half + 2), slice(4 + 2 * half, 6 + 2 * half)
    return rms_heads(k, [oT], k.c["mean128"][:, :], lambda i: k.col("hg_g"), [g[:, s, :]], 0, [t],
                     [k.XH[:, mixed, SEQS]], [k.XL[:, mixed, SEQS]])


def odd_mixer(k, toks):
    nc = k.nc
    with ExitStack() as scope:
        qT, kT = k.sb(scope, "odd_q", DC, SEQ), k.sb(scope, "odd_k", DC, SEQ)
        V = k.sb(scope, "odd_v", NQ, D)
        mh, ml = (k.sb(scope, f"odd_mixed_{n}", DC, SEQ, dt=F32R) for n in ("high", "low"))
        k.load_consts(scope, ["dilated", "cos1", "sin1", "rot1"], 3, k.scope_marks)
        attention_buffers(k, scope, "odd")
        rot = (k.c["rot1"][:, :], k.c["cos1"][:, :], k.c["sin1"][:, :])
        whole = lambda dst: dst
        columns = [[2 * DC + 4 * half + i for i in range(4)] for half in range(2)]
        for _ in projections(k, "od_w_in", 0, [(None, columns[half], V, 512 * half, range(2, 4)) for half in range(2)],
                             toks):
            pass
        t_values = k.value_tok
        heads = [projections(k, "od_w_in", 0, [(c, [qT[:, c, :]], SEQS, QSCALE, ACT.Copy, rot, whole),
                                               (DC + c, [kT[:, c, :]], SEQS, 1.0, ACT.Copy, rot, whole)], toks)
                 for c in range(DC)]
        k.fillers = heads + k.fillers

        ready = {}

        def prepare(h):
            c = (h + 1) // 2
            if c < DC and c not in ready:
                k.finish(heads[c])
                ready[c] = k.dve.now()
            return [ready[h // 2]]

        mask = view(k.c["dilated"], NQ, SEQ)
        units, done = [], []
        for h in range(HEADS_O):
            r, c = head_rows(h), h // 2
            parts = [(qt * SEQ, (qt + 1) * P, qT[r, c, qt * P:(qt + 1) * P], kT[r, c, 0:(qt + 1) * P])
                     for qt in range(NQ)]
            bank_cols = [(qt * SEQ, mask[:, qt, 0:(qt + 1) * P], BIGNUM, None) for qt in range(NQ)]
            units.append(dict(prepare=lambda h=h: prepare(h), scores=[(bank_cols, parts)],
                              diff=False, first=h % 2 == 0, last=h % 2 == 1, at=r,
                              v=lambda kt, h=h: V[:, kt, h * HD:(h + 1) * HD], tok=done,
                              store=lambda bank, t, c=c: split(k, bank, [t], mh[:, c, :], ml[:, c, :])))
        k.pe.wait(t_values)
        k.xh_read = None
        attend(k, units, 3.0, heads)

        def moving(c):
            k.pe.wait(done[c])
            return mh[:, c, :], ml[:, c, :]

        mean = SlowMean(k, SEQ, k.c["meanD"][:, :], square=False)
        residual(k, "od_w_out", 0, moving, range(DC), ALPHA, mean)
        k.xh_read = k.pe.now()
        scope_end(k)
    return mean



def modulations(k, layer, cs, row):
    nc = k.nc
    row_read, waiting = [None, None], None

    def turn_rows(i, t):
        b = k.take("gemm")
        k.pe.wait(t)
        for j in range(4):
            t = k.pe.done(nc.tensor.transpose(k.bank[b][:, 4 * j:4 * j + 4], row[0:4, i % 2, j * P:(j + 1) * P],
                                              k.c["ident"][0:4, 0:4]))
        row_read[i % 2] = t
        bias = k.col("b_mod", 48 * layer + 4 * i, 4).unsqueeze(2).to_broadcast([P, 4, 2])
        m, parts = k.mod[:, layer, 4 * i:4 * i + 4, :], k.bank[b][:, 0:16].rearrange("p (c s) -> p c s", s=4)
        t = on(k.dve, [t], nc.vector.tensor_tensor, m, parts[:, :, 0:2], bias, ALU.add)
        k.read[b] = k.mod_ready = on(k.dve, [t], nc.vector.tensor_tensor, m, m, parts[:, :, 2:4], ALU.add)

    for i in range(12):
        k.pe.wait(k.c_ready)
        b = k.take("gemm")
        out = k.bank[b][:, 0:512]
        for c in range(DC):
            wh, wl = k.weights([("w_mod_2", layer, c, 4 * i + j) for j in range(4)])
            k.matmul(out, cs[:, c, :], wh, hold=True, start=(c == 0), stop=False)
            if c < DC - 1:
                k.matmul(out, cs[:, c, :], wl, start=False, stop=False)
            else:
                t = k.last_matmul(out, cs[:, c, :], wl, start=False, stop=True)
        k.read[b] = t = on(k.act, [t, row_read[i % 2]], nc.scalar.copy, row[0:4, i % 2, :], k.bank[b][0:4, :])
        if waiting is not None:
            turn_rows(*waiting)
        waiting = (i, t)
        yield 3.5
    turn_rows(*waiting)
    yield 0.2


def split_conditions(k, cs):
    nc = k.nc
    cc = k.col("cc", 0, 16)
    ccv = cc.rearrange("p (c s) -> p c s", s=2)
    t = on(k.act, [], nc.scalar.activation, cc, cc, ACT.Silu)
    t0 = on(k.dve, [], nc.vector.memset, cs[:, :, :].bitcast(F32), 0.0)
    t = on(k.act, [t, t0], nc.scalar.copy, cs[:, :, 0:2], ccv)
    k.c_ready = on(k.dve, [t], nc.vector.tensor_tensor, cs[:, :, 2:4], ccv, cs[:, :, 0:2].bitcast(F32), ALU.subtract)


def context_norm(k):
    mean = Mean(k, CTX, k.c["meanD"][:, :], pool="score")
    for i in range(DC):
        mean.add(k.X[:, i, 0:CTX], None)
        yield 0.5
    t = rsqrt_of(k, mean, 1, 1)
    k.context_toks = modulate(k, 0, "norm_mix", 0, [0], 0, 1, t)


def modulate(k, layer, norm, section, sides, lo, r, t):
    nc = k.nc
    sh, sc = (k.mod[:, layer, section + o:section + o + DC, :] for o in (0, DC))
    gs = k.gs[:, :].rearrange("p (c s) -> p c s", s=2)
    g = k.col(norm, layer * DC, DC).unsqueeze(2).to_broadcast([P, DC, 2])
    tg = on(k.dve, [k.mod_ready], nc.vector.tensor_scalar, gs, sc, 1.0, None, ALU.add)
    tg = on(k.dve, [tg], nc.vector.tensor_tensor, gs, gs, g, ALU.mult)
    started, out = [], [None] * DC

    def finish_part():
        i, s, shift, tmp, ts, read = started.pop(0)
        xh, xl = k.XH[:, i, s], k.XL[:, i, s]
        th = on(k.act, [ts, k.xh_read], nc.scalar.activation, xh, tmp, ACT.Identity, bias=shift)
        out[i] = on(k.dve, [th], nc.vector.scalar_tensor_tensor, xl, tmp, shift, xh.bitcast(F32), ALU.add, ALU.subtract)
        read(out[i])

    for i in range(DC):
        for side in sides:
            s = slice(side * CTX, (side + 1) * CTX)
            tmp, free, read = k.scratch(CTX)
            ts = on(k.dve, [t, tg, *free], nc.vector.scalar_tensor_tensor, tmp, k.X[:, i, s], gs[:, i, side:side + 1],
                    k.RS[:, r, side * CTX - lo:side * CTX - lo + CTX], ALU.mult, ALU.mult)
            if len(started) == 2:
                finish_part()
            started.append((i, s, sh[:, i, side:side + 1], tmp, ts, read))
    while started:
        finish_part()
    k.rs_read[r] = k.dve.now()
    return out


def modulated_norm(k, layer, norm, section, lo, mean):
    t = rsqrt_of(k, mean, 1)
    k.fill(4)
    return modulate(k, layer, norm, section, range(lo // CTX, 2), lo, 0, t)


def gated_residual(k, name, layer, moving, ks, gate, lo, mean):
    nc = k.nc
    for i in range(DC):
        b = k.take("gemm")
        t = k.product(k.bank[b][:, 0:T2 - lo], name, layer, i, ks, moving)
        for side in range(lo // CTX, 2):
            s = slice(side * CTX, (side + 1) * CTX)
            t2 = on(k.dve, [t], nc.vector.scalar_tensor_tensor, k.X[:, i, s],
                    k.bank[b][:, side * CTX - lo:(side + 1) * CTX - lo], k.mod[:, layer, gate + i, side:side + 1],
                    k.X[:, i, s], ALU.mult, ALU.add)
        k.read[b] = t2
        if mean is not None:
            mean.add(k.X[:, i, lo:T2], t2)


def second_block(k, mean):
    nc = k.nc
    for layer in range(DEPTH):
        lo = 0 if layer == 0 else CTX
        mixed = token_mixers(k, layer, lo, mean)
        mean = SlowMean(k, T2 - lo, k.c["meanD"][:, :])
        gated_residual(k, "w_out_2", layer, moving_x(k, mixed, slice(lo, T2)), range(DC), 16, lo, mean)
        k.xh_read = k.pe.now()
        toks = modulated_norm(k, layer, "norm_ffn", 24, lo, mean)
        mean = swiglu(k, layer, lo, toks)
    t = rsqrt_of(k, mean, 1)
    with ExitStack() as scope:
        y = k.sb(scope, "y", DC, SEQ)
        for i in range(DC):
            t2 = on(k.dve, [t], nc.vector.scalar_tensor_tensor, y[:, i, :], k.X[:, i, SEQS], k.col("final", i),
                    k.RS[:, 0, 0:SEQ], ALU.mult, ALU.mult)
            k.act.wait(t2)
            nc.scalar.dma_start(k.io["out"][:, i, :], y[:, i, :]).then_inc(k.s_out, 16)
        nc.scalar.wait_ge(k.s_out, 16 * DC)


def swiglu(k, layer, lo, toks):
    nc = k.nc
    n, half = T2 - lo, DFF // P // 2
    with ExitStack() as scope:
        hh, hl = (k.sb(scope, f"hidden2_{x}{layer}", half, n, dt=F32R) for x in ("high", "low"))
        hid_read = None
        for part in range(2):
            th = []
            for i in range(half):
                col = part * half + i
                bg = k.take("gemm")
                columns = [(w, layer, col) for w in ("w_gate_2", "w_up_2")]
                x = moving_x(k, toks, slice(lo, T2))
                if col == 0:
                    bu = k.take("gemm")
                    tg, tu = k.products([k.bank[b][:, 0:n] for b in (bg, bu)], columns, range(DC), x)
                else:
                    tg = k.product(k.bank[bg][:, 0:n], *columns[0], range(DC), x)
                tmp, free, read = k.scratch(n)
                k.read[bg] = tg = on(k.act, [tg, *free], nc.scalar.activation, tmp, k.bank[bg][:, 0:n], ACT.Silu)
                if col > 0:
                    bu = k.take("gemm")
                    tu = k.product(k.bank[bu][:, 0:n], *columns[1], range(DC), x)
                k.read[bu] = t = on(k.dve, [tg, tu], nc.vector.tensor_tensor, tmp, tmp, k.bank[bu][:, 0:n], ALU.mult)
                t = on(k.act, [t, hid_read], nc.scalar.copy, hh[:, i, :], tmp)
                t = on(k.dve, [t], nc.vector.tensor_tensor, hl[:, i, :], tmp, hh[:, i, :].bitcast(F32), ALU.subtract)
                read(t)
                th.append(t)

            def moving(c):
                k.pe.wait(th[c - part * half])
                return hh[:, c - part * half, :], hl[:, c - part * half, :]

            if part == 1:
                nc.scalar.preload_act_table_set(LNEXP)
            mean = SlowMean(k, n, k.c["meanD"][:, :]) if part == 1 else None
            gated_residual(k, "w_down_2", layer, moving, range(part * half, (part + 1) * half), 40, lo, mean)
            hid_read = k.pe.now()
        k.xh_read = hid_read
        scope_end(k)
    return mean


def token_mixers(k, layer, lo, mean):
    nc = k.nc
    if layer == 0:
        toks = modulated_norm(k, layer, "norm_mix", 0, CTX, mean)
        k.pe.wait(k.context_toks[-1])
    else:
        toks = modulated_norm(k, layer, "norm_mix", 0, 0, mean)
    with ExitStack() as scope:
        sb = lambda n, *shape: k.sb(scope, f"{n}{layer}", *shape)
        nq, nk, sq, sk = sb("nq", 3, T2), sb("nk", 3, T2), sb("sq", 3, T2), sb("sk", 1, T2)
        V = sb("v2", 4, 512)
        k.load_consts(scope, ["cos2", "sin2", "rot2", "window", "near"], 2 + layer, k.scope_marks)
        if layer > 0:
            k.pool.wait(k.pe.now())
        nc.gpsimd.dma_start(k.wa2[:, :], k.io["wa2"][layer]).then_inc(k.s_wa2, 16)
        rot = (k.c["rot2"][:, :], k.c["cos2"][:, :], k.c["sin2"][:, :])
        new, both = slice(lo, T2), slice(0, T2)
        chunks = lambda buf, n, s: [buf[:, i, s] for i in range(n)]
        project = lambda *plan, early=False: projections(k, "w_in_2", layer, plan, toks, early)
        x_part = lambda dst: dst[:, dst.shape[1] - SEQ:dst.shape[1]]
        with ExitStack() as inner:
            g2 = lambda n, *shape: k.sb(inner, f"{n}{layer}", *shape)
            gq, gk, gg, z = g2("gq", 2, T2), g2("gk", 2, T2), g2("gg", 2, T2), g2("z", 1, T2)
            GV, o = g2("gv", 4, 256), g2("go", 2, T2)
            for _ in project((6, chunks(gg, 2, new), new, 1.0, ACT.Silu, None, None), early=True):
                pass
            nc.scalar.preload_act_table_set(LNEXP)
            for _ in project((8, chunks(z, 1, both), both, 1.0, ACT.Copy, None, None),
                             (0, chunks(gq, 2, new), new, QSCALE, ACT.Copy, None, None),
                             (2, chunks(gk, 2, both), both, 1.0, ACT.Copy, None, None),
                             (None, [4, 5], GV, 0, range(4))):
                pass
            k.wa2_loads = 16 * (layer + 1)
            attentions = project((9, chunks(nq, 3, new), new, QSCALE, ACT.Copy, None, None),
                                 (12, chunks(nk, 3, both), both, 1.0, ACT.Copy, None, None),
                                 (18, chunks(sq, 3, new), new, QSCALE, ACT.Copy, rot, x_part),
                                 (21, chunks(sk, 1, both), both, 1.0, ACT.Copy, rot, x_part),
                                 (None, [15, 16, 17, 22], V, 0, range(4)))
            k.fillers.insert(0, attentions)
            k.act.wait(k.dve.now())
            k.dve.wait(k.act.now())
            k.pe.wait(k.act.now())
            o_tokens = gla(k, inner, layer, lo, gq, gk, z, GV, o)

            def rest():
                k.finish(attentions)
                k.xh_read = k.pe.now()
                return k.act.now(), k.dve.now()

            projected = []
            mixed = rms_heads(k, [o[:, p, new] for p in range(2)], k.c["mean64"][:, :],
                              lambda i: k.col("gla_norm", layer * 2 + i), [gg[:, i, new] for i in range(2)], 1,
                              o_tokens, [k.XH[:, i, new] for i in range(2)], [k.XL[:, i, new] for i in range(2)],
                              between=lambda: projected.extend(rest()))
            scope_end(k)
        attention_buffers(k, scope, f"mix{layer}")
        k.NB = sb("nb", 2, 1024)
        k.nb_read = [on(k.pool, [], nc.gpsimd.memset, k.NB[:, :, :], 0.0)] * 2
        k.nb_ready = [None] * 2
        k.SW = sb("swapped", T2)
        k.need_consts()
        window, near = view(k.c["window"], NQ, T2), view(k.c["near"], NQ, SEQ)
        zeros = window[:, 0, 0:CTX]
        for h in range(2):
            near_bias(k, layer, h, near)
        swapped = swap_keys(k, sk, projected)
        k.pe.wait(*projected)
        units, done = [], []
        for kind in range(2) if layer == 0 else (1, 0):
            for side in range(lo // CTX, 2):
                for h in range(6):
                    c, r = h // 2, head_rows(h)
                    keys = CTX if side == 0 else T2
                    prepare, nb = None, None
                    if kind == 0:
                        q, kk, vo = nq, nk[:, c, :], h * HD
                        start, sink = BIGNUM, None
                        if side:
                            if 1 <= h < NA_H - 1:
                                prepare = lambda h=h: near_bias(k, layer, h + 1, near)
                            nb = h % 2
                            bias = [k.NB[:, h % 2, qt * 512:(qt + 1) * 512] for qt in range(NQ)]
                    else:
                        kv = h // SWA_G
                        prepare = lambda: [swapped]
                        q, kk, vo = sq, k.SK[(kv, h % 2)], 384 + kv * HD
                        start, sink = k.negsink[:, layer * 6 + h:layer * 6 + h + 1], k.col("sink", layer * 6 + h)
                        bias = [window[:, qt, :] for qt in range(NQ)]
                    if not side:
                        bias = [zeros, zeros]
                    sc = []
                    for qt in range(NQ):
                        qs = q[r, c, side * CTX + qt * P:side * CTX + (qt + 1) * P]
                        sc.append(([(qt * 512, bias[qt], start, sink)], [(0, keys, qs, kk[r, 0:keys])]))
                    at = (2 + 3 * kind + c, slice(side * CTX, (side + 1) * CTX))
                    units.append(dict(prepare=prepare, scores=sc, diff=False, first=h % 2 == 0, last=h % 2 == 1, at=r,
                                      nb=nb, v=lambda kt, vo=vo: V[:, kt, vo:vo + HD], tok=done,
                                      store=lambda bank, t, at=at: split(k, bank, [t], k.XH[:, at[0], at[1]],
                                                                         k.XL[:, at[0], at[1]])))
        attend(k, units)
        scope_end(k)
        k.pe.wait(k.dve.now())
    return [None] * DC


def swap_keys(k, sk, toks):
    nc = k.nc
    base = sk[:, 0, :]
    other = k.SW[:, :]
    on(k.dve, toks, nc.vector.tensor_copy, other[0:HD, :], base[HD:P, :])
    t = on(k.dve, [], nc.vector.tensor_copy, other[HD:P, :], base[0:HD, :])
    k.SK = {(0, 0): base, (1, 1): base, (0, 1): other, (1, 0): other}
    return t


def near_bias(k, layer, h, near):
    nc = k.nc
    s = k.s_bias[h % 2]
    nb = k.NB[:, h % 2, :].rearrange("p (a b) -> p a b", b=512)
    k.pool.wait(k.nb_read[h % 2])
    nc.gpsimd.dma_start(nb[:, :, CTX:T2], k.io["rpb"][layer, h]).then_inc(s, 16)
    k.bias_count[h % 2] += 16
    nc.gpsimd.wait_ge(s, k.bias_count[h % 2])
    t = on(k.pool, [], nc.gpsimd.tensor_tensor, nb[:, :, CTX:T2], nb[:, :, CTX:T2], near, ALU.add)
    k.nb_ready[h % 2] = t


def gla(k, scope, layer, lo, q, kT, z, V, o):
    nc = k.nc
    n_chunks = T2 // CH
    buf = lambda name, *shape: k.sb(scope, f"gla{layer}_{name}", *shape)
    decay = [buf(name, T2)[:, :] for name in ("log_decay", "sum", "sum_from_end")]
    sets = [[buf(f"{name}{i}", T2)[:, :] for name in ("q", "k_in", "k_out")] + [k.small[:, 80 + 8 * i:88 + 8 * i]]
            for i in range(2)]
    keT, AT, S = (buf(n, *shape)[:] for n, shape in (("keT", (4, P)), ("A", (2, 4, P)), ("state", (n_chunks - 1, P))))
    free, o_tokens = [None, None], [None, None]
    nc.tensor.wait_ge(k.s_wa2, k.wa2_loads)
    share = 4.5 if layer == 0 else 3.0
    units = [(d, pair) for d in range(2) for pair in range(2)]
    steps = [gla_decays(k, layer, lo, *units[i], q, kT, z, decay, sets[i % 2], free, i) for i in range(4)]
    for tokens in steps[0]:
        k.fill(share)
    for i, (d, pair) in enumerate(units):
        ahead = steps[i + 1] if i < 3 else iter(())
        if pair == 0:
            t_zero = on(k.pool, [k.pe.now()], nc.gpsimd.memset, AT, 0.0)
        o_tokens[pair] = gla_unit(k, lo, d, pair, V, o, sets[i % 2], keT, AT, S, tokens, t_zero, ahead, share,
                                  o_tokens[pair])
        free[i % 2] = k.pe.now()
        tokens = (list(ahead) or [None])[-1]
    return o_tokens


def gla_decays(k, layer, lo, d, pair, q, kT, z, decay, out, free, i):
    nc = k.nc
    v1, a1 = nc.vector, nc.scalar
    n_chunks = T2 // CH
    ch = lambda x: x.rearrange("p (c t) -> p c t", t=CH)
    la, b, b_end = decay
    qi, ki, ke, dc = out
    rows = slice(32 * d, 32 * d + RANK)
    bz = k.take("out")
    t = k.last_matmul(k.bank[bz][:, :], k.wa2[rows, pair * P:(pair + 1) * P], z[rows, 0, :], start=True, stop=True)
    k.read[bz] = t = on(k.act, [t, k.dve.now()], a1.activation, la, k.bank[bz][:, :], ACT.Identity,
                        bias=k.col("ba", (layer * 2 + d) * 2 + pair))
    t1 = on(k.dve, [t, k.act.now()], v1.scalar_tensor_tensor, b, la, -1.0, la, ALU.mult, ALU.min)
    t1 = on(k.act, [t1], a1.activation, b, b, ACT.Exp)
    t1 = on(k.act, [t1], a1.activation, b, b, ACT.Ln, bias=k.c["cols"][:, 2:3])
    yield None
    t = on(k.dve, [t1], v1.scalar_tensor_tensor, la, la, 0.0, b, ALU.min, ALU.subtract)
    t = on(k.dve, [t], v1.tensor_tensor_scan, b, k.keep[:, 0:T2], la, 0.0, ALU.mult, ALU.add)
    if d == 1:
        t = on(k.dve, [t], v1.tensor_tensor, la, la, b, ALU.subtract)
        t = on(k.dve, [t], v1.tensor_tensor, ch(b_end), ch(la), ch(b)[:, :, CH - 1:CH].to_broadcast([P, n_chunks, CH]),
               ALU.add)
        b = b_end
    edge = slice(CH - 1, CH) if d == 0 else slice(0, 1)
    td = on(k.dve, [t], v1.tensor_tensor, ch(la), ch(b), ch(b)[:, :, edge].to_broadcast([P, n_chunks, CH]),
            ALU.subtract)
    t3 = on(k.act, [td, free[i % 2]], a1.activation, ke, la, ACT.Exp, scale=-1.0 / 16)
    t1 = on(k.act, [t], a1.activation, qi, b, ACT.Exp, scale=1.0 / 16)
    t2 = on(k.act, [t], a1.activation, ki, b, ACT.Exp, scale=-1.0 / 16)
    yield None
    t3 = on(k.dve, [t3], v1.tensor_tensor, ke, ke, kT[:, pair, :], ALU.mult)
    tdc = on(k.dve, [t1], v1.tensor_copy, dc, ch(qi)[:, :, edge])
    t1 = on(k.dve, [t1, tdc], v1.tensor_tensor, qi[:, lo:T2], qi[:, lo:T2], q[:, pair, lo:T2], ALU.mult)
    t2 = on(k.dve, [t2], v1.tensor_tensor, ki, ki, kT[:, pair, :], ALU.mult)
    yield t1, t2, t3


def gla_unit(k, lo, d, pair, V, o, inputs, keT, AT, S, tokens, t_zero, ahead, share, t_out):
    nc = k.nc
    v1, a1 = nc.vector, nc.scalar
    n_chunks, first_tile = T2 // CH, lo // P
    qi, ki, ke, dc = inputs
    t1, t2, t3 = tokens
    bt = k.take("turned")
    k.pe.wait(t3)
    for tile in range(4):
        t = k.pe.done(nc.tensor.transpose(k.bank[bt][:, tile * P:(tile + 1) * P], ke[:, tile * P:(tile + 1) * P],
                                          k.c["ident"][:, :]))
    k.read[bt] = tk = on(k.act, [t], a1.copy, keT, k.bank[bt][:, :].rearrange("p (a f) -> p a f", f=P))
    k.pe.wait(t1, t2)
    for hh in range(2):
        r = slice(hh * HD, (hh + 1) * HD)
        b0 = k.take("score")
        for tile in range(first_tile, 4):
            for j in range(2):
                at = tile * P + j * CH
                t = k.last_matmul(k.bank[b0][j * CH:(j + 1) * CH, tile * CH:(tile + 1) * CH], ki[r, at:at + CH],
                                  qi[r, at:at + CH], start=True, stop=True)
        for j in range(2):
            s = slice(j * CH, (j + 1) * CH)
            mask = k.c["before" if d == 0 else "after"][s, :].bitcast(U32).unsqueeze(1) \
                .to_broadcast([CH, 4 - first_tile, CH])
            ta = on(k.dve, [t, t_zero], v1.copy_predicated, AT[s, hh, first_tile:4, j * CH:(j + 1) * CH], mask,
                    k.bank[b0][s, lo // 2:256].rearrange("p (a t) -> p a t", t=CH))
        k.read[b0] = ta
    next(ahead, None)
    k.fill(share)
    k.pe.wait(tk)
    order = list(range(n_chunks)) if d == 0 else [3, 2, 1, 0, 7, 6, 5, 4]
    banks = [k.take("out"), k.take("out")]
    for c in order[:-1]:
        j, tile = c % 2, c // 2
        s = slice(j * CH, (j + 1) * CH)
        t = k.last_matmul(k.bank[banks[j]][:, tile * P:(tile + 1) * P], keT[s, tile, :],
                          V[s, tile, pair * P:(pair + 1) * P], start=True, stop=True)
    enter = {}
    for n, c in enumerate(order[:-1]):
        add = k.bank[banks[c % 2]][:, c // 2 * P:(c // 2 + 1) * P]
        if n == 0:
            ts = on(k.dve, [t], v1.tensor_copy, S[:, n, :], add)
        else:
            ts = on(k.dve, [t, ts], v1.scalar_tensor_tensor, S[:, n, :], S[:, n - 1, :], dc[:, c:c + 1], add,
                    ALU.mult, ALU.add)
        enter[order[n + 1]] = n
    k.read[banks[0]] = k.read[banks[1]] = ts
    next(ahead, None)
    k.fill(2 * share)
    k.pe.wait(ta, ts)
    bo = k.take("turned")
    for hh in range(2):
        r = slice(hh * HD, (hh + 1) * HD)
        for tile in range(first_tile, 4):
            k.matmul(k.bank[bo][r, tile * P:(tile + 1) * P], V[:, tile, pair * P + hh * HD:pair * P + (hh + 1) * HD],
                     AT[:, hh, tile, :], start=(tile == first_tile), stop=False, skip_group_check=True)
    for hh in range(2):
        r = slice(hh * HD, (hh + 1) * HD)
        for c in range(lo // CH, n_chunks):
            if c in enter:
                t = k.last_matmul(k.bank[bo][r, c * CH:(c + 1) * CH], S[r, enter[c], hh * HD:(hh + 1) * HD],
                                  qi[r, c * CH:(c + 1) * CH], start=False, stop=True, skip_group_check=True)
    dst = o[:, pair, lo:T2]
    if d == 0:
        k.read[bo] = on(k.act, [t], a1.copy, dst, k.bank[bo][:, lo:T2])
    else:
        k.read[bo] = on(k.dve, [t, t_out], v1.tensor_tensor, dst, dst, k.bank[bo][:, lo:T2], ALU.add)
    return k.read[bo]


def load_stream(k, tiles):
    nc, io = k.nc, k.io
    stream = io["stream"]
    k.tiles = tiles
    assert tiles % RING == 0

    def first_tiles(slots):
        for s in slots:
            nc.sync.dma_start(k.ring[:, s, :], stream[s]).then_inc(k.s_tile[s], 16)

    for i, half in enumerate((slice(0, DC // 2), slice(DC // 2, DC))):
        nc.sync.dma_start(k.X[:, half, SEQS], io["x"][:, half]).then_inc(k.s_x[i], 16)
    first_tiles(range(0, 3))
    loads = [(k.par, "params")] + [(k.c[name], name) for name in GLOBAL_CONSTS]
    for buffer, name in loads:
        nc.sync.dma_start(buffer[:, :], io[name]).then_inc(k.s_start[0], 16)
    first_tiles(range(3, RING))
    nc.sync.dma_start(k.X[:, :, 0:CTX], io["ctx"]).then_inc(k.s_start[0], 16)
    k.n_loads[0] = 16 * (len(loads) + 1)
    with nc.sync.Fori(1, tiles // RING) as i:
        for s in range(RING):
            nc.sync.wait_ge(k.s_low, i * RING + (s - RING + 1))
            nc.sync.dma_start(k.ring[:, s, :], stream[bass.ds(i * RING + s, 1)].rearrange("a p n -> (a p) n")) \
                .then_inc(k.s_tile[s], 16)



def kernel(**inputs):
    import numpy as _np
    import concourse.bacc as _bacc
    from concourse import mybir as _mybir
    from concourse.bass_utils import run_bass_kernel_spmd as _run

    nc = _bacc.Bacc("TRN2", target_bir_lowering=False, num_devices=1)
    arrays, io = {}, {}

    def give(name, a):
        a = _np.ascontiguousarray(a)
        arrays["in_" + name] = a
        io[name] = nc.dram_tensor("in_" + name, a.shape, _mybir.dt.from_np(a.dtype), kind="ExternalInput").ap()

    x = {n: _np.asarray(a) for n, a in inputs.items()}
    chunked = lambda a: a.reshape(*a.shape[:-1], a.shape[-1] // P, P)
    feat = lambda a: chunked(a.reshape(-1)).T
    toks = lambda a: _np.transpose(chunked(a), (2, 1, 0))
    for n, a in CONST.items():
        give(n, a)
    rows = lambda a: _np.broadcast_to(a.reshape(1, -1), (P, a.size))
    par = {"ln1_g": feat(x["ln1_g"]), "ln1_b": feat(x["ln1_b"]), "ln2_g": feat(x["ln2_g"]), "ln2_b": feat(x["ln2_b"]),
           "ple_g": feat(x["ple_norm_g"]), "sub_g": feat(x["da_subln_g"]), "hg_g": feat(x["hg_norm_g"]),
           "lb": feat(x["hg_lb_logits"]), "norm_mix": feat(x["norm_mix_2"]), "norm_ffn": feat(x["norm_ffn_2"]),
           "final": feat(x["final_norm_2"]), "b_mod": feat(x["b_mod_2"]),
           "ba": feat(_np.stack([x["gla_ba_f_2"], x["gla_ba_b_2"]], 1)), "gla_norm": feat(x["gla_norm_2"]),
           "sink": rows(x["swa_sink_2"]), "lam": rows(x["da_lambda"]),
           "cc": _np.stack([feat(x["c_ctx_2"]), feat(x["c_2"])], 2).reshape(P, 16)}
    give("params", _np.concatenate([par[n] for n in PARAMS], 1))
    give("x", toks(x["x"][0]))
    give("ctx", toks(x["ctx_2"][0]))
    give("p", _np.stack([toks(x["p"][l, 0]) for l in range(DEPTH)]))
    wa2 = _np.zeros((DEPTH, P, GLA_W), _np.float32)
    wa2[:, 0:RANK] = x["gla_wa2_f_2"]
    wa2[:, 32:32 + RANK] = x["gla_wa2_b_2"]
    give("wa2", wa2)
    rpb = _np.zeros((DEPTH, NA_H, RPB_R, RPB_C), _np.float32)
    rpb[..., GRID_W - 16:GRID_W + 15] = x["na_rpb_2"]
    rpb = _np.lib.stride_tricks.sliding_window_view(rpb, GRID_W, axis=-1)[..., ::-1, :]
    rows = SEQ // GRID_W
    rpb = _np.stack([rpb[:, :, 7 - row:7 - row + rows] for row in range(rows)], 2)
    rpb = rpb.reshape(DEPTH, NA_H, NQ, rows // NQ, rows, GRID_W, GRID_W)
    give("rpb", _np.transpose(rpb, (0, 1, 3, 5, 2, 4, 6)).reshape(DEPTH, NA_H, P, NQ, SEQ))
    W = {n: x[n] for n in ("ev_w_in", "ev_w_out", "od_w_in", "od_w_out", "ffn_w1", "ffn_w2", "ple_w_proj", "ple_w_gate",
                           "w_mod_2", "w_out_2", "w_gate_2", "w_up_2", "w_down_2")}
    w = x["w_in_2"]
    low = _np.zeros((DEPTH, D, P), _np.float32)
    low[..., 0:RANK] = w[..., 1024:1024 + RANK]
    low[..., 32:32 + RANK] = w[..., 1024 + RANK:1024 + 2 * RANK]
    W["w_in_2"] = _np.concatenate([w[..., :1024], low, w[..., 1024 + 2 * RANK:]], -1)
    n_blocks = sum(a.size for a in W.values()) // (P * P)
    tiles = -(-n_blocks // (TB * RING)) * RING
    give("stream", _np.zeros((tiles, P, TB * P), _np.float32))
    io["out"] = nc.dram_tensor("out_0", (P, DC, SEQ), _mybir.dt.float32, kind="ExternalOutput").ap()
    k = build(nc, io, tiles)
    assert len(k.blocks) == n_blocks, (len(k.blocks), n_blocks)
    stream = arrays["in_stream"]
    for i, (name, layer, kc, col) in enumerate(k.blocks):
        stream[i // TB, :, i % TB * P:(i % TB + 1) * P] = W[name][layer, kc * P:(kc + 1) * P, col * P:(col + 1) * P]
    r = _run(nc, [arrays], core_ids=[0])
    out = r.results[0]["out_0"]
    return _np.ascontiguousarray(_np.transpose(out, (2, 1, 0))).reshape(1, SEQ, D)


def build(nc, io, tiles):
    ctx = ExitStack()
    with ctx:
        k = Program(nc, ctx, io)
        load_stream(k, tiles)
        emit(k)
        for s in k.s_tile:
            nc.tensor.wait_ge(s, 16 * tiles // RING)
        nc.tensor.wait_ge(k.s_low, k.split)
    return k
```
